# Optimizing a Trainium2 kernel written in Bass

```python
import jax, jax.numpy as jnp
from jax import lax
import numpy as np

D_MODEL = 1024
BATCH = 1
SEQ = 1024
DEPTH = 1

A_HEADS = 4
A_HEAD_DIM = 64
A_WIDTH = A_HEADS * A_HEAD_DIM
A_DECAY_LORA = 64
A_ICL_LORA = 64
A_GATE_LORA = 128
A_LN_EPS = 64e-5
B_HEADS = 4
B_HEAD_DIM = 64
B_WIDTH = B_HEADS * B_HEAD_DIM
B_CONV = 4
B_CHUNK = 128
C_Q_HEADS = 8
C_KV_HEADS = 2
C_HEAD_DIM = 64
C_WIDTH = C_Q_HEADS * C_HEAD_DIM
C_KV_WIDTH = C_KV_HEADS * C_HEAD_DIM
WINDOW = 128
C_BLOCK = 128
N_BRANCH = 3
N_GROUPS = 4
EXPERTS_PER_GROUP = 8
N_EXPERTS = N_GROUPS * EXPERTS_PER_GROUP
TOP_K = 2
D_EXPERT = 512
MOE_BLOCK = 128
EPS = 1e-6
ADA_GATE_INIT = 0.5

A_SIZES = (A_WIDTH, A_WIDTH, A_WIDTH, A_DECAY_LORA, A_ICL_LORA, A_GATE_LORA)
A_SHIFT_WIDTH = sum(A_SIZES)
REST_SIZES = (B_WIDTH, B_WIDTH, B_WIDTH, B_WIDTH, B_HEADS, B_HEADS,
              C_WIDTH, C_KV_WIDTH, C_KV_WIDTH, N_BRANCH * D_MODEL)
N_IN = A_SHIFT_WIDTH + sum(REST_SIZES)

kernel_name = 'hybrid_rwkv7_mlstm_swa_hmoe_block'

def _split(z, sizes):
    return jnp.split(z, np.cumsum(sizes)[:-1].tolist(), axis=-1)

def rms_norm(x, g):
    xf = x.astype(jnp.float32)
    y = xf * lax.rsqrt(jnp.mean(xf * xf, axis=-1, keepdims=True) + EPS)
    return (y * g).astype(x.dtype)

def token_shift(z):
    return jnp.pad(z, ((0, 0), (1, 0), (0, 0)))[:, :-1]

def causal_conv(x, w, b):
    K, C = w.shape
    y = lax.conv_general_dilated(x, w[:, None, :], window_strides=(1,), padding=((K - 1, 0),),
                                 dimension_numbers=('NWC', 'WIO', 'NWC'), feature_group_count=C)
    return y + b

def alibi_slopes(n):
    return jnp.exp2(-8.0 * jnp.arange(1, n + 1, dtype=jnp.float32) / n)

def rwkv7_time_mix(r, k, v, w_lo, a_lo, g_lo, w0, w2, a0, a2, g2, k_k, k_a, r_k, lnx_g, lnx_b):
    dt = r.dtype
    f32 = jnp.float32
    Bsz, T, _ = r.shape
    H, N = A_HEADS, A_HEAD_DIM
    r, k, v, w_lo, a_lo, g_lo = (z.astype(f32) for z in (r, k, v, w_lo, a_lo, g_lo))
    w_log = -jax.nn.softplus(-(w0 + jnp.tanh(w_lo) @ w2)) - 0.5
    decay = jnp.exp(-jnp.exp(w_log))
    a = jax.nn.sigmoid(a0 + a_lo @ a2)
    g = jax.nn.sigmoid(g_lo) @ g2
    heads = lambda z: z.reshape(Bsz, T, H, N)
    kk = heads(k * k_k)
    kk = kk / jnp.maximum(jnp.sqrt(jnp.sum(kk * kk, axis=-1, keepdims=True)), 1e-12)
    k = k * (1 + (a - 1) * k_a)
    rh, kh, vh, ah, wh = heads(r), heads(k), heads(v), heads(a), heads(decay)
    a_vec = -kk
    b_vec = kk * ah

    def step(S, inp):
        r_t, w_t, k_t, v_t, av_t, bv_t = inp
        sa = jnp.einsum('bhij,bhj->bhi', S, av_t)
        S = S * w_t[:, :, None, :] + sa[..., None] * bv_t[:, :, None, :] + v_t[..., None] * k_t[:, :, None, :]
        return S, jnp.einsum('bhij,bhj->bhi', S, r_t)

    S0 = jnp.zeros((Bsz, H, N, N), f32)
    _, y = lax.scan(step, S0, tuple(jnp.moveaxis(z, 1, 0) for z in (rh, wh, kh, vh, a_vec, b_vec)))
    y = jnp.moveaxis(y, 0, 1)
    mu = jnp.mean(y, axis=-1, keepdims=True)
    var = jnp.mean(jnp.square(y - mu), axis=-1, keepdims=True)
    y = ((y - mu) * lax.rsqrt(var + A_LN_EPS)).reshape(Bsz, T, A_WIDTH) * lnx_g + lnx_b
    bonus = jnp.sum(rh * kh * r_k, axis=-1, keepdims=True) * vh
    y = (y + bonus.reshape(Bsz, T, A_WIDTH)) * g
    return y.astype(dt)

def mlstm_chunkwise(q, k, v, o, i_pre, f_pre, conv_w, conv_b, b_i, b_f, hn_g):
    dt = q.dtype
    f32 = jnp.float32
    Bsz, T, _ = q.shape
    H, d, L = B_HEADS, B_HEAD_DIM, B_CHUNK
    NC = T // L
    qk = jax.nn.silu(causal_conv(jnp.concatenate([q, k], axis=-1), conv_w, conv_b))
    q, k = jnp.split(qk, 2, axis=-1)
    chunks = lambda z: z.reshape(Bsz, NC, L, H, d).transpose(0, 3, 1, 2, 4).astype(f32)
    qc, kc, vc = chunks(q), chunks(k) * d ** -0.5, chunks(v)
    gate_chunks = lambda z: z.astype(f32).reshape(Bsz, NC, L, H).transpose(0, 3, 1, 2)
    ig = gate_chunks(i_pre + b_i)
    logf = jax.nn.log_sigmoid(gate_chunks(f_pre + b_f))
    F = jnp.cumsum(logf, axis=-1)
    F_last = F[..., -1]
    g_end = F_last[..., None] - F + ig

    def chunk_step(carry, inp):
        C, n, m = carry
        k_c, v_c, g_c, fl_c = inp
        m_new = jnp.maximum(fl_c + m, jnp.max(g_c, axis=-1))
        carry_decay = jnp.exp(fl_c + m - m_new)
        w = jnp.exp(g_c - m_new[..., None])
        C_new = carry_decay[..., None, None] * C + jnp.einsum('bhs,bhsd,bhse->bhde', w, v_c, k_c)
        n_new = carry_decay[..., None] * n + jnp.einsum('bhs,bhse->bhe', w, k_c)
        return (C_new, n_new, m_new), (C, n, m)

    init = (jnp.zeros((Bsz, H, d, d), f32), jnp.zeros((Bsz, H, d), f32), jnp.zeros((Bsz, H), f32))
    cm = lambda z: jnp.moveaxis(z, 2, 0)
    _, (C0, n0, m0) = lax.scan(chunk_step, init, (cm(kc), cm(vc), cm(g_end), cm(F_last)))
    C0 = jnp.moveaxis(C0, 0, 2)
    n0 = jnp.moveaxis(n0, 0, 2)
    m0 = jnp.moveaxis(m0, 0, 2)
    D = F[..., :, None] - F[..., None, :] + ig[..., None, :]
    D = jnp.where(jnp.tril(jnp.ones((L, L), bool)), D, -jnp.inf)
    g_inter = F + m0[..., None]
    m_t = jnp.maximum(g_inter, jnp.max(D, axis=-1))
    Sw = jnp.einsum('bhctd,bhcsd->bhcts', qc, kc) * jnp.exp(D - m_t[..., None])
    inter = jnp.exp(g_inter - m_t)
    num = jnp.einsum('bhcts,bhcsd->bhctd', Sw, vc) + inter[..., None] * jnp.einsum('bhcde,bhcte->bhctd', C0, qc)
    den = jnp.sum(Sw, axis=-1) + inter * jnp.einsum('bhcd,bhctd->bhct', n0, qc)
    h = num / jnp.maximum(jnp.abs(den), jnp.exp(-m_t))[..., None]
    h = h.transpose(0, 2, 3, 1, 4).reshape(Bsz, T, H, d)
    h = h * lax.rsqrt(jnp.mean(h * h, axis=-1, keepdims=True) + EPS) * hn_g
    h = h.reshape(Bsz, T, B_WIDTH) * jax.nn.sigmoid(o.astype(f32))
    return h.astype(dt)

def sliding_window_sink_attention(q, k, v, qn_g, kn_g, sinks):
    dt = q.dtype
    f32 = jnp.float32
    Bsz, T, _ = q.shape
    Hkv, d, Bk = C_KV_HEADS, C_HEAD_DIM, C_BLOCK
    G = C_Q_HEADS // Hkv
    NB = T // Bk

    def hnorm(z, g):
        z = z.astype(f32)
        return z * lax.rsqrt(jnp.mean(z * z, axis=-1, keepdims=True) + EPS) * g

    qh = hnorm(q.reshape(Bsz, NB, Bk, Hkv, G, d), qn_g) * d ** -0.5
    kh = hnorm(k.reshape(Bsz, NB, Bk, Hkv, d), kn_g)
    vh = v.reshape(Bsz, NB, Bk, Hkv, d).astype(f32)

    def band(z):
        prev = jnp.pad(z, ((0, 0), (1, 0), (0, 0), (0, 0), (0, 0)))[:, :-1]
        return jnp.concatenate([prev, z], axis=2)

    kb, vb = band(kh), band(vh)
    s = jnp.einsum('bnqkgd,bnskd->bkgnqs', qh, kb)
    blk = jnp.arange(NB)[:, None, None]
    q_pos = blk * Bk + jnp.arange(Bk)[None, :, None]
    k_pos = (blk - 1) * Bk + jnp.arange(2 * Bk)[None, None, :]
    dist = q_pos - k_pos
    valid = (dist >= 0) & (dist < WINDOW) & (k_pos >= 0)
    slopes = alibi_slopes(C_Q_HEADS).reshape(Hkv, G)[None, :, :, None, None, None]
    s = jnp.where(valid, s - slopes * dist.astype(f32), -jnp.inf)
    sink = sinks.astype(f32).reshape(Hkv, G)[None, :, :, None, None, None]
    m = jnp.maximum(jnp.max(s, axis=-1, keepdims=True), sink)
    p = jnp.exp(s - m)
    den = jnp.sum(p, axis=-1, keepdims=True) + jnp.exp(sink - m)
    out = jnp.einsum('bkgnqs,bnskd->bnqkgd', p / den, vb)
    return out.reshape(Bsz, T, C_WIDTH).astype(dt)

def hybrid_mixer(h, w_in, mu_a, w0_a, w2_a, a0_a, a2_a, g2_a, kk_a, ka_a, rk_a, lnx_g_a, lnx_b_a,
                 conv_w_b, conv_b_b, bi_b, bf_b, hn_g_b, qn_g_c, kn_g_c, sink_c,
                 w_br_a, w_br_b, w_br_c, w_out):
    p = h @ w_in
    p_a, p_rest = p[..., :A_SHIFT_WIDTH], p[..., A_SHIFT_WIDTH:]
    p_a = p_a + mu_a * (token_shift(p_a) - p_a)
    rA, kA, vA, wloA, aloA, gloA = _split(p_a, A_SIZES)
    qB, kB, vB, oB, iB, fB, qC, kC, vC, gate_logits = _split(p_rest, REST_SIZES)
    y_a = rwkv7_time_mix(rA, kA, vA, wloA, aloA, gloA, w0_a, w2_a, a0_a, a2_a, g2_a,
                         kk_a, ka_a, rk_a, lnx_g_a, lnx_b_a)
    y_b = mlstm_chunkwise(qB, kB, vB, oB, iB, fB, conv_w_b, conv_b_b, bi_b, bf_b, hn_g_b)
    y_c = sliding_window_sink_attention(qC, kC, vC, qn_g_c, kn_g_c, sink_c)
    g_a, g_b, g_c = jnp.split(jax.nn.sigmoid(gate_logits), N_BRANCH, axis=-1)
    merged = g_a * (y_a @ w_br_a) + g_b * (y_b @ w_br_b) + g_c * (y_c @ w_br_c)
    return merged @ w_out

def hier_moe(h, w_rg, b_rg, w_re, b_re, w_e_in, w_e_out):
    f32 = jnp.float32
    Bsz, T, D = h.shape
    x = h.reshape(-1, D)
    NT = x.shape[0]
    g_prob = jax.nn.softmax((x @ w_rg).astype(f32) + b_rg.astype(f32), axis=-1)
    g_top, g_idx = lax.top_k(g_prob, 1)
    e_logits = ((x @ w_re).astype(f32) + b_re.astype(f32)).reshape(NT, N_GROUPS, EXPERTS_PER_GROUP)
    e_in_group = jnp.take_along_axis(e_logits, g_idx[:, :, None], axis=1)[:, 0]
    e_top, e_idx = lax.top_k(jax.nn.softmax(e_in_group, axis=-1), TOP_K)
    weights = g_top * e_top / jnp.sum(e_top, axis=-1, keepdims=True)
    expert = g_idx * EXPERTS_PER_GROUP + e_idx
    NA = NT * TOP_K
    a_exp = expert.reshape(-1).astype(jnp.int32)
    a_tok = jnp.repeat(jnp.arange(NT, dtype=jnp.int32), TOP_K)
    a_w = weights.reshape(-1)
    order = jnp.argsort(a_exp)
    s_exp = a_exp[order]
    counts = jax.ops.segment_sum(jnp.ones((NA,), jnp.int32), a_exp, num_segments=N_EXPERTS)
    starts = jnp.cumsum(counts) - counts
    padded = (counts + MOE_BLOCK - 1) // MOE_BLOCK * MOE_BLOCK
    pad_ends = jnp.cumsum(padded)
    pad_starts = pad_ends - padded
    dest = pad_starts[s_exp] + jnp.arange(NA, dtype=jnp.int32) - starts[s_exp]
    n_blocks = -(-NA // MOE_BLOCK) + N_EXPERTS
    n_slots = n_blocks * MOE_BLOCK
    slot_tok = jnp.zeros((n_slots,), jnp.int32).at[dest].set(a_tok[order])
    slot_w = jnp.zeros((n_slots,), f32).at[dest].set(a_w[order])
    block_exp = jnp.minimum(jnp.searchsorted(pad_ends, jnp.arange(n_blocks, dtype=jnp.int32) * MOE_BLOCK,
                                             side='right'), N_EXPERTS - 1)
    xb = x[slot_tok].reshape(n_blocks, MOE_BLOCK, D)

    def expert_block(args):
        xs, e = args
        gate, up = jnp.split(xs @ w_e_in[e], 2, axis=-1)
        return (jax.nn.silu(gate) * up) @ w_e_out[e]

    yb = lax.map(expert_block, (xb, block_exp)).reshape(n_slots, D)
    y = jnp.zeros((NT, D), f32).at[slot_tok].add(yb.astype(f32) * slot_w[:, None])
    return y.reshape(Bsz, T, D).astype(h.dtype)

def setup_inputs(seed: int = 0) -> dict:
    key = jax.random.key(seed)
    k = jax.random.split(key, 36)
    L, D = DEPTH, D_MODEL
    f32 = jnp.float32
    nrm = lambda kk, shape, std: std * jax.random.normal(kk, shape, f32)
    uni = lambda kk, shape, lo, hi: jax.random.uniform(kk, shape, f32, minval=lo, maxval=hi)
    ada_offset = jnp.array([0.0, 0.0, ADA_GATE_INIT, 0.0, 0.0, ADA_GATE_INIT], f32)[None, :, None]
    return {
        'x': nrm(k[0], (BATCH, SEQ, D), 1.0),
        'c': nrm(k[1], (BATCH, D), 1.0),
        'w_ada': nrm(k[2], (L, D, 6 * D), 0.1 * D ** -0.5),
        'b_ada': (nrm(k[3], (L, 6, D), 0.02) + ada_offset).reshape(L, 6 * D),
        'norm1_g': 1.0 + nrm(k[4], (L, D), 0.02),
        'norm2_g': 1.0 + nrm(k[5], (L, D), 0.02),
        'w_in': nrm(k[6], (L, D, N_IN), D ** -0.5),
        'mu_a': uni(k[7], (L, A_SHIFT_WIDTH), 0.0, 1.0),
        'w0_a': uni(k[8], (L, A_WIDTH), -6.0, 1.0),
        'w2_a': nrm(k[9], (L, A_DECAY_LORA, A_WIDTH), 0.1),
        'a0_a': nrm(k[10], (L, A_WIDTH), 0.5),
        'a2_a': nrm(k[11], (L, A_ICL_LORA, A_WIDTH), 0.5 * A_ICL_LORA ** -0.5),
        'g2_a': nrm(k[12], (L, A_GATE_LORA, A_WIDTH), A_GATE_LORA ** -0.5),
        'kk_a': 0.85 + nrm(k[13], (L, A_WIDTH), 0.1),
        'ka_a': 1.0 + nrm(k[14], (L, A_WIDTH), 0.1),
        'rk_a': nrm(k[15], (L, A_HEADS, A_HEAD_DIM), 0.1),
        'lnx_g_a': 1.0 + nrm(k[16], (L, A_WIDTH), 0.02),
        'lnx_b_a': nrm(k[17], (L, A_WIDTH), 0.02),
        'conv_w_b': nrm(k[18], (L, B_CONV, 2 * B_WIDTH), B_CONV ** -0.5),
        'conv_b_b': nrm(k[19], (L, 2 * B_WIDTH), 0.02),
        'bi_b': nrm(k[20], (L, B_HEADS), 0.1),
        'bf_b': jnp.linspace(3.0, 6.0, B_HEADS, dtype=f32)[None] + nrm(k[21], (L, B_HEADS), 0.1),
        'hn_g_b': 1.0 + nrm(k[22], (L, B_HEADS, B_HEAD_DIM), 0.02),
        'qn_g_c': 1.0 + nrm(k[23], (L, C_HEAD_DIM), 0.02),
        'kn_g_c': 1.0 + nrm(k[24], (L, C_HEAD_DIM), 0.02),
        'sink_c': nrm(k[25], (L, C_Q_HEADS), 0.5),
        'w_br_a': nrm(k[26], (L, A_WIDTH, D), A_WIDTH ** -0.5),
        'w_br_b': nrm(k[27], (L, B_WIDTH, D), B_WIDTH ** -0.5),
        'w_br_c': nrm(k[28], (L, C_WIDTH, D), C_WIDTH ** -0.5),
        'w_out': nrm(k[29], (L, D, D), D ** -0.5),
        'w_rg': nrm(k[30], (L, D, N_GROUPS), D ** -0.5),
        'b_rg': nrm(k[31], (L, N_GROUPS), 0.01),
        'w_re': nrm(k[32], (L, D, N_EXPERTS), D ** -0.5),
        'b_re': nrm(k[33], (L, N_EXPERTS), 0.01),
        'w_e_in': nrm(k[34], (L, N_EXPERTS, D, 2 * D_EXPERT), D ** -0.5),
        'w_e_out': nrm(k[35], (L, N_EXPERTS, D_EXPERT, D), D_EXPERT ** -0.5),
    }

def reference(x, c, w_ada, b_ada, norm1_g, norm2_g, w_in, mu_a, w0_a, w2_a, a0_a, a2_a, g2_a,
              kk_a, ka_a, rk_a, lnx_g_a, lnx_b_a, conv_w_b, conv_b_b, bi_b, bf_b, hn_g_b,
              qn_g_c, kn_g_c, sink_c, w_br_a, w_br_b, w_br_c, w_out, w_rg, b_rg, w_re, b_re,
              w_e_in, w_e_out):
    cond = jax.nn.silu(c)
    for l in range(DEPTH):
        mod = cond @ w_ada[l] + b_ada[l]
        sh1, sc1, gt1, sh2, sc2, gt2 = jnp.split(mod[:, None, :], 6, axis=-1)
        h = rms_norm(x, norm1_g[l]) * (1 + sc1) + sh1
        y = hybrid_mixer(h, w_in[l], mu_a[l], w0_a[l], w2_a[l], a0_a[l], a2_a[l], g2_a[l],
                         kk_a[l], ka_a[l], rk_a[l], lnx_g_a[l], lnx_b_a[l],
                         conv_w_b[l], conv_b_b[l], bi_b[l], bf_b[l], hn_g_b[l],
                         qn_g_c[l], kn_g_c[l], sink_c[l],
                         w_br_a[l], w_br_b[l], w_br_c[l], w_out[l])
        x = x + gt1 * y
        h = rms_norm(x, norm2_g[l]) * (1 + sc2) + sh2
        x = x + gt2 * hier_moe(h, w_rg[l], b_rg[l], w_re[l], b_re[l], w_e_in[l], w_e_out[l])
    return x


_drawn_inputs = setup_inputs


def setup_inputs(seed=0):
    import zlib

    import numpy as np

    out = dict(_drawn_inputs(seed))
    spreads = {}
    factors = {'norm1_g': 4.242,
     'norm2_g': 3.757,
     'w2_a': 5.4,
     'kk_a': 3.041,
     'ka_a': 2.678,
     'lnx_g_a': 19.658,
     'lnx_b_a': 22.72,
     'conv_b_b': 25.233,
     'bi_b': 200.0,
     'hn_g_b': 22.551,
     'qn_g_c': 8.0,
     'kn_g_c': 8.0,
     'sink_c': 200.0,
     'b_rg': 5.665,
     'b_re': 7.348}
    for name, (base, spread) in spreads.items():
        noise = np.random.default_rng([zlib.crc32(name.encode()), seed]).standard_normal(out[name].shape)
        drawn = base * np.exp(spread * noise) if base else spread * noise
        out[name] = __import__('jax').numpy.asarray(drawn.astype(out[name].dtype))
    for name, factor in factors.items():
        out[name] = (out[name] * factor).astype(out[name].dtype)
    return out
```

```python
import concourse.bass as bass
from concourse import mybir
from contextlib import ExitStack

T, D = 1024, 1024
P = 128
NT, KT = T // P, D // P
H, N = 4, 64
CH = 8
NG, NE, TOPK, DE = 4, 32, 2, 512
NX = (T * TOPK - 1) // P
NB = NE + NX
NBP = 48
EPS, A_EPS = 1e-6, 64e-5
KAPPA = 0.6065306597126334
BIG = 1e30


def hybrid_block(nc, I, out, dram):
    f32, i32 = mybir.dt.float32, mybir.dt.int32
    ALU, ACT, AX = mybir.AluOpType, mybir.ActivationFunctionType, mybir.AxisListType.X
    ds, ts = bass.ds, bass.ts
    x1_d, xn_d, yslot_d, table_d, gates_d = dram

    ctx = ExitStack()
    with ctx:
        SB = ctx.enter_context(nc.sbuf_tensor("arena", [P, 52992], f32))[:, :]
        PS = [ctx.enter_context(nc.psum_tensor(f"bank{i}", [P, 512], f32))[:, :] for i in range(8)]
        sems = {}

        def sem(name):
            if name not in sems:
                sems[name] = ctx.enter_context(nc.semaphore(name))
            return sems[name]

        def view(off, *dims):
            n = 1
            for d in dims:
                n *= d
            v = SB[:, off:off + n]
            if len(dims) == 2:
                v = v.rearrange("p (a b) -> p a b", a=dims[0])
            if len(dims) == 3:
                v = v.rearrange("p (a b c) -> p a b c", a=dims[0], b=dims[1])
            return v

        B_CLEARED, G_AX, G_LF, G_Z, G_D, G_MR, G_ARGS = range(1, 8)
        G_F, G_ZT, G_ZM, G_MT = range(1, 5)
        G_LN, G_DONE = range(1, 3)
        VECS, MOD1 = range(1, 3)
        R_MS, SLOTS_KNOWN = range(1, 3)
        CONSTS, R_IOTA = range(1, 3)
        COND, A_TANH, A_GSIG = range(1, 4)
        ROOT_KK = NT
        ROOT_A = ROOT_KK + 4

        RING = [view(0, 8, 512), view(4096, 8, 512)]
        HT = view(8192, KT, T)
        PA = view(16384, 8, T)
        ADA = [view(16384, 8, 512), view(20480, 8, 512)]
        QK = view(24576, 4, T)
        VO = view(28672, NT, 512)
        XB = [view(28672 + 1024 * i, D) for i in range(4)]
        QC = view(32768, 4, T)
        KC = view(36864, 9 * P)
        VC = view(38016, 9, 2, 65)
        TMP0 = 39296
        CS = view(TMP0, 2, 9, 129)
        KK = view(TMP0 + 2322, 2, T)
        BA = view(TMP0 + 4370, 2, T)
        TMP1 = TMP0 + 6418
        RAW = [view(TMP1, 1028), view(TMP1 + 1028, 1028)]
        at = [TMP1 + 2056]

        def small(*dims):
            n = 1
            for d in dims:
                n *= d
            v = view(at[0], *dims)
            at[0] += n
            assert at[0] <= 52992, at[0]
            return v

        ident, ones = small(P), small(P)
        msk = small(4, P)
        sU, U = msk[:, 0, :], msk[:, 1, :]
        dist = small(2, 2 * P)
        blk1 = small(P)
        hd2 = small(2)
        id64 = small(N)
        lvl = small(7, P)
        lnxg, lnxb, hng = small(256), small(256), small(256)
        w2a2 = small(256)
        g2s = small(256)
        wr = small(KT, 36)
        br = small(36)
        vecs = small(112)
        at_v = [0]

        def vcol(n):
            at_v[0] += n
            return vecs[:, at_v[0] - n:at_v[0]]

        badac, n1g, n2g, mu = vcol(48), vcol(8), vcol(8), vcol(8)
        w0c, a0c, kkc, kac, rkc = (vcol(2) for _ in range(5))
        cb, cw, cond, qkg = vcol(4), vcol(16), vcol(8), vcol(2)
        cw = cw.rearrange("p (j i) -> p j i", j=4)
        vrow = view(24576, P)
        sh1, sc1, sh2, sc2 = small(8), small(8), small(8), small(8)
        kac1 = small(2)
        bif = small(8)
        sinkr, sinkb = small(8), small(8)
        ss, rstd = small(8), small(8)
        gif = small(NT, 8)
        eps24 = small(1)
        rowb = RAW[1][:, 4:516]
        acc = small(512)

        c_sc = view(TMP0, 8, 2 * P)
        c_pT = view(TMP0 + 2048, 16, P)
        c_q = view(TMP0 + 4096, 4, P)
        c_y = view(TMP0 + 4608, 8, N)
        c_mx, c_nm, c_es, c_dn = (view(TMP0 + 5120 + 8 * i, 8) for i in range(4))
        c_k = view(TMP0 + 5160, 2 * P)
        c_sq = view(TMP0, T)
        c_rs = [view(TMP0 + 1024, 512), view(TMP0 + 1536, 512)]
        b0 = [TMP0]

        def btmp(*dims):
            n = 1
            for d in dims:
                n *= d
            v = view(b0[0], *dims)
            b0[0] += n
            assert b0[0] <= TMP1
            return v

        g_x, g_ax, g_lf, g_F, g_FL, g_Z, g_ZM = (btmp(32) for _ in range(7))
        g_M = btmp(H, 9)
        g_ml, g_dec, g_w, g_mt, g_int, g_emt, g_t = (btmp(32) for _ in range(7))
        g_zT, g_cm, g_mr, g_D = btmp(P), btmp(P), btmp(P), btmp(32)
        g_mc = btmp(1)
        b_q, b_k, b_kt = btmp(2, P), btmp(2, P), btmp(256)
        b_v, b_wv, b_st = btmp(H, 65), btmp(H, 65), btmp(2, 65)
        b_bd, b_e, b_sw = btmp(H, P), btmp(H, P), btmp(H, P)
        b_h, b_hh, b_sq = btmp(H, 65), btmp(H, N), btmp(H, N)
        b_d, b_rd, b_ms = btmp(H), btmp(H), btmp(H)
        a0_ = [28672]

        def atmp(*dims):
            n = 1
            for d in dims:
                n *= d
            if a0_[0] <= 32768 < a0_[0] + n:
                a0_[0] = 36864
            if 36864 < a0_[0] < TMP0 < a0_[0] + n:
                a0_[0] = 26624
            v = view(a0_[0], *dims)
            a0_[0] += n
            assert a0_[0] <= TMP0 and (a0_[0] <= 28672 or n + a0_[0] > 28672)
            return v

        a_sm = atmp(H, 4, P)
        a_lo = [atmp(H, P), atmp(H, P)]
        a_T, a_Tt = atmp(H, P), atmp(H, P)
        a_A1, a_AZ, a_WU = atmp(H, P), atmp(H, P), atmp(H, P)
        a_tok = atmp(3, 256)
        a_ar, a_bk = atmp(2, 2, P), atmp(2, 2, P)
        a_v, a_rk = atmp(2, P), view(TMP1, 2, P)
        a_sg = view(TMP1 + 256, P)
        a_wr = view(TMP1 + 384, 2, P)
        a_e = view(TMP1 + 640, 2, 129)
        a_ei = view(TMP1 + 898, 2, P)
        a_qs = view(TMP1 + 1154, 2, N)
        a_st = view(TMP1 + 1282, 2, N)
        a_gs = view(TMP1 + 1410, 2, N)
        a_nb, a_g = view(TMP1 + 1538, 2), view(TMP1 + 1540, 2)
        a_pb = view(TMP1 + 1542, 2)
        a_y = view(TMP1 + 1544, H, N)
        a_t4, a_m4, a_bon = view(TMP1 + 1800, H), view(TMP1 + 1804, H), view(TMP1 + 1808, H)
        a_y2 = acc[:, 0:256].rearrange("p (h n) -> p h n", h=H)
        a_sgt = view(TMP1 + 1812, 2)
        MT = [view(18432 + T * c, T) for c in range(6)] + [view(26624, T), view(27648, T)]
        YT = [PA[:, 0], PA[:, 1], QK[:, 0], QK[:, 1], QC[:, 0], QC[:, 1], QC[:, 2], QC[:, 3]]
        m_sg = [view(TMP0 + 512 * i, 512) for i in range(4)]
        m_t = [view(TMP0 + 2048 + 512 * i, 512) for i in range(2)]
        o_x = [view(28672 + 1024 * i, D) for i in range(2)]
        o_n = [view(30720 + 1024 * i, D) for i in range(2)]
        gt1, gtb = view(36864, D), view(37888, D)
        o_hT = view(TMP0 + 1024, KT, P)
        o_sq = view(TMP0 + 2048, D)
        r_lg = view(TMP0 + 3072, NT, 36)
        r0_ = [TMP0 + 3072 + 288]

        def rtmp(*dims):
            n = 1
            for d in dims:
                n *= d
            v = view(r0_[0], *dims)
            r0_[0] += n
            assert r0_[0] <= TMP1 + 2056
            return v

        r_8 = [rtmp(NT) for _ in range(10)]
        r_g4 = [rtmp(NT, NG) for _ in range(3)]
        r_m1, r_m2 = rtmp(NT, NE), rtmp(NT, NE)
        r_em, r_t = rtmp(NT, NE), rtmp(NT, NE)
        r_cnt, r_nx, r_cum, r_ov, r_io = (rtmp(NE) for _ in range(5))
        r_i4, r_ij = rtmp(NG), rtmp(NX)
        r_ex = rtmp(NX, NE)
        r_exs = rtmp(NX + 1)
        sb_i = ctx.enter_context(nc.sbuf_tensor("ints", [P, 160], i32))[:, :]
        i_tok, i_s1, i_s2, i_t1, i_t2 = (sb_i[:, 8 * k:8 * k + 8] for k in range(5))
        i_tab = sb_i[:, 40:40 + NBP]
        i_ex = sb_i[:, 88:88 + NX + 1]
        i_z = sb_i[:, 104:104 + NBP]
        i_hi, i_lo = sb_i[:, 104:112], sb_i[:, 112:120]
        i_ix = [sb_i[:, 152:153], sb_i[:, 153:154], sb_i[:, 154:155]]
        WE = [[view(12288 * s + 4096 * j, 4, 1024) for j in range(3)] for s in range(2)]
        e_xs = [view(24576, D), view(25600, D)]
        e_xT = [view(26624, KT, P), view(27648, KT, P)]
        e_h, e_hT, e_g = view(32768, DE), view(33280, 4, P), view(33792, DE)
        e_y = [view(34304, D), view(35328, D)]
        f_y = [[view(4096 * i, D), view(4096 * i + 1024, D)] for i in range(2)]
        f_x = [view(4096 * i + 2048, D) for i in range(2)]
        f_o = [view(4096 * i + 3072, D) for i in range(2)]
        gt2, gt2b = view(8192, D), view(9216, D)

        def bc(ap, n):
            return ap.unsqueeze(2).to_broadcast([ap.shape[0], ap.shape[1], n])

        def mm(o, l, r, start=True, stop=True):
            return nc.tensor.matmul(o, l, r, start=start, stop=stop)

        V, A, G, E = nc.vector, nc.scalar, nc.gpsimd, nc.tensor
        TT, TS, STT = V.tensor_tensor, V.tensor_scalar, V.scalar_tensor_tensor

        w_in = I["w_in"][0].rearrange("(k p) n -> p k n", p=P)
        w_ada = I["w_ada"][0].rearrange("(k p) n -> p k n", p=P)
        w_out = I["w_out"][0].rearrange("(k p) n -> p k n", p=P)
        w_bra = I["w_br_a"][0].rearrange("(k p) n -> p k n", p=P)
        w_brb = I["w_br_b"][0].rearrange("(k p) n -> p k n", p=P)
        w_brc = I["w_br_c"][0].rearrange("(a i q) n -> a q i n", a=2, q=N)
        x_t = I["x"][0].rearrange("(t p) n -> t p n", p=P)
        out_t = out[0].rearrange("(t p) n -> t p n", p=P)
        x1_t = x1_d.rearrange("(t p) n -> t p n", p=P)
        xn_t = xn_d.rearrange("(t p) n -> t p n", p=P)
        ys_b = yslot_d.rearrange("(b p) n -> b p n", p=P)
        OFF_QK, OFF_VO, OFF_IF, OFF_QC, OFF_KC, OFF_G = 1024, 1536, 2048, 2056, 2568, 2824

        def as_rows(ap):
            while len(ap.shape) > 1:
                ap = ap[0] if ap.shape[0] == 1 else ap.rearrange("a b -> (a b)")
            return ap.rearrange("(k p) -> k p", p=P)

        vec_rows, n = [], 0
        for name in ("b_ada", "norm1_g", "norm2_g", "mu_a", "w0_a", "a0_a", "kk_a", "ka_a", "rk_a", "conv_b_b", "conv_w_b", "c"):
            src = as_rows(I[name])
            vec_rows.append((vrow[n:n + src.shape[0], :], src))
            n += src.shape[0]
        for k, name in enumerate(("qn_g_c", "kn_g_c")):
            for a in range(2):
                vec_rows.append((vrow[n + k:n + k + 1, N * a:N * a + N], I[name]))
        NV = n + 2

        def slot_loads(r):
            w = RING[r % 2]
            flat = w.rearrange("p k n -> p (k n)")
            if r == 0:
                return [(w[:, :, P * i + N * a:P * i + N * a + N],
                         w_in[:, :, OFF_QC + 256 * a + N * i:OFF_QC + 256 * a + N * i + N])
                        for i in range(4) for a in range(2)]
            if r == 1:
                return [(w[:, :, 0:256], w_in[:, :, OFF_KC:OFF_KC + 256]),
                        (w[:, :, 256:264], w_in[:, :, OFF_IF:OFF_IF + 8])]
            if r < 6:
                o = {2: OFF_QK, 3: OFF_VO, 4: 0, 5: 512}[r]
                return [(w[:, :, :], w_in[:, :, o:o + 512])]
            if r < 14:
                c = r - 6
                g = flat[:, 0:3072].rearrange("p (k a n) -> p k a n", k=8, a=3)
                b = flat[:, 3072:4096].rearrange("p (k n) -> p k n", k=8)
                cs = slice(c * P, c * P + P)
                return [(g[:, :, a, :], w_in[:, :, OFF_G + D * a + c * P:OFF_G + D * a + c * P + P]) for a in range(3)] + \
                       [(b[:, 0:2, :], w_bra[:, :, cs]), (b[:, 2:4, :], w_brb[:, :, cs]),
                        (b[0:64, 4:8, :], w_brc[0, :, :, cs]), (b[64:128, 4:8, :], w_brc[1, :, :, cs])]
            return [(w[:, :, :], w_out[:, :, 512 * (r - 14):512 * (r - 13)])]

        slot_count = [0, 0]
        slot_target = []
        for r in range(16):
            slot_count[r % 2] += 16 * len(slot_loads(r))
            slot_target.append(slot_count[r % 2])
        s_slot = [sem("weights_slot0"), sem("weights_slot1")]

        smalls = [
            (bif[:, 0:4], I["bi_b"].to_broadcast([P, 4])), (bif[:, 4:8], I["bf_b"].to_broadcast([P, 4])),
            (lnxg, I["lnx_g_a"].to_broadcast([P, 256])), (lnxb, I["lnx_b_a"].to_broadcast([P, 256])),
            (hng, I["hn_g_b"].rearrange("a h n -> a (h n)").to_broadcast([P, 256])),
            (w2a2[0:64, :], I["w2_a"][0]), (w2a2[64:128, :], I["a2_a"][0]), (g2s, I["g2_a"][0]),
            (wr[:, :, 0:4], I["w_rg"][0].rearrange("(k p) n -> p k n", p=P)),
            (wr[:, :, 4:36], I["w_re"][0].rearrange("(k p) n -> p k n", p=P)),
            (br[:, 0:4], I["b_rg"].to_broadcast([P, 4])), (br[:, 4:36], I["b_re"].to_broadcast([P, 32])),
            (sinkr, I["sink_c"].to_broadcast([P, CH])),
        ]

        block = ctx.enter_context(nc.Block())

        @block.sync
        def _(sp):
            for t in range(4):
                sp.dma_start(XB[t], x_t[t]).then_inc(sem(f"rows_in{t % 4}"), 16)

            def ada(i):
                if i >= 2:
                    sp.wait_ge(sem("ada_acc"), i - 1)
                sp.dma_start(ADA[i % 2], w_ada[:, :, 512 * i:512 * i + 512]).then_inc(sem(f"wide_in{i % 2}"), 16)

            def weights(r):
                if 2 <= r < 8:
                    sp.wait_ge(sem("proj"), (8, 18, 26, 34, 42, 50)[r - 2])
                if r >= 8:
                    sp.wait_ge(sem("m_pair"), 6 * (r - 7))
                for dst, src in slot_loads(r):
                    sp.dma_start(dst, src).then_inc(s_slot[r % 2], 16)

            for i in range(4):
                ada(i)
            for t in range(4, NT):
                sp.wait_ge(sem("x_used"), t - 3)
                sp.dma_start(XB[t % 4], x_t[t]).then_inc(sem(f"rows_in{t % 4}"), 16)
            weights(0)
            weights(1)
            for i in range(4, 12):
                ada(i)
            for r in range(2, 16):
                weights(r)

            sp.wait_ge(sem("row_out"), 16 * 4)
            sp.wait_ge(sem("m_pair"), 6)
            sp.dma_start(gt1, gates_d[0:1, :].to_broadcast([P, D])).then_inc(sem("gt1_in"), 16)
            sp.dma_start(gtb, I["b_ada"][:, 2 * D:3 * D].to_broadcast([P, D])).then_inc(sem("gt1_in"), 16)
            for t in range(NT):
                if t >= 2:
                    sp.wait_ge(sem(f"rows_st{t % 2}"), 16 * (t // 2))
                    sp.wait_ge(sem("o_norm"), t - 1)
                    sp.wait_ge(sem("o_ss"), t - 1)
                sp.dma_start(o_x[t % 2], x_t[t]).then_inc(sem(f"rows_in{t % 2}"), 16)

            def expert_weights(e, s, first):
                if not first:
                    sp.wait_ge(sem("win_used"), e - 1)
                for j in range(2):
                    if first:
                        sp.wait_ge(sem("o_mm"), 16)
                    sp.dma_start(WE[s][j], I["w_e_in"][0, ds(e, 1), 512 * j:512 * j + 512, :]
                                 .rearrange("a (k p) n -> p (a k) n", p=P)).then_inc(sem(f"win{s}_in"), 16)
                if not first:
                    sp.wait_ge(sem("y"), 2 * (e - 1))
                sp.dma_start(WE[s][2], I["w_e_out"][0, ds(e, 1)]
                             .rearrange("a (k p) n -> p (a k) n", p=P)).then_inc(sem(f"wout{s}_in"), 16)

            expert_weights(0, 0, True)
            expert_weights(1, 1, True)
            with sp.Fori(1, NE // 2) as i:
                for s in range(2):
                    expert_weights(2 * i + s, s, False)
            sp.wait_ge(sem("router_dve"), SLOTS_KNOWN)
            n_extra = sp.value_load(i_ex[0:1, NX:NX + 1], min_val=0, max_val=NX)
            sp.wait_ge(sem("y"), 2 * NE)
            with sp.Fori(0, NX) as j:
                with sp.If(n_extra > j):
                    e = sp.value_load(i_ex[0:1, ds(j, 1)], min_val=0, max_val=NE - 1)
                    sp.wait_ge(sem("extra_go"), j + 1)
                    for k in range(2):
                        sp.dma_start(WE[0][k], I["w_e_in"][0, ds(e, 1), 512 * k:512 * k + 512, :]
                                     .rearrange("a (k p) n -> p (a k) n", p=P)).then_inc(sem("extra_w"), 16)
                    sp.dma_start(WE[0][2], I["w_e_out"][0, ds(e, 1)]
                                 .rearrange("a (k p) n -> p (a k) n", p=P)).then_inc(sem("extra_w"), 16)
                with sp.Else():
                    sp.nop()
            sp.wait_ge(sem("extra_end"), 1)
            sp.dma_start(gt2, gates_d[1:2, :].to_broadcast([P, D])).then_inc(sem("gt2_in"), 16)
            sp.dma_start(gt2b, I["b_ada"][:, 5 * D:6 * D].to_broadcast([P, D])).then_inc(sem("gt2_in"), 16)
            for t in range(NT):
                if t >= 2:
                    sp.wait_ge(sem("f_sum"), t - 1)
                sp.dma_start(f_x[t % 2], x1_t[t]).then_inc(sem(f"rows_in{2 + t % 2}"), 16)

        @block.gpsimd
        def _(pool):
            chain = [0]

            def link(ins):
                chain[0] += 1
                ins.then_inc(sem("pool_step"), 1)
                pool.wait_ge(sem("pool_step"), chain[0])

            link(G.memset(ones, 1.0))
            link(G.memset(ident, 0.0))
            link(G.affine_select(out=ident, in_=ident, compare_op=ALU.not_equal, fill=1.0, base=0,
                                 pattern=[[-1, P]], channel_multiplier=1))
            link(G.memset(msk, 1.0))
            for k, op in ((0, ALU.is_gt), (1, ALU.is_ge)):
                link(G.affine_select(out=msk[:, k, :], in_=msk[:, k, :], compare_op=op, fill=0.0, base=0,
                                pattern=[[1, P]], channel_multiplier=-1))
                link(G.affine_select(out=msk[:, k + 2, :], in_=msk[:, k + 2, :], compare_op=op, fill=0.0, base=0,
                                pattern=[[1, P]], channel_multiplier=-1))
            link(G.memset(blk1, 0.0))
            link(G.memset(hd2, 0.0))
            link(G.memset(id64, 0.0))
            link(G.memset(lvl, 0.0))
            for a in range(2):
                link(G.memset(blk1[64 * a:64 * a + 64, 64 * a:64 * a + 64], 1.0))
                link(G.memset(hd2[64 * a:64 * a + 64, a:a + 1], 1.0))
                link(G.affine_select(out=id64[64 * a:64 * a + 64, :], in_=id64[64 * a:64 * a + 64, :], compare_op=ALU.not_equal,
                                fill=1.0, base=0, pattern=[[-1, N]], channel_multiplier=1))
            for q in range(7):
                n = 1 << q
                v = lvl[:, q, :].rearrange("p (a b c) -> p a b c", b=2, c=n)[:, :, 1, :]
                m = P // (2 * n)
                link(G.memset(v, 1.0))
                link(G.affine_select(out=v, in_=v, compare_op=ALU.is_ge, fill=0.0, base=0,
                                     pattern=[[-2 * n, m], [0, n]], channel_multiplier=1))
                link(G.affine_select(out=v, in_=v, compare_op=ALU.is_gt, fill=0.0, base=n,
                                     pattern=[[2 * n, m], [0, n]], channel_multiplier=-1))
            link(G.iota(dist, pattern=[[0, 2], [-1, 2 * P]], base=P, channel_multiplier=1,
                        allow_small_or_imprecise_dtypes=True))
            link(G.affine_select(out=dist, in_=dist, compare_op=ALU.is_ge, fill=BIG, base=P,
                                 pattern=[[0, 2], [-1, 2 * P]], channel_multiplier=1))
            link(G.affine_select(out=dist, in_=dist, compare_op=ALU.is_gt, fill=BIG, base=0,
                                 pattern=[[0, 2], [1, 2 * P]], channel_multiplier=-1))
            link(G.memset(dist[:, 0, 0:P], BIG))
            link(G.memset(KC[:, 0:P], 0.0))
            link(G.memset(VC[:, 0, :, 0:64], 0.0))
            link(G.memset(VC[:, :, :, 64:65], 1.0))
            link(G.memset(RAW[0][:, 0:3], 0.0))
            link(G.memset(RAW[1][:, 0:3], 0.0))
            link(G.iota(i_tok, pattern=[[P, NT]], base=0, channel_multiplier=1))
            link(G.memset(i_z, 0))
            G.memset(eps24, 1e-24).then_inc(sem("setup_pool"), 1)
            pool.wait_ge(sem("setup_pool"), CONSTS)
            pool.dma_start(table_d.rearrange("(p b) o -> p (b o)", p=P), i_z).then_inc(sem("table"), 16)

            pool.wait_ge(sem("c_normed"), 5)
            def attn(c, first=False):
                if not first:
                    pool.wait_ge(sem("c_scores"), c)
                G.tensor_copy(c_k, KC[:, ds(P * c, 2 * P)])
                G.tensor_copy(c_q, QC[:, :, ts(c, P)]).then_inc(sem("mix_staged"), 1)
            attn(0, True)
            with pool.Fori(1, NT) as c:
                attn(c)

            pool.wait_ge(sem("gates_dve"), B_CLEARED)
            pool.wait_ge(sem("b_silu"), 4)
            pool.wait_ge(sem("proj_out"), 34)
            def mlstm(c, first=False):
                if not first:
                    pool.wait_ge(sem("b_num"), c)
                    pool.wait_ge(sem("b_wv"), c)
                G.tensor_copy(b_q, QK[:, 0:2, ts(c, P)])
                G.tensor_copy(b_v[:, :, 0:64], VO[:, ds(c, 1), 0:256].rearrange("p o (h n) -> p (o h) n", h=H))\
                    .then_inc(sem("mix_staged"), 1)
                pool.wait_ge(sem("b_exp"), c + 1)
                G.tensor_tensor(b_e, b_e, U.unsqueeze(1).to_broadcast([P, H, P]), ALU.mult).then_inc(sem("b_masked"), 1)
            mlstm(0, True)
            with pool.Fori(1, NT) as c:
                mlstm(c)

            pool.wait_ge(sem("a_prep"), 1)
            def tmix(c, first=False):
                if not first:
                    pool.wait_ge(sem("a_tr"), c)
                G.tensor_copy(a_v, PA[:, 4:6, ts(c, P)]).then_inc(sem("mix_staged"), 1)
                pool.wait_ge(sem("a_sm"), 4 * c + 4)
                for q in range(7):
                    if q >= 2:
                        pool.wait_ge(sem("a_A1"), 7 * c + q - 1)
                    elif not first:
                        pool.wait_ge(sem("a_A1"), 7 * c)
                    if q == 2:
                        pool.wait_ge(sem("a_Tt"), 7 * c + 1)
                    G.tensor_tensor(a_lo[q % 2], a_sm[:, :, 0, :], lvl[:, q, :].unsqueeze(1).to_broadcast([P, H, P]),
                                    ALU.mult).then_inc(sem("a_lo"), 1)
            tmix(0, True)
            with pool.Fori(1, NT) as c:
                tmix(c)

            pool.wait_ge(sem("mix_done"), 3 * NT)
            link(G.memset(RAW[0][:, 0:D], 0.0))
            for b in range(NE, NB):
                pool.dma_start(ys_b[b], RAW[0][:, 0:D]).then_inc(sem("slots_zero"), 16)

            k = 0
            for c in range(8):
                for half in range(2):
                    hs = slice(512 * half, 512 * half + 512)
                    for b in range(1, 3):
                        pool.wait_ge(sem("m_prod"), 3 * (2 * c + half) + b + 1)
                        if k:
                            pool.wait_ge(sem("m_added"), k)
                        G.tensor_tensor(MT[c][:, hs], MT[c][:, hs], m_t[b - 1], ALU.add).then_inc(sem("m_added"), 1)
                        k += 1

            pool.wait_ge(sem("o_mm"), 2)
            link(G.iota(r_i4, pattern=[[1, NG]], base=0, channel_multiplier=0, allow_small_or_imprecise_dtypes=True))
            G.iota(r_io, pattern=[[1, NE]], base=0, channel_multiplier=0, allow_small_or_imprecise_dtypes=True)\
                .then_inc(sem("setup_pool"), 1)
            pool.wait_ge(sem("router_dve"), SLOTS_KNOWN)
            pool.wait_ge(sem("table"), 16)
            for t in range(NT):
                for ix in (i_t1, i_t2):
                    pool.indirect_dma_start(out=table_d, out_offset=bass.IndirectOffsetOnAxis(ap=ix[:, t:t + 1], axis=0),
                                            in_=i_tok[:, t:t + 1], in_offset=None).then_inc(sem("table"), 16)
            pool.wait_ge(sem("table"), 16 + 16 * 2 * NT)
            pool.dma_start(i_tab, table_d.rearrange("(p b) o -> p (b o)", p=P)).then_inc(sem("table"), 16)
            pool.wait_ge(sem("table"), 32 + 16 * 2 * NT)
            pool.wait_ge(sem("xn_st0"), 16 * NT // 2)
            pool.wait_ge(sem("xn_st1"), 16 * NT // 2)

            def gather(e, s, wait):
                G.tensor_copy(i_ix[s], i_tab[:, ds(e, 1)]).then_inc(sem("ix_set"), 1)
                pool.wait_ge(sem("ix_set"), e + 1)
                if wait:
                    pool.wait_ge(sem("xs_used"), e - 1)
                pool.sem_inc(sem("gather_go"), 1)
                pool.indirect_dma_start(out=e_xs[s], out_offset=None, in_=xn_d,
                                        in_offset=bass.IndirectOffsetOnAxis(ap=i_ix[s], axis=0))\
                    .then_inc(sem(f"xs{s}_in"), 16)
            gather(0, 0, False)
            gather(1, 1, False)
            with pool.Fori(1, NE // 2) as i:
                for s in range(2):
                    pool.wait_ge(sem(f"xs{s}_in"), 16 * i)
                    gather(2 * i + s, s, True)
            n_extra = pool.value_load(i_ex[0:1, NX:NX + 1], min_val=0, max_val=NX)
            pool.wait_ge(sem("xs_used"), NE)
            with pool.Fori(0, NX) as j:
                with pool.If(n_extra > j):
                    pool.wait_ge(sem("extra_go"), j + 1)
                    G.tensor_copy(i_ix[2], i_tab[:, ds(NE + j, 1)]).then_inc(sem("ix_set"), 1)
                    pool.wait_ge(sem("ix_set"), NE + 1 + j)
                    pool.sem_inc(sem("gather_go"), 1)
                    pool.indirect_dma_start(out=e_xs[0], out_offset=None, in_=xn_d,
                                            in_offset=bass.IndirectOffsetOnAxis(ap=i_ix[2], axis=0))\
                        .then_inc(sem("extra_xs"), 16)
                with pool.Else():
                    pool.nop()
            pool.wait_ge(sem("slots_zero"), 16 * NX)
            pool.wait_ge(sem("extra_end"), 1)
            for t in range(NT):
                if t >= 2:
                    pool.wait_ge(sem("f_sum"), t - 1)
                for k, ix in enumerate((i_s1, i_s2)):
                    pool.indirect_dma_start(out=f_y[t % 2][k], out_offset=None, in_=yslot_d,
                                            in_offset=bass.IndirectOffsetOnAxis(ap=ix[:, t:t + 1], axis=0))\
                        .then_inc(sem(f"fy_in{t % 2}"), 16)

        @block.tensor
        def _(pe):
            pe.wait_ge(sem("setup_pool"), CONSTS)
            pe.wait_ge(sem("vecs_in"), 16 * len(vec_rows))
            E.transpose(PS[7][:, 0:NV], vrow[0:NV, :], ident[0:NV, 0:NV]).then_inc(sem("vecs_T"), 1)
            def ada(i):
                pe.wait_ge(sem("ada_acc"), i + 1)
                if i % 6 < 4:
                    for q in range(4):
                        ins = mm(PS[6][:, 4 * i + q:4 * i + q + 1], acc[:, ts(q, P)], ones[:, 0:1])
                else:
                    if i == 4:
                        pe.wait_ge(sem("setup_dve"), VECS)
                    if i > 4:
                        pe.wait_ge(sem("row"), (5, 10, 11).index(i) + 1)
                    ins = mm(PS[7][:, :], ones, acc)
                ins.then_inc(sem("ada_sum"), 1)

            for i in range(4):
                ada(i)
            for t in range(NT):
                pe.wait_ge(sem("x_norm"), t + 1)
                if t >= 2:
                    pe.wait_ge(sem("xT_a"), t - 1)
                    pe.wait_ge(sem("xT_v"), t - 1)
                for k in range(KT):
                    ins = E.transpose(PS[2 * (t % 2) + k // 4][:, ts(k % 4, P)], XB[t % 4][:, ts(k, P)], ident)
                ins.then_inc(sem("x_used"), 1)
            pe.wait_ge(sem("xT_a"), NT)
            pe.wait_ge(sem("xT_v"), NT)

            g = [0]

            def group(width, operands, lastslot=None):
                b = PS[g[0] % 2]
                if g[0] >= 2:
                    pe.wait_ge(sem("proj_out"), g[0] - 1)
                for k in range(KT):
                    l, r = operands(k)
                    ins = mm(b[:, 0:width], l, r, k == 0, k == KT - 1)
                ins.then_inc(sem("proj"), 1)
                g[0] += 1
                return ins

            def by_channel(r, n_tiles, after=None):
                pe.wait_ge(s_slot[r % 2], slot_target[r])
                w = RING[r % 2]
                for i in range(n_tiles):
                    for half in range(2):
                        group(512, lambda k: (w[:, k, ts(i, P)], HT[:, k, ts(half, 512)]))
                    if after:
                        after(i)

            def c_norm(i):
                for half in range(2):
                    pe.wait_ge(sem("c_sq"), 2 * i + half + 1)
                    if i:
                        pe.wait_ge(sem("c_rs"), 2 * i + half - 1)
                    mm(PS[2 + half], blk1, c_sq[:, ts(half, 512)]).then_inc(sem("c_ss"), 1)

            def after_q(i):
                if i:
                    c_norm(i - 1)
                    ada(2 * i + 2)
                    ada(2 * i + 3)

            by_channel(0, 4, after_q)
            pe.wait_ge(s_slot[1], slot_target[1])
            w1 = RING[1]
            for half in range(2):
                group(512, lambda k: (w1[:, k, 0:P], HT[:, k, ts(half, 512)]))
            c_norm(3)
            ada(10)
            ada(11)
            for t in range(NT):
                group(136, lambda k: (HT[:, k, ts(t, P)], w1[:, k, P:264]))
                if t == 0:
                    c_norm(4)
            by_channel(2, 4)
            pe.wait_ge(s_slot[1], slot_target[3])
            for t in range(NT):
                group(512, lambda k: (HT[:, k, ts(t, P)], RING[1][:, k, :]))

            pe.wait_ge(sem("c_normed"), 5)
            pe.wait_ge(sem("proj_out"), g[0])
            def attn(c, first=False):
                pe.wait_ge(sem("mix_staged"), c + 1)
                for a in range(2):
                    for i in range(4):
                        ins = mm(PS[2 + 2 * a + i // 2][:, ts(i % 2, 2 * P)], c_q[64 * a:64 * a + 64, i, :],
                                 c_k[64 * a:64 * a + 64, :])
                ins.then_inc(sem("c_scores"), 1)
                pe.wait_ge(sem("c_p"), c + 1)
                for j in range(16):
                    ins = E.transpose(PS[2 + j // 4][:, ts(j % 4, P)], c_sc[:, j // 2, ts(j % 2, P)], ident)
                    if j % 4 == 3:
                        ins.then_inc(sem("c_pT"), 1)
                pe.wait_ge(sem("c_pT_out_v"), c + 1)
                pe.wait_ge(sem("c_pT_out_a"), c + 1)
                for j in range(8):
                    o = PS[6 + j // 4][:, ds(65 * (j % 4), 65)]
                    for kb in range(2):
                        ins = mm(o, c_pT[:, 2 * j + kb, :], VC[:, ds(c + kb, 1), j % 2, :].rearrange("p o n -> p (o n)"),
                                 kb == 0, kb == 1)
                ins.then_inc(sem("c_pv"), 1)
                pe.wait_ge(sem("mix_y"), c + 1)
                for i in range(4):
                    ins = E.transpose(PS[0][:, ts(i, P)], c_y[:, 2 * i:2 * i + 2, :].rearrange("p a n -> p (a n)"), ident)
                ins.then_inc(sem("mix_yT"), 1)
            attn(0, True)
            with pe.Fori(1, NT) as c:
                attn(c)
            pe.wait_ge(sem("mix_done"), NT)

            by_channel(4, 4)
            by_channel(5, 4)

            pe.wait_ge(sem("gates_dve"), G_LF)
            mm(PS[6][:, 0:32], U, g_lf)
            mm(PS[6][:, 32:64], ones, g_lf).then_inc(sem("gates_pe"), 1)
            pe.wait_ge(sem("gates_dve"), G_Z)
            E.transpose(PS[7][0:32, 0:P], g_Z, ident).then_inc(sem("gates_pe"), 1)
            pe.wait_ge(sem("gates_dve"), G_D)
            mm(PS[6][:, 64:96], ones[0:32, :], g_D[0:32, :]).then_inc(sem("gates_pe"), 1)
            pe.wait_ge(sem("gates_dve"), G_MR)
            E.transpose(PS[7][:, 128:160], g_mr[0:32, :], ident[0:32, 0:32]).then_inc(sem("gates_pe"), 1)
            pe.wait_ge(sem("gates_act"), G_DONE)
            pe.wait_ge(sem("proj_out"), g[0])

            def mlstm(c, first=False):
                pe.wait_ge(sem("mix_staged"), NT + c + 1)
                pe.wait_ge(sem("b_k"), c + 1)
                pe.wait_ge(sem("b_bd"), c + 1)
                mm(PS[0], ones[0:32, :], b_bd[0:32]).then_inc(sem("b_mu"), 1)
                for a in range(2):
                    for p in range(2):
                        ins = mm(PS[1 + a][:, ts(p, P)], b_k[64 * a:64 * a + 64, p, :], b_q[64 * a:64 * a + 64, p, :])
                for p in range(2):
                    ins = E.transpose(PS[3][:, ts(p, P)], b_k[:, p, :], ident)
                ins.then_inc(sem("b_scores"), 1)
                if not first:
                    pe.wait_ge(sem("b_state"), c)
                for a in range(2):
                    for p in range(2):
                        ins = mm(PS[5 + a][:, ds(65 * p, 65)], b_q[64 * a:64 * a + 64, p, :], b_st[64 * a:64 * a + 64, p, :])
                pe.wait_ge(sem("b_kt"), c + 1)
                pe.wait_ge(sem("b_wv"), c + 1)
                for h in range(H):
                    a, p = h % 2, h // 2
                    ins = mm(PS[7][64 * a:64 * a + 64, ds(65 * p, 65)], b_kt[:, ts(h, N)], b_wv[:, h, :])
                ins.then_inc(sem("b_inter"), 1)
                pe.wait_ge(sem("b_sw"), c + 1)
                for h in range(H):
                    ins = mm(PS[4][:, ds(65 * h, 65)], b_sw[:, h, :], b_v[:, h, :])
                ins.then_inc(sem("b_num"), 1)
                pe.wait_ge(sem("mix_y"), NT + c + 1)
                for p in range(2):
                    ins = E.transpose(PS[3][:, ts(2 + p, P)], b_hh[:, 2 * p:2 * p + 2, :].rearrange("p a n -> p (a n)"), ident)
                ins.then_inc(sem("mix_yT"), 1)
            mlstm(0, True)
            with pe.Fori(1, NT) as c:
                mlstm(c)
            pe.wait_ge(sem("mix_done"), NT + NT)

            pe.wait_ge(sem("setup_act"), A_TANH)
            q = 0
            for p in range(2):
                for half in range(2):
                    hs = slice(512 * half, 512 * half + 512)
                    if q >= 2:
                        pe.wait_ge(sem("a_sig"), 2 * (q - 1))
                    mm(PS[2 * (q % 2)], w2a2[0:64, ts(p, P)], PA[0:64, 6, hs])
                    mm(PS[2 * (q % 2) + 1], w2a2[64:128, ts(p, P)], PA[64:128, 6, hs]).then_inc(sem("a_lora"), 1)
                    q += 1
            for q in range(4):
                pe.wait_ge(sem("a_sq"), q + 1)
                if q >= 2:
                    pe.wait_ge(sem("a_kkn"), q - 1)
                mm(PS[4 + q % 2], blk1, RAW[q % 2][:, 0:512]).then_inc(sem("a_ss"), 1)
            pe.wait_ge(sem("a_prep"), 1)

            def tmix(c, first=False):
                pe.wait_ge(sem("a_abkr"), c + 1)
                pe.wait_ge(sem("mix_staged"), 2 * NT + c + 1)
                for p in range(2):
                    E.transpose(PS[0][:, ts(p, P)], a_ar[:, p, 0, :], ident)
                    E.transpose(PS[0][:, ts(2 + p, P)], a_bk[:, p, 0, :], ident)
                    E.transpose(PS[1][:, ts(p, P)], a_bk[:, p, 1, :], ident)
                    ins = E.transpose(PS[1][:, ts(2 + p, P)], a_v[:, p, :], ident)
                ins.then_inc(sem("a_tr"), 1)
                for h in range(H):
                    a, p = h % 2, h // 2
                    rows = slice(64 * a, 64 * a + 64)
                    ar = a_ar[rows, p].rearrange("p a n -> p (a n)")
                    mm(PS[2 + h][:, 0:256], a_bk[rows, p, 0, :], ar)
                    mm(PS[2 + h][:, 256:512], a_bk[rows, p, 1, :], ar).then_inc(sem("a_scores"), 1)
                pe.wait_ge(sem("a_rk"), c + 1)
                pe.wait_ge(sem("a_sg"), c + 1)
                for p in range(2):
                    mm(PS[7][:, ds(256 + 2 * p, 2)], a_rk[:, p, :], hd2)
                mm(PS[7][:, 0:256], a_sg, g2s).then_inc(sem("a_gb"), 1)
                for q in range(7):
                    pe.wait_ge(sem("a_lo"), 7 * c + q + 1)
                    if q:
                        pe.wait_ge(sem("a_T"), 6 * c + q)
                        pe.wait_ge(sem("a_Tt"), 7 * c + q)
                    for h in range(H):
                        ins = mm(PS[2][:, ts(h, P)], a_lo[q % 2][:, h, :], ident if q == 0 else a_T[:, h, :])
                    ins.then_inc(sem("a_A1"), 1)
                    if q:
                        pe.wait_ge(sem("a_A1s"), 6 * c + q)
                        if q < 6:
                            for h in range(H):
                                ins = mm(PS[3][:, ts(h, P)], a_Tt[:, h, :], a_A1[:, h, :])
                            ins.then_inc(sem("a_P2"), 1)
                        for h in range(H):
                            ins = mm(PS[4][:, ts(h, P)], a_A1[:, h, :], a_Tt[:, h, :])
                        ins.then_inc(sem("a_Pt"), 1)
                pe.wait_ge(sem("a_tok"), c + 1)
                for h in range(H):
                    ins = mm(PS[5][:, ts(h, N)], a_sm[:, h, 2, :], a_tok[:, 2, ts(h, N)])
                ins.then_inc(sem("a_Z"), 1)
                pe.wait_ge(sem("a_Zs"), c + 1)
                pe.wait_ge(sem("a_Tt"), 7 * c + 7)
                for h in range(H):
                    ins = mm(PS[2][:, ts(h, P)], a_Tt[:, h, :], a_AZ[:, h, :])
                ins.then_inc(sem("a_WU"), 1)
                pe.wait_ge(sem("a_WUs"), c + 1)
                for h in range(H):
                    a, p = h % 2, h // 2
                    rows = slice(64 * a, 64 * a + 64)
                    mm(PS[3][rows, ts(p, P)], a_WU[:, h, 0:N], a_sm[:, h, 1, :])
                    ins = mm(PS[4][rows, ts(p, N)], a_WU[:, h, 0:N], a_tok[:, 0, ts(h, N)])
                for h in range(H):
                    a, p = h % 2, h // 2
                    rows = slice(64 * a, 64 * a + 64)
                    mm(PS[5][rows, ds(256 + 64 * p, N)], a_tok[:, 1, ts(h, N)], a_tok[:, 2, ts(h, N)], True, False)
                    ins = mm(PS[5][rows, ds(256 + 64 * p, N)], a_tok[:, 0, ts(h, N)], a_WU[:, h, N:P], False, True)
                ins.then_inc(sem("a_GS"), 1)
                pe.wait_ge(sem("a_Qs"), c + 1)
                if not first:
                    pe.wait_ge(sem("a_state"), c)
                for h in range(H):
                    o = PS[6][:, ts(h, N)]
                    mm(o, a_sm[:, h, 3, :], a_tok[:, 2, ts(h, N)], True, False)
                    mm(o, a_sm[:, h, 1, :], a_WU[:, h, N:P], False, True)
                for h in range(H):
                    a, p = h % 2, h // 2
                    rows = slice(64 * a, 64 * a + 64)
                    mm(PS[3 + a][:, ts(p, N)], a_wr[rows, p, :], a_st[rows, p, :])
                    ins = mm(PS[3 + a][rows, ts(2 + p, N)], a_qs[rows, p, :], a_st[rows, p, :])
                ins.then_inc(sem("a_Y"), 1)
                pe.wait_ge(sem("mix_y"), 2 * NT + c + 1)
                for p in range(2):
                    ins = E.transpose(PS[0][:, ts(p, P)], a_y[:, 2 * p:2 * p + 2, :].rearrange("p a n -> p (a n)"), ident)
                ins.then_inc(sem("mix_yT"), 1)
                pe.wait_ge(sem("mix_done"), 2 * NT + c + 1)
            tmix(0, True)
            with pe.Fori(1, NT) as c:
                tmix(c)

            n = 0
            for c in range(8):
                r = 6 + c
                pe.wait_ge(s_slot[r % 2], slot_target[r])
                flat = RING[r % 2].rearrange("p k n -> p (k n)")
                wg = flat[:, 0:3072].rearrange("p (k a n) -> p k a n", k=8, a=3)
                wb = flat[:, 3072:4096].rearrange("p (k n) -> p k n", k=8)
                for half in range(2):
                    hs = slice(512 * half, 512 * half + 512)
                    for b, (k0, k1) in enumerate(((0, 2), (2, 4), (4, 8))):
                        if n >= 4:
                            pe.wait_ge(sem("m_prod"), n - 3)
                        for k in range(KT):
                            mm(PS[2 * (n % 4)], wg[:, k, b, :], HT[:, k, hs], k == 0, k == KT - 1)
                        for k in range(k0, k1):
                            ins = mm(PS[2 * (n % 4) + 1], wb[:, k, :], YT[k][:, hs], k == k0, k == k1 - 1)
                        ins.then_inc(sem("m_pair"), 1)
                        n += 1
            pe.wait_ge(sem("m_added"), 32)
            pe.wait_ge(sem("m_prod"), 48)
            pe.wait_ge(s_slot[0], slot_target[14])
            pe.wait_ge(s_slot[1], slot_target[15])

            def router(t):
                pe.wait_ge(sem("o_norm"), t + 1)
                for k in range(KT):
                    ins = E.transpose(PS[4 + k // 4][:, ts(k % 4, P)], o_n[t % 2][:, ts(k, P)], ident)
                ins.then_inc(sem("o_T"), 1)
                pe.wait_ge(sem("o_hT_a"), t + 1)
                pe.wait_ge(sem("o_hT_v"), t + 1)
                if t:
                    pe.wait_ge(sem("r_lg"), t)
                for k in range(KT):
                    ins = mm(PS[6][:, 0:36], o_hT[:, k, :], wr[:, k, :], k == 0, k == KT - 1)
                ins.then_inc(sem("r_mm"), 1)

            for t in range(NT):
                for j in range(2):
                    if t >= 2:
                        pe.wait_ge(sem("o_out"), 2 * (t - 2) + j + 1)
                    for k in range(KT):
                        ins = mm(PS[2 * (t % 2) + j], MT[k][:, ts(t, P)], RING[j][:, k, :], k == 0, k == KT - 1)
                    ins.then_inc(sem("o_mm"), 1)
                if t:
                    router(t - 1)
            router(NT - 1)
            pe.wait_ge(sem("router_dve"), R_MS)
            for t in range(NT):
                for i in range(t + 1):
                    mm(PS[7][:, ts(t, NE)], sU if i == t else ones, r_t[:, i, :], i == 0, i == t)
            for t in range(NT):
                ins = mm(PS[6][:, 64:96], ones, r_t[:, t, :], t == 0, t == NT - 1)
            ins.then_inc(sem("r_rank"), 1)
            pe.wait_ge(sem("router_dve"), SLOTS_KNOWN)

            def xT(e, s):
                for k in range(KT):
                    ins = E.transpose(PS[k // 4][:, ts(k % 4, P)], e_xs[s][:, ts(k, P)], ident)
                ins.then_inc(sem("xs_used"), 1)

            def first(s, j):
                for u in range(2):
                    for k in range(4):
                        ins = mm(PS[3 + u], e_xT[s][:, 4 * j + k, :], WE[s][j][:, k, ts(u, DE)], j == 0 and k == 0, j == 1 and k == 3)
                return ins

            def hT():
                for k in range(4):
                    ins = E.transpose(PS[2][:, ts(k, P)], e_h[:, ts(k, P)], ident)
                ins.then_inc(sem("hT"), 1)

            def second(s):
                for u in range(2):
                    for k in range(4):
                        ins = mm(PS[5 + u], e_hT[:, k, :], WE[s][2][:, k, ts(u, 512)], k == 0, k == 3)
                    ins.then_inc(sem("y"), 1)

            def step(e, s, lo, i):
                pe.wait_ge(sem(f"win{s}_in"), 32 * i + 32)
                pe.wait_ge(sem("e_xT"), e + 1)
                if lo:
                    pe.wait_ge(sem("e_act"), e)
                first(s, 0)
                if lo:
                    hT()
                first(s, 1).then_inc(sem("win_used"), 1)

            def close(e, s, i):
                pe.wait_ge(sem("e_hT"), e + 1)
                pe.wait_ge(sem(f"wout{s}_in"), 16 * i + 16)

            pe.wait_ge(sem("xs0_in"), 16)
            xT(0, 0)
            step(0, 0, False, 0)
            pe.wait_ge(sem("xs1_in"), 16)
            pe.wait_ge(sem("e_xT"), 1)
            xT(1, 1)
            step(1, 1, True, 0)
            pe.wait_ge(sem("xs0_in"), 32)
            pe.wait_ge(sem("e_xT"), 2)
            xT(2, 0)
            close(0, 0, 0)
            second(0)
            with pe.Fori(1, NE // 2) as i:
                e = 2 * i
                step(e, 0, True, i)
                pe.wait_ge(sem("xs1_in"), 16 * i + 16)
                pe.wait_ge(sem("e_xT"), e + 1)
                xT(e + 1, 1)
                close(e - 1, 1, i - 1)
                pe.wait_ge(sem("y_out"), 2 * (e - 1))
                second(1)
                step(e + 1, 1, True, i)
                with pe.If(i < NE // 2 - 1):
                    pe.wait_ge(sem("xs0_in"), 16 * i + 32)
                    pe.wait_ge(sem("e_xT"), e + 2)
                    xT(e + 2, 0)
                with pe.Else():
                    pe.nop()
                close(e, 0, i)
                pe.wait_ge(sem("y_out"), 2 * e)
                second(0)
            pe.wait_ge(sem("e_act"), NE)
            hT()
            close(NE - 1, 1, NE // 2 - 1)
            pe.wait_ge(sem("y_out"), 2 * (NE - 1))
            second(1)
            n_extra = pe.value_load(i_ex[0:1, NX:NX + 1], min_val=0, max_val=NX)
            with pe.Fori(0, NX) as j:
                with pe.If(n_extra > j):
                    pe.wait_ge(sem("extra_xs"), 16 * j + 16)
                    pe.wait_ge(sem("extra_w"), 48 * j + 48)
                    pe.wait_ge(sem("e_xT"), NE + j)
                    xT(0, 0)
                    pe.wait_ge(sem("e_xT"), NE + j + 1)
                    pe.wait_ge(sem("e_act"), NE + j)
                    first(0, 0)
                    first(0, 1).then_inc(sem("win_used"), 1)
                    pe.wait_ge(sem("e_act"), NE + j + 1)
                    hT()
                    pe.wait_ge(sem("e_hT"), NE + j + 1)
                    pe.wait_ge(sem("y_out"), 2 * (NE + j))
                    second(0)
                with pe.Else():
                    pe.nop()

        @block.scalar
        def _(act):
            chain = [0]

            def link(ins):
                chain[0] += 1
                ins.then_inc(sem("act_step"), 1)
                act.wait_ge(sem("act_step"), chain[0])

            for dst, src in vec_rows:
                act.dma_start(dst, src).then_inc(sem("vecs_in"), 16)
            for dst, src in smalls:
                act.dma_start(dst, src).then_inc(sem("small_in"), 16)
            act.wait_ge(sem("setup_dve"), VECS)
            A.activation(cond, cond, ACT.Silu).then_inc(sem("setup_act"), 1)
            act.wait_ge(sem("setup_pool"), CONSTS)
            def squares(t):
                act.wait_ge(sem(f"rows_in{t % 4}"), 16 * (t // 4) + 16)
                if t:
                    act.wait_ge(sem("x_ss"), t)
                link(A.activation(c_sq, XB[t % 4], ACT.Square, accum_out=ss[:, t:t + 1]))
                A.activation(ss[:, t:t + 1], ss[:, t:t + 1], ACT.Sqrt, scale=1.0 / D, bias=EPS).then_inc(sem("x_ss"), 1)
            for t in range(4):
                squares(t)
            act.wait_ge(sem("setup_dve"), MOD1)
            for t in range(NT):
                act.wait_ge(sem("x_used"), t + 1)
                for k in range(4):
                    ins = A.activation(HT[:, k, ts(t, P)], PS[2 * (t % 2)][:, ts(k, P)], ACT.Identity,
                                       scale=sc1[:, k:k + 1], bias=sh1[:, k:k + 1])
                ins.then_inc(sem("xT_a"), 1)
                if t + 4 < NT:
                    squares(t + 4)
            g = [0]

            def bank():
                act.wait_ge(sem("proj"), g[0] + 1)
                b = PS[g[0] % 2]
                g[0] += 1
                return b

            def done(ins):
                ins.then_inc(sem("proj_out"), 1)

            def c_root(i):
                if i:
                    act.wait_ge(sem("c_normed"), i)
                for half in range(2):
                    act.wait_ge(sem("c_ss"), 2 * i + half + 1)
                    A.activation(c_rs[half], PS[2 + half], ACT.Sqrt, scale=1.0 / N, bias=EPS).then_inc(sem("c_rs"), 1)

            def c_tile(dst, i):
                for half in range(2):
                    b = bank()
                    done(A.activation(dst[:, ts(half, 512)], b, ACT.Copy))
                if i:
                    c_root(i - 1)
                for half in range(2):
                    act.wait_ge(sem("proj_out"), g[0] - 1 + half)
                    A.activation(c_sq[:, ts(half, 512)], dst[:, ts(half, 512)], ACT.Square).then_inc(sem("c_sq"), 1)
            def row(n):
                act.wait_ge(sem("ada_sum"), (5, 6, 11, 12)[n])
                if n:
                    act.wait_ge(sem("row_out"), 16 * n)
                A.activation(rowb[0:1, :], PS[7][0:1, :], ACT.Copy).then_inc(sem("row"), 1)
                act.wait_ge(sem("row"), n + 1)
                act.dma_start(gates_d[n // 2:n // 2 + 1, ts(n % 2, 512)], rowb[0:1, :]).then_inc(sem("row_out"), 16)

            for i in range(4):
                c_tile(QC[:, i], i)
                if i == 1:
                    row(0)
                    row(1)
            c_tile(KC[:, P:], 4)
            row(2)
            row(3)
            for t in range(NT):
                b = bank()
                A.activation(VC[:, t + 1, :, 0:64], b[:, 0:128].rearrange("p (a n) -> p a n", a=2), ACT.Copy)
                done(A.activation(gif[:, t, :], b[:, 128:136], ACT.Copy))
                if t == 0:
                    c_root(4)
            act.wait_ge(sem("row_out"), 64)
            for i in range(4):
                if i >= 2:
                    act.wait_ge(sem("b_conv"), i - 1)
                for half in range(2):
                    b = bank()
                    done(A.activation(RAW[i % 2][:, ds(3 + 512 * half, 512)], b, ACT.Copy))
            for i in range(4):
                act.wait_ge(sem("b_conv"), i + 1)
                A.activation(QK[:, i], QK[:, i], ACT.Silu).then_inc(sem("b_silu"), 1)
            for t in range(NT):
                b = bank()
                A.activation(VO[:, t, 256:512], b[:, 256:512], ACT.Sigmoid)
                done(A.activation(VO[:, t, 0:256], b[:, 0:256], ACT.Copy))

            def attn(c):
                act.wait_ge(sem("c_nm"), c + 1)
                for j in range(8):
                    A.activation(c_sc[:, j, :], c_sc[:, j, :], ACT.Exp, bias=c_nm[:, j:j + 1])
                A.activation(c_es, c_es, ACT.Exp).then_inc(sem("c_p"), 1)
                act.wait_ge(sem("c_pT"), 4 * c + 2)
                A.activation(c_pT[:, 0:4, :], PS[2], ACT.Copy)
                A.activation(c_pT[:, 4:8, :], PS[3], ACT.Copy).then_inc(sem("c_pT_out_a"), 1)
                act.wait_ge(sem("mix_yT"), c + 1)
                A.activation(QC[:, :, ts(c, P)], PS[0].rearrange("p (i n) -> p i n", i=4), ACT.Copy).then_inc(sem("mix_done"), 1)
            with act.Fori(0, NT) as c:
                attn(c)

            act.wait_ge(sem("gates_dve"), G_AX)
            link(A.activation(g_t, g_ax, ACT.Exp, scale=-1.0))
            A.activation(g_t, g_t, ACT.Ln, bias=1.0).then_inc(sem("gates_act"), 1)

            for i in range(8):
                if i >= 2:
                    act.wait_ge(sem("a_shift"), i - 1)
                else:
                    act.wait_ge(sem("b_conv"), 3 + i)
                for half in range(2):
                    b = bank()
                    done(A.activation(RAW[i % 2][:, ds(3 + 512 * half, 512)], b, ACT.Copy))
            act.wait_ge(sem("gates_dve"), G_ARGS)
            for v, sc in ((g_dec, 1.0), (g_w, 1.0), (g_int, 1.0), (g_emt, -1.0)):
                ins = A.activation(v, v, ACT.Exp, scale=sc)
            ins.then_inc(sem("gates_act"), 1)

            def root(v, n, turn):
                act.wait_ge(sem("root_asked"), n)
                A.activation(v, v, ACT.Ln).then_inc(sem("root_ln"), 1)
                act.wait_ge(sem("root_ln"), turn + 1)
                A.activation(v, v, ACT.Exp, scale=-0.5).then_inc(sem("root_done"), 1)

            def mlstm(c, first=False):
                if not first:
                    act.wait_ge(sem("b_inter"), c)
                    act.wait_ge(sem("b_scores"), c)
                A.activation(b_k, QK[:, 2:4, ts(c, P)], ACT.Copy, scale=N ** -0.5).then_inc(sem("b_k"), 1)
                act.wait_ge(sem("b_scores"), c + 1)
                A.activation(b_kt, PS[3][:, 0:256], ACT.Copy).then_inc(sem("b_kt"), 1)
                act.wait_ge(sem("b_arg"), c + 1)
                A.activation(b_e, b_e, ACT.Exp, scale=-1.0).then_inc(sem("b_exp"), 1)
                root(b_ms, c + 1, c)
                act.wait_ge(sem("mix_yT"), NT + c + 1)
                A.activation(QK[:, 0:2, ts(c, P)], PS[3][:, 256:512].rearrange("p (a n) -> p a n", a=2), ACT.Copy)\
                    .then_inc(sem("mix_done"), 1)
            mlstm(0, True)
            with act.Fori(1, NT) as c:
                mlstm(c)

            act.wait_ge(sem("a_shift"), 8)
            A.activation(PA[0:64, 6], PA[0:64, 6], ACT.Tanh).then_inc(sem("setup_act"), 1)
            q = 0
            for p in range(2):
                for half in range(2):
                    hs = slice(512 * half, 512 * half + 512)
                    act.wait_ge(sem("a_lora"), q + 1)
                    A.activation(KK[:, p, hs], PS[2 * (q % 2)], ACT.Sigmoid, bias=w0c[:, p:p + 1]).then_inc(sem("a_sig"), 1)
                    A.activation(BA[:, p, hs], PS[2 * (q % 2) + 1], ACT.Sigmoid, bias=a0c[:, p:p + 1]).then_inc(sem("a_sig"), 1)
                    q += 1
            A.activation(PA[:, 7], PA[:, 7], ACT.Sigmoid).then_inc(sem("setup_act"), 1)
            for q in range(4):
                act.wait_ge(sem("a_kk"), q // 2 + 1)
                if q >= 2:
                    act.wait_ge(sem("a_ss"), q - 1)
                A.activation(RAW[q % 2][:, 0:512], KK[:, q // 2, ts(q % 2, 512)], ACT.Square).then_inc(sem("a_sq"), 1)
                act.wait_ge(sem("root_asked"), ROOT_KK + q + 1)
                A.activation(RAW[1][:, 516:1028], RAW[1][:, 516:1028], ACT.Sqrt).then_inc(sem("root_done"), 1)
            act.wait_ge(sem("setup_act"), A_GSIG)
            act.wait_ge(sem("a_prep"), 1)

            def tmix(c):
                act.wait_ge(sem("a_nb"), c + 1)
                for p in range(2):
                    A.activation(a_e[:, p, :], CS[:, p, ds(c, 1), :].rearrange("p o n -> p (o n)"), ACT.Exp,
                                 scale=-KAPPA, bias=a_nb[:, p:p + 1])
                    A.activation(a_ei[:, p, :], CS[:, p, ds(c, 1), 1:129].rearrange("p o n -> p (o n)"), ACT.Exp,
                                 scale=KAPPA, bias=a_pb[:, p:p + 1])
                A.activation(a_g, a_sgt, ACT.Exp, scale=-KAPPA).then_inc(sem("a_e"), 1)
                A.activation(a_sg, PA[:, 7, ts(c, P)], ACT.Copy).then_inc(sem("a_sg"), 1)
                act.wait_ge(sem("a_tr"), c + 1)
                A.activation(a_AZ[:, :, 0:N], PS[0][:, 0:256].rearrange("p (h n) -> p h n", h=H), ACT.Copy)
                A.activation(a_tok[:, 0, :], PS[0][:, 256:512], ACT.Copy)
                A.activation(a_tok[:, 1:3, :], PS[1].rearrange("p (a n) -> p a n", a=2), ACT.Copy).then_inc(sem("a_tok"), 1)
                for q in range(1, 7):
                    act.wait_ge(sem("a_A1"), 7 * c + q + 1)
                    A.activation(a_A1, PS[2].rearrange("p (h n) -> p h n", h=H), ACT.Copy).then_inc(sem("a_A1s"), 1)
                act.wait_ge(sem("a_Z"), c + 1)
                A.activation(a_AZ[:, :, N:P], PS[5][:, 0:256].rearrange("p (h n) -> p h n", h=H), ACT.Copy).then_inc(sem("a_Zs"), 1)
                act.wait_ge(sem("a_WU"), c + 1)
                A.activation(a_WU, PS[2].rearrange("p (h n) -> p h n", h=H), ACT.Copy).then_inc(sem("a_WUs"), 1)
                root(a_t4, ROOT_A + 1 + c, NT + c)
                act.wait_ge(sem("mix_yT"), 2 * NT + c + 1)
                A.activation(PA[:, 0:2, ts(c, P)], PS[0][:, 0:256].rearrange("p (a n) -> p a n", a=2), ACT.Copy)\
                    .then_inc(sem("mix_done"), 1)
            with act.Fori(0, NT) as c:
                tmix(c)

            for n in range(48):
                act.wait_ge(sem("m_pair"), n + 1)
                A.activation(m_sg[n % 4], PS[2 * (n % 4)], ACT.Sigmoid).then_inc(sem("m_sg"), 1)

            for t in range(NT):
                act.wait_ge(sem("o_x1"), t + 1)
                act.dma_start(x1_t[t], o_x[t % 2]).then_inc(sem(f"rows_st{t % 2}"), 16)
                if t:
                    act.wait_ge(sem("o_ss"), t)
                link(A.activation(o_sq, o_x[t % 2], ACT.Square, accum_out=ss[:, t:t + 1]))
                A.activation(ss[:, t:t + 1], ss[:, t:t + 1], ACT.Sqrt, scale=1.0 / D, bias=EPS).then_inc(sem("o_ss"), 1)
                act.wait_ge(sem("o_norm"), t + 1)
                act.dma_start(xn_t[t], o_n[t % 2]).then_inc(sem(f"xn_st{t % 2}"), 16)
                act.wait_ge(sem("o_T"), t + 1)
                for k in range(4):
                    ins = A.activation(o_hT[:, k, :], PS[4][:, ts(k, P)], ACT.Identity, scale=sc2[:, k:k + 1], bias=sh2[:, k:k + 1])
                ins.then_inc(sem("o_hT_a"), 1)
            for n, v in enumerate((r_g4[1].rearrange("p a b -> p (a b)"), r_8[5])):
                act.wait_ge(sem("r_arg"), n + 1)
                A.activation(v, v, ACT.Exp).then_inc(sem("r_exp"), 1)
            act.wait_ge(sem("router_dve"), SLOTS_KNOWN)

            def xT_out(e, s):
                act.wait_ge(sem("xs_used"), e + 1)
                for k in range(KT):
                    ins = A.activation(e_xT[s][:, k, :], PS[k // 4][:, ts(k % 4, P)], ACT.Identity,
                                       scale=sc2[:, k:k + 1], bias=sh2[:, k:k + 1])
                ins.then_inc(sem("e_xT"), 1)

            def hT_out(e):
                act.wait_ge(sem("hT"), e + 1)
                A.activation(e_hT, PS[2].rearrange("p (k n) -> p k n", k=4), ACT.Copy).then_inc(sem("e_hT"), 1)

            def silu(e, first=False):
                act.wait_ge(sem("win_used"), e + 1)
                if not first:
                    act.wait_ge(sem("e_act"), e)
                A.activation(e_g, PS[3], ACT.Silu).then_inc(sem("e_silu"), 1)

            def store(e, s):
                act.wait_ge(sem("y_out"), 2 * e + 2)
                act.dma_start(ys_b[ds(e, 1)].rearrange("o p n -> (o p) n"), e_y[s]).then_inc(sem(f"y_st{s}"), 16)

            xT_out(0, 0)
            silu(0, True)
            xT_out(1, 1)
            hT_out(0)
            silu(1)
            xT_out(2, 0)
            store(0, 0)
            with act.Fori(1, NE // 2) as i:
                e = 2 * i
                hT_out(e - 1)
                silu(e)
                xT_out(e + 1, 1)
                store(e - 1, 1)
                hT_out(e)
                silu(e + 1)
                with act.If(i < NE // 2 - 1):
                    xT_out(e + 2, 0)
                with act.Else():
                    act.nop()
                store(e, 0)
            hT_out(NE - 1)
            store(NE - 1, 1)
            for s in range(2):
                act.wait_ge(sem(f"y_st{s}"), 16 * NE // 2)
            n_extra = act.value_load(i_ex[0:1, NX:NX + 1], min_val=0, max_val=NX)
            act.wait_ge(sem("slots_zero"), 16 * NX)
            act.sem_inc(sem("extra_go"), 1)
            with act.Fori(0, NX) as j:
                with act.If(n_extra > j):
                    xT_out(NE + j, 0)
                    silu(NE + j)
                    hT_out(NE + j)
                    act.wait_ge(sem("y_out"), 2 * (NE + j) + 2)
                    act.dma_start(ys_b[ds(NE + j, 1)].rearrange("o p n -> (o p) n"), e_y[0]).then_inc(sem("y_stx"), 16)
                    act.wait_ge(sem("y_stx"), 16 * j + 16)
                    act.sem_inc(sem("extra_go"), 1)
                with act.Else():
                    act.nop()
            act.sem_inc(sem("extra_end"), 1)
            for t in range(NT):
                act.wait_ge(sem("f_sum"), t + 1)
                act.dma_start(out_t[t], f_o[t % 2]).then_inc(sem(f"rows_st{t % 2}"), 16)
            for s in range(2):
                act.wait_ge(sem(f"rows_st{s}"), 64 + 16 * NT // 2)

        @block.vector
        def _(dve):
            chain = [0]
            dsem = sem("dve_step")

            def link(ins):
                chain[0] += 1
                ins.then_inc(dsem, 1)
                dve.wait_ge(dsem, chain[0])

            def body_link(per_turn, c, turns=NT, begin=0):
                n = [0]

                def f(ins):
                    n[0] += 1
                    ins.then_inc(dsem, 1)
                    dve.wait_ge(dsem, c * per_turn + begin + n[0])
                f.n = n
                return f

            def root_by_act(ins, n):
                ins.then_inc(sem("root_asked"), 1)
                dve.wait_ge(sem("root_done"), n)

            dve.wait_ge(sem("small_in"), 16 * len(smalls))
            dve.wait_ge(sem("vecs_T"), 1)
            V.tensor_copy(vecs[:, 0:NV], PS[7][:, 0:NV]).then_inc(sem("setup_dve"), 1)
            dve.wait_ge(sem("setup_dve"), VECS)
            link(TS(qkg[:, 0:1], qkg[:, 0:1], N ** -0.5, None, ALU.mult))
            V.tensor_copy(sinkb.rearrange("p (i a) -> p a i", a=2), sinkr.rearrange("p (a i) -> p a i", a=2))
            link(TS(kac1, kac, -1.0, 1.0, ALU.mult, ALU.add))

            def norm(t):
                dve.wait_ge(sem("x_ss"), t + 1)
                r = rstd[:, t:t + 1]
                link(V.reciprocal(r, ss[:, t:t + 1]))
                TS(XB[t % 4], XB[t % 4], r, None, ALU.mult).then_inc(sem("x_norm"), 1)

            def ada(i):
                dve.wait_ge(sem(f"wide_in{i % 2}"), 16 * (i // 2) + 16)
                if i:
                    dve.wait_ge(sem("ada_sum"), i)
                w = ADA[i % 2]
                link(TS(acc, w[:, 0, :], cond[:, 0:1], None, ALU.mult))
                for k in range(1, KT):
                    ins = STT(acc, w[:, k, :], cond[:, k:k + 1], acc, ALU.mult, ALU.add)
                    if k < KT - 1:
                        link(ins)
                ins.then_inc(sem("ada_acc"), 1)

            for t in range(4):
                norm(t)
            dve.wait_ge(sem("setup_act"), COND)
            for i in range(4):
                ada(i)

            def modulation(i0, sh, sc, gamma):
                link(TT(sh, PS[6][:, 4 * i0:4 * i0 + 8], badac[:, 4 * i0:4 * i0 + 8], ALU.add))
                link(TT(sc, PS[6][:, 4 * i0 + 8:4 * i0 + 16], badac[:, 4 * i0 + 8:4 * i0 + 16], ALU.add))
                return STT(sc, sc, 1.0, gamma, ALU.add, ALU.mult)

            dve.wait_ge(sem("ada_sum"), 4)
            modulation(0, sh1, sc1, n1g).then_inc(sem("setup_dve"), 1)
            dve.wait_ge(sem("setup_dve"), MOD1)
            for t in range(NT):
                dve.wait_ge(sem("x_used"), t + 1)
                for k in range(4, 8):
                    ins = TS(HT[:, k, ts(t, P)], PS[2 * (t % 2) + 1][:, ts(k - 4, P)], sc1[:, k:k + 1], sh1[:, k:k + 1],
                             ALU.mult, ALU.add)
                ins.then_inc(sem("xT_v"), 1)
                if t + 4 < NT:
                    norm(t + 4)

            def c_norm(i):
                dst = QC[:, i] if i < 4 else KC[:, P:]
                g = qkg[:, 0:1] if i < 4 else qkg[:, 1:2]
                for half in range(2):
                    dve.wait_ge(sem("c_rs"), 2 * i + half + 1)
                    link(V.reciprocal(c_rs[half], c_rs[half]))
                    ins = STT(dst[:, ts(half, 512)], dst[:, ts(half, 512)], g, c_rs[half], ALU.mult, ALU.mult)
                ins.then_inc(sem("c_normed"), 1)

            for i in range(4):
                c_norm(i)
                ada(4 + 2 * i)
                ada(5 + 2 * i)
            c_norm(4)
            dve.wait_ge(sem("ada_sum"), 12)
            link(modulation(6, sh2, sc2, n2g))

            for i in range(4):
                dve.wait_ge(sem("proj_out"), 18 + 2 * i + 2)
                link(TS(QK[:, i], RAW[i % 2][:, 3:3 + T], cw[:, 3, i:i + 1], cb[:, i:i + 1], ALU.mult, ALU.add))
                for j in (2, 1, 0):
                    ins = STT(QK[:, i], RAW[i % 2][:, j:j + T], cw[:, j, i:i + 1], QK[:, i], ALU.mult, ALU.add)
                    if j:
                        link(ins)
                ins.then_inc(sem("b_conv"), 1)

            chain0 = chain[0]

            def attn(c, row):
                lk = body_link(5, c, begin=chain0)
                dve.wait_ge(sem("c_scores"), c + 1)
                for i in range(4):
                    for a in range(2):
                        slope = 2.0 ** -(4 * a + i + 1)
                        ins = STT(c_sc[:, 2 * i + a, :], dist[:, row, :], -slope,
                                  PS[2 + 2 * a + i // 2][:, ts(i % 2, 2 * P)], ALU.mult, ALU.add)
                lk(ins)
                lk(V.tensor_reduce(out=c_mx, in_=c_sc, axis=AX, op=ALU.max))
                lk(TT(c_mx, c_mx, sinkb, ALU.max))
                TS(c_nm, c_mx, -1.0, None, ALU.mult)
                TT(c_es, sinkb, c_mx, ALU.subtract).then_inc(sem("c_nm"), 1)
                dve.wait_ge(sem("c_pT"), 4 * c + 4)
                V.tensor_copy(c_pT[:, 8:12, :], PS[4])
                V.tensor_copy(c_pT[:, 12:16, :], PS[5]).then_inc(sem("c_pT_out_v"), 1)
                dve.wait_ge(sem("c_pv"), c + 1)
                pv = [PS[6 + k][:, 0:260].rearrange("p (j n) -> p j n", j=4) for k in range(2)]
                for k in range(2):
                    ins = TT(c_dn[:, 4 * k:4 * k + 4], pv[k][:, :, 64], c_es[:, 4 * k:4 * k + 4], ALU.add)
                lk(ins)
                lk(V.reciprocal(c_dn, c_dn))
                for k in range(2):
                    ins = TT(c_y[:, 4 * k:4 * k + 4, :], pv[k][:, :, 0:64], bc(c_dn[:, 4 * k:4 * k + 4], 64), ALU.mult)
                ins.then_inc(sem("mix_y"), 1)
            attn(0, 0)
            with dve.Fori(1, NT) as c:
                attn(c, 1)
            chain[0] += 5 * NT
            dve.wait_ge(sem("mix_done"), NT)

            def g48(v):
                return v.rearrange("p (c h) -> p c h", h=H)
            V.memset(b_v[:, :, 64:65], 1.0)
            V.memset(b_st, 0.0)
            V.memset(g_M, 0.0).then_inc(sem("gates_dve"), 1)
            link(TT(gif, gif, bif.unsqueeze(1).to_broadcast([P, NT, 8]), ALU.add))
            STT(g48(g_ax), gif[:, :, 4:8], -1.0, gif[:, :, 4:8], ALU.mult, ALU.max).then_inc(sem("gates_dve"), 1)
            dve.wait_ge(sem("gates_act"), G_LN)
            STT(g48(g_lf), gif[:, :, 4:8], 0.0, g48(g_t), ALU.min, ALU.subtract).then_inc(sem("gates_dve"), 1)

            for i in range(8):
                dve.wait_ge(sem("proj_out"), 34 + 2 * i + 2)
                link(TT(PA[:, i], RAW[i % 2][:, 2:2 + T], RAW[i % 2][:, 3:3 + T], ALU.subtract))
                STT(PA[:, i], PA[:, i], mu[:, i:i + 1], RAW[i % 2][:, 3:3 + T], ALU.mult, ALU.add).then_inc(sem("a_shift"), 1)

            dve.wait_ge(sem("gates_pe"), G_F)
            V.tensor_copy(g_F, PS[6][:, 0:32])
            V.tensor_copy(g_FL, PS[6][:, 32:64])
            TT(g48(g_Z), gif[:, :, 0:4], g48(PS[6][:, 0:32]), ALU.subtract).then_inc(sem("gates_dve"), 1)
            dve.wait_ge(sem("gates_pe"), G_ZT)
            link(V.tensor_copy(g_zT[0:32, :], PS[7][0:32, 0:P]))
            link(V.tensor_tensor_scan(out=g_cm[0:32, :], data0=g_zT[0:32, :], data1=g_zT[0:32, :], initial=-3e38,
                                      op0=ALU.max, op1=ALU.max))
            TS(g_D[0:32, :], ident[0:32, 0:32], g_cm[0:32, 127:128], None, ALU.mult).then_inc(sem("gates_dve"), 1)
            dve.wait_ge(sem("gates_pe"), G_ZM)
            link(V.tensor_copy(g_ZM, PS[6][:, 64:96]))
            for h in range(H):
                ins = V.tensor_tensor_scan(out=g_M[:, h, 1:9], data0=g48(g_ZM)[:, :, h], data1=g48(g_FL)[:, :, h],
                                           initial=0.0, op0=ALU.max, op1=ALU.add)
            link(ins)
            M0 = g_M[:, :, 0:8].rearrange("p h c -> p c h")
            M1 = g_M[:, :, 1:9].rearrange("p h c -> p c h")
            link(TT(g48(g_ml), M1, g48(g_FL), ALU.subtract))
            TT(g48(g_dec), M0, g48(g_ml), ALU.subtract)
            TT(g_w, g_Z, g_ml, ALU.subtract)
            link(TT(g48(g_t[0:32, :]), g48(ident[0:32, 0:32]), M0[0:32], ALU.mult))
            link(V.tensor_reduce(out=g_mc[0:32, :], in_=g_t[0:32, :], axis=AX, op=ALU.add))
            TS(g_mr[0:32, :], g_cm[0:32, :], g_mc[0:32, 0:1], None, ALU.max).then_inc(sem("gates_dve"), 1)
            dve.wait_ge(sem("gates_pe"), G_MT)
            link(V.tensor_copy(g_mt, PS[7][:, 128:160]))
            TT(g48(g_int), M0, g48(g_mt), ALU.subtract)
            TT(g_emt, g_F, g_mt, ALU.add).then_inc(sem("gates_dve"), 1)
            dve.wait_ge(sem("gates_act"), G_DONE)
            dve.wait_ge(sem("gates_dve"), G_MR)

            chain0 = chain[0]

            def mlstm(c):
                lk = body_link(10, c, begin=chain0)
                dve.wait_ge(sem("mix_staged"), NT + c + 1)
                TT(b_wv, b_v, bc(g_w[:, ts(c, 4)], 65), ALU.mult).then_inc(sem("b_wv"), 1)
                TT(b_bd[0:32], g_mr[0:32, :].unsqueeze(1).to_broadcast([32, H, P]), bc(ident[0:32, ts(c, 4)], P), ALU.mult)\
                    .then_inc(sem("b_bd"), 1)
                dve.wait_ge(sem("b_mu"), c + 1)
                for h in range(H):
                    ins = TS(b_e[:, h, :], PS[0][:, ts(h, P)], g_Z[:, ds(4 * c + h, 1)], 0.0, ALU.subtract, ALU.max)
                ins.then_inc(sem("b_arg"), 1)
                dve.wait_ge(sem("b_scores"), c + 1)
                dve.wait_ge(sem("b_masked"), c + 1)
                for a in range(2):
                    ins = TT(b_sw.rearrange("p (q a) n -> p q a n", a=2)[:, :, a, :], PS[1 + a][:, 0:256].rearrange("p (q n) -> p q n", q=2),
                             b_e.rearrange("p (q a) n -> p q a n", a=2)[:, :, a, :], ALU.mult)
                ins.then_inc(sem("b_sw"), 1)
                dve.wait_ge(sem("b_inter"), c + 1)
                for a in range(2):
                    ins = TT(b_h.rearrange("p (q a) n -> p q a n", a=2)[:, :, a, :], PS[5 + a][:, 0:130].rearrange("p (q n) -> p q n", q=2),
                             bc(g_int[:, ts(c, 4)].rearrange("p (q a) -> p q a", a=2)[:, :, a], 65), ALU.mult)
                lk(ins)
                for h in range(H):
                    a, p = h % 2, h // 2
                    rows = slice(64 * a, 64 * a + 64)
                    ins = STT(b_st[rows, p, :], b_st[rows, p, :], g_dec[rows, ds(4 * c + h, 1)], PS[7][rows, ds(65 * p, 65)],
                              ALU.mult, ALU.add)
                ins.then_inc(sem("b_state"), 1)
                dve.wait_ge(sem("b_num"), c + 1)
                lk(TT(b_h, b_h, PS[4][:, 0:260].rearrange("p (h n) -> p h n", h=H), ALU.add))
                lk(STT(b_d, b_h[:, :, 64], -1.0, b_h[:, :, 64], ALU.mult, ALU.max))
                lk(TT(b_d, b_d, g_emt[:, ts(c, 4)], ALU.max))
                lk(V.reciprocal(b_rd, b_d))
                lk(TT(b_hh, b_h[:, :, 0:64], bc(b_rd, 64), ALU.mult))
                lk(TT(b_sq, b_hh, b_hh, ALU.mult))
                lk(V.tensor_reduce(out=b_ms, in_=b_sq, axis=AX, op=ALU.add))
                root_by_act(TS(b_ms, b_ms, 1.0 / N, EPS, ALU.mult, ALU.add), c + 1)
                lk(TT(b_hh, b_hh, bc(b_ms, 64), ALU.mult))
                lk(TT(b_hh, b_hh, hng.rearrange("p (h n) -> p h n", h=H), ALU.mult))
                TT(b_hh, b_hh, VO[:, ds(c, 1), 256:512].rearrange("p o (h n) -> p (o h) n", h=H), ALU.mult).then_inc(sem("mix_y"), 1)
            with dve.Fori(0, NT) as c:
                mlstm(c)
            chain[0] += 10 * NT
            dve.wait_ge(sem("mix_done"), NT + NT)

            dve.wait_ge(sem("a_sig"), 8)
            link(V.memset(CS, 0.0))
            for p in range(2):
                for c in range(NT):
                    ins = V.tensor_tensor_scan(out=CS[:, p, c, 1:129], data0=ones, data1=KK[:, p, ts(c, P)], initial=0.0,
                                               op0=ALU.mult, op1=ALU.add)
                link(ins)
                TS(KK[:, p], PA[:, 2 + p], kkc[:, p:p + 1], None, ALU.mult).then_inc(sem("a_kk"), 1)
                dve.wait_ge(sem("a_kk"), p + 1)
            tmp = RAW[0][:, 516:1028], RAW[1][:, 516:1028]
            for q in range(4):
                p, hs = q // 2, slice(512 * (q % 2), 512 * (q % 2) + 512)
                link(TS(tmp[0], BA[:, p, hs], kac[:, p:p + 1], kac1[:, p:p + 1], ALU.mult, ALU.add))
                TT(PA[:, 2 + p, hs], PA[:, 2 + p, hs], tmp[0], ALU.mult)
                dve.wait_ge(sem("a_ss"), q + 1)
                root_by_act(TS(tmp[1], PS[4 + q % 2], 1e-24, None, ALU.max), ROOT_KK + q + 1)
                link(V.reciprocal(tmp[1], tmp[1]))
                link(TT(KK[:, p, hs], KK[:, p, hs], tmp[1], ALU.mult))
                TT(BA[:, p, hs], BA[:, p, hs], KK[:, p, hs], ALU.mult).then_inc(sem("a_kkn"), 1)
            dve.wait_ge(sem("a_kkn"), 4)
            V.memset(a_st, 0.0).then_inc(sem("a_prep"), 1)
            dve.wait_ge(sem("a_prep"), 1)

            chain0 = chain[0]

            def tmix(c):
                lk = body_link(14, c, begin=chain0)
                mid = CS[:, :, ds(c, 1), 64].rearrange("p a o -> p (a o)")
                TS(a_pb, mid, -KAPPA, None, ALU.mult)
                TS(a_nb, mid, KAPPA, None, ALU.mult)
                lk(TT(a_sgt, CS[:, :, ds(c, 1), 128].rearrange("p a o -> p (a o)"), mid, ALU.subtract))
                TT(a_sgt, a_sgt, CS[:, :, ds(c + 1, 1), 64].rearrange("p a o -> p (a o)"), ALU.add).then_inc(sem("a_nb"), 1)
                cs = ts(c, P)
                for p in range(2):
                    ins = STT(a_rk[:, p, :], PA[:, p, cs], rkc[:, p:p + 1], PA[:, 2 + p, cs], ALU.mult, ALU.mult)
                ins.then_inc(sem("a_rk"), 1)
                dve.wait_ge(sem("a_e"), c + 1)
                STT(a_ar[:, :, 0, :], KK[:, :, cs], -1.0, a_e[:, :, 0:128], ALU.mult, ALU.mult)
                TT(a_ar[:, :, 1, :], PA[:, 0:2, cs], a_e[:, :, 1:129], ALU.mult)
                TT(a_bk[:, :, 0, :], BA[:, :, cs], a_ei, ALU.mult)
                TT(a_bk[:, :, 1, :], PA[:, 2:4, cs], a_ei, ALU.mult).then_inc(sem("a_abkr"), 1)
                for h in range(H):
                    dve.wait_ge(sem("a_scores"), 4 * c + h + 1)
                    TT(a_sm[:, h], PS[2 + h].rearrange("p (a n) -> p a n", a=4), msk, ALU.mult).then_inc(sem("a_sm"), 1)
                idb = ident.unsqueeze(1).to_broadcast([P, H, P])
                for q in range(7):
                    if q == 0:
                        dve.wait_ge(sem("a_lo"), 7 * c + 1)
                        TT(a_Tt, a_lo[0], idb, ALU.add).then_inc(sem("a_Tt"), 1)
                        dve.wait_ge(sem("a_A1"), 7 * c + 1)
                        TT(a_T, PS[2].rearrange("p (h n) -> p h n", h=H), idb, ALU.add).then_inc(sem("a_T"), 1)
                        continue
                    if q < 6:
                        dve.wait_ge(sem("a_P2"), 5 * c + q)
                        TT(a_T, a_T, PS[3].rearrange("p (h n) -> p h n", h=H), ALU.add).then_inc(sem("a_T"), 1)
                    dve.wait_ge(sem("a_Pt"), 6 * c + q)
                    TT(a_Tt, a_Tt, PS[4].rearrange("p (h n) -> p h n", h=H), ALU.add).then_inc(sem("a_Tt"), 1)
                dve.wait_ge(sem("a_GS"), c + 1)
                TT(a_wr, PS[3][:, 0:256].rearrange("p (a n) -> p a n", a=2), a_ar[:, :, 1, :], ALU.add)
                TT(a_qs, PS[4][:, 0:128].rearrange("p (a n) -> p a n", a=2), id64.unsqueeze(1).to_broadcast([P, 2, N]), ALU.add)
                for p in range(2):
                    ins = TS(a_gs[:, p, :], PS[5][:, ds(256 + 64 * p, N)], a_g[:, p:p + 1], None, ALU.mult)
                ins.then_inc(sem("a_Qs"), 1)
                dve.wait_ge(sem("a_Qs"), c + 1)
                dve.wait_ge(sem("a_Y"), c + 1)
                for h in range(H):
                    a, p = h % 2, h // 2
                    rows = slice(64 * a, 64 * a + 64)
                    ins = STT(a_st[rows, p, :], PS[3 + a][rows, ts(2 + p, N)], a_g[rows, p:p + 1], a_gs[rows, p, :], ALU.mult, ALU.add)
                ins.then_inc(sem("a_state"), 1)
                for a in range(2):
                    ins = V.tensor_copy(a_y.rearrange("p (q a) n -> p q a n", a=2)[:, :, a, :],
                                        PS[3 + a][:, 0:128].rearrange("p (q n) -> p q n", q=2))
                lk(ins)
                lk(TT(a_y, a_y, PS[6][:, 0:256].rearrange("p (h n) -> p h n", h=H), ALU.add))
                lk(V.tensor_reduce(out=a_m4, in_=a_y, axis=AX, op=ALU.add))
                lk(TS(a_m4, a_m4, -1.0 / N, None, ALU.mult))
                lk(TT(a_y, a_y, bc(a_m4, N), ALU.add))
                lk(TT(a_y2, a_y, a_y, ALU.mult))
                lk(V.tensor_reduce(out=a_t4, in_=a_y2, axis=AX, op=ALU.add))
                root_by_act(TS(a_t4, a_t4, 1.0 / N, A_EPS, ALU.mult, ALU.add), ROOT_A + 1 + c)
                lk(TT(a_y, a_y, bc(a_t4, N), ALU.mult))
                lk(TT(a_y, a_y, lnxg.rearrange("p (h n) -> p h n", h=H), ALU.mult))
                lk(TT(a_y, a_y, lnxb.rearrange("p (h n) -> p h n", h=H), ALU.add))
                dve.wait_ge(sem("a_gb"), c + 1)
                dve.wait_ge(sem("a_tok"), c + 1)
                lk(V.tensor_copy(a_bon, PS[7][:, 256:260]))
                lk(TT(a_y2, a_tok[:, 2, :].rearrange("p (h n) -> p h n", h=H), bc(a_bon, N), ALU.mult))
                lk(TT(a_y, a_y, a_y2, ALU.add))
                TT(a_y, a_y, PS[7][:, 0:256].rearrange("p (h n) -> p h n", h=H), ALU.mult).then_inc(sem("mix_y"), 1)
                assert lk.n[0] == 14, lk.n
            with dve.Fori(0, NT) as c:
                tmix(c)
            chain[0] += 14 * NT
            dve.wait_ge(sem("mix_done"), 2 * NT + NT)

            n = 0
            for c in range(8):
                for half in range(2):
                    hh = 2 * c + half
                    for b in range(3):
                        dve.wait_ge(sem("m_sg"), n + 1)
                        if b and hh:
                            dve.wait_ge(sem("m_added"), 2 * (hh - 1) + b)
                        dst = MT[c][:, ts(half, 512)] if b == 0 else m_t[b - 1]
                        TT(dst, m_sg[n % 4], PS[2 * (n % 4) + 1], ALU.mult).then_inc(sem("m_prod"), 1)
                        n += 1

            dve.wait_ge(sem("gt1_in"), 32)
            link(TT(gt1, gt1, gtb, ALU.add))

            def router(t):
                dve.wait_ge(sem("o_T"), t + 1)
                for k in range(4, 8):
                    ins = TS(o_hT[:, k, :], PS[5][:, ts(k - 4, P)], sc2[:, k:k + 1], sh2[:, k:k + 1], ALU.mult, ALU.add)
                ins.then_inc(sem("o_hT_v"), 1)
                dve.wait_ge(sem("r_mm"), t + 1)
                TT(r_lg[:, t, :], PS[6][:, 0:36], br, ALU.add).then_inc(sem("r_lg"), 1)

            for t in range(NT):
                if t >= 2:
                    dve.wait_ge(sem(f"xn_st{t % 2}"), 16 * (t // 2))
                for j in range(2):
                    dve.wait_ge(sem("o_mm"), 2 * t + j + 1)
                    TT(o_n[t % 2][:, ts(j, 512)], PS[2 * (t % 2) + j], gt1[:, ts(j, 512)], ALU.mult).then_inc(sem("o_out"), 1)
                dve.wait_ge(sem("o_out"), 2 * t + 2)
                dve.wait_ge(sem(f"rows_in{t % 2}"), 32 + 16 * (t // 2) + 16)
                TT(o_x[t % 2], o_x[t % 2], o_n[t % 2], ALU.add).then_inc(sem("o_x1"), 1)
                dve.wait_ge(sem("o_ss"), t + 1)
                r = rstd[:, t:t + 1]
                link(V.reciprocal(r, ss[:, t:t + 1]))
                TS(o_n[t % 2], o_x[t % 2], r, None, ALU.mult).then_inc(sem("o_norm"), 1)
                if t == NT - 1:
                    router(t)
                if t < NT - 1:
                    router(t)

            dve.wait_ge(sem("r_lg"), NT)
            V.memset(r_cnt, 0.0)
            dve.wait_ge(sem("setup_pool"), R_IOTA)
            gmx, gsum, gi, l1, l2, te, w1, w2, s1, s2 = r_8
            gl = r_lg[:, :, 0:4]
            link(V.tensor_reduce(out=gmx, in_=gl, axis=AX, op=ALU.max))
            TT(r_g4[1], gl, bc(gmx, 4), ALU.subtract).then_inc(sem("r_arg"), 1)
            i4 = r_i4.unsqueeze(1).to_broadcast([P, NT, NG])
            i32_ = r_io.unsqueeze(1).to_broadcast([P, NT, NE])
            link(TT(r_g4[0], gl, bc(gmx, 4), ALU.is_lt))
            link(STT(r_g4[0], r_g4[0], 99.0, i4, ALU.mult, ALU.add))
            link(V.tensor_reduce(out=gi, in_=r_g4[0], axis=AX, op=ALU.min))
            link(TT(r_g4[2], i4, bc(gi, 4), ALU.not_equal))
            em4 = r_em.rearrange("p t (g e) -> p t g e", g=NG)
            for g in range(NG):
                ins = STT(em4[:, :, g, :], bc(r_g4[2][:, :, g], 8), -BIG, r_lg[:, :, 4 + 8 * g:12 + 8 * g], ALU.mult, ALU.add)
            link(ins)

            def best(l, m):
                link(V.tensor_reduce(out=l, in_=r_em, axis=AX, op=ALU.max))
                link(TT(r_t, r_em, bc(l, NE), ALU.is_lt))
                link(STT(r_t, r_t, 99.0, i32_, ALU.mult, ALU.add))
                link(V.tensor_reduce(out=te, in_=r_t, axis=AX, op=ALU.min))
                link(TT(m, i32_, bc(te, NE), ALU.is_equal))
            best(l1, r_m1)
            link(STT(r_em, r_m1, -2 * BIG, r_em, ALU.mult, ALU.add))
            best(l2, r_m2)
            TT(r_t, r_m1, r_m2, ALU.add).then_inc(sem("router_dve"), 1)
            dve.wait_ge(sem("router_dve"), R_MS)
            TT(te, l2, l1, ALU.subtract).then_inc(sem("r_arg"), 1)
            dve.wait_ge(sem("r_exp"), 2)
            link(V.tensor_reduce(out=gsum, in_=r_g4[1], axis=AX, op=ALU.add))
            link(TS(w2, te, 1.0, None, ALU.add))
            link(TT(gsum, gsum, w2, ALU.mult))
            link(V.reciprocal(w1, gsum))
            link(TT(w2, w1, te, ALU.mult))
            dve.wait_ge(sem("r_rank"), 1)
            link(V.tensor_copy(r_cnt, PS[6][:, 64:96]))
            link(TS(r_nx, r_cnt, float(P), None, ALU.is_gt))
            for m in range(2, NT):
                link(STT(r_nx, r_cnt, float(P * m), r_nx, ALU.is_gt, ALU.add))
            link(V.tensor_tensor_scan(out=r_cum, data0=ones[:, 0:NE], data1=r_nx, initial=0.0, op0=ALU.mult, op1=ALU.add))
            link(TT(r_ov, r_cum, r_nx, ALU.subtract))
            link(TT(r_ov, r_ov, r_io, ALU.subtract))
            link(TS(r_ov, r_ov, float(NE - 1), float(P), ALU.add, ALU.mult))
            rank = PS[7][:, 0:256].rearrange("p (t e) -> p t e", t=NT)
            link(TS(r_em, rank, float(P), None, ALU.is_ge))
            link(TT(r_em, r_em, r_ov.unsqueeze(1).to_broadcast([P, NT, NE]), ALU.mult))
            link(TT(r_em, r_em, rank, ALU.add))
            link(STT(r_em, i32_, float(P), r_em, ALU.mult, ALU.add))
            for m, sl, isl, itb in ((r_m1, s1, i_s1, i_t1), (r_m2, s2, i_s2, i_t2)):
                link(TT(r_t, m, r_em, ALU.mult))
                link(V.tensor_reduce(out=sl, in_=r_t, axis=AX, op=ALU.add))
                link(V.tensor_copy(isl, sl))
                dve.wait_ge(sem("table"), 16)
                TS(i_hi, isl, 7, None, ALU.logical_shift_right)
                link(TS(i_lo, isl, P - 1, None, ALU.bitwise_and))
                link(STT(itb, i_lo, float(NBP), i_hi, ALU.mult, ALU.add))
            for j in range(NX):
                ins = TS(r_ex[:, j, :], r_cum, float(j), None, ALU.is_le)
            link(ins)
            link(V.tensor_reduce(out=r_exs[:, 0:NX], in_=r_ex, axis=AX, op=ALU.add))
            link(TS(r_exs[:, 0:NX], r_exs[:, 0:NX], float(NE - 1), None, ALU.min))
            link(V.tensor_copy(r_exs[:, NX:NX + 1], r_cum[:, NE - 1:NE]))
            link(V.tensor_copy(i_ex, r_exs))
            V.tensor_copy(r_exs[:, 0:1], r_cum[:, 0:1]).then_inc(sem("router_dve"), 1)

            def activate(e):
                dve.wait_ge(sem("e_silu"), e + 1)
                TT(e_h, e_g, PS[4], ALU.mult).then_inc(sem("e_act"), 1)

            def y_out(e, s, wait):
                for u in range(2):
                    dve.wait_ge(sem("y"), 2 * e + u + 1)
                    if u == 0 and wait is not None:
                        dve.wait_ge(sem(f"y_st{s}"), wait)
                    V.tensor_copy(e_y[s][:, ts(u, 512)], PS[5 + u]).then_inc(sem("y_out"), 1)

            activate(0)
            activate(1)
            y_out(0, 0, None)
            activate(2)
            y_out(1, 1, None)
            activate(3)
            y_out(2, 0, 16)
            with dve.Fori(2, NE // 2) as i:
                activate(2 * i)
                y_out(2 * i - 1, 1, 16 * (i - 1))
                activate(2 * i + 1)
                y_out(2 * i, 0, 16 * i)
            y_out(NE - 1, 1, 16 * (NE // 2 - 1))
            n_extra = dve.value_load(i_ex[0:1, NX:NX + 1], min_val=0, max_val=NX)
            with dve.Fori(0, NX) as j:
                with dve.If(n_extra > j):
                    dve.wait_ge(sem("extra_go"), j + 1)
                    activate(NE + j)
                    y_out(NE + j, 0, None)
                with dve.Else():
                    dve.nop()

            dve.wait_ge(sem("gt2_in"), 32)
            link(TT(gt2, gt2, gt2b, ALU.add))
            for t in range(NT):
                s = t % 2
                dve.wait_ge(sem(f"fy_in{s}"), 32 * (t // 2) + 32)
                dve.wait_ge(sem(f"rows_in{2 + s}"), 32 + 16 * (t // 2) + 16)
                if t >= 2:
                    dve.wait_ge(sem(f"rows_st{s}"), 64 + 16 * (t // 2))
                link(TS(f_o[s], f_y[s][0], w1[:, t:t + 1], None, ALU.mult))
                link(STT(f_o[s], f_y[s][1], w2[:, t:t + 1], f_o[s], ALU.mult, ALU.add))
                link(TT(f_o[s], f_o[s], gt2, ALU.mult))
                TT(f_o[s], f_o[s], f_x[s], ALU.add).then_inc(sem("f_sum"), 1)


def kernel(**inputs):
    import numpy as np
    import concourse.bacc as bacc
    from concourse.bass_utils import run_bass_kernel_spmd

    nc = bacc.Bacc("TRN2", target_bir_lowering=False, num_devices=1)
    arrays, I = {}, {}
    for name, a in inputs.items():
        a = np.ascontiguousarray(a)
        arrays[f"in_{name}"] = a
        I[name] = nc.dram_tensor(f"in_{name}", a.shape, mybir.dt.from_np(a.dtype), kind="ExternalInput").ap()
    f32, i32 = mybir.dt.float32, mybir.dt.int32
    out = nc.dram_tensor("out_0", (1, T, D), f32, kind="ExternalOutput").ap()
    dram = [nc.dram_tensor(n, s, d, kind="Internal").ap() for n, s, d in (
        ("x1", (T, D), f32), ("xnorm", (T, D), f32), ("y_slots", (NB * P, D), f32),
        ("slot_table", (NBP * P, 1), i32), ("gate_rows", (2, D), f32))]
    hybrid_block(nc, I, out, dram)
    r = run_bass_kernel_spmd(nc, [arrays], core_ids=[0])
    return r.results[0]["out_0"]
```

```python
import concourse.bass as bass
from concourse import mybir
from contextlib import ExitStack

T, D = 1024, 1024
P = 128
NT, KT = T // P, D // P
H, N = 4, 64
CH = 8
NG, NE, TOPK, DE = 4, 32, 2, 512
NX = (T * TOPK - 1) // P
NB = NE + NX
NBP = 48
EPS, A_EPS = 1e-6, 64e-5
KAPPA = 0.6065306597126334
BIG = 1e30


def hybrid_block(nc, I, out, dram):
    f32, i32 = mybir.dt.float32, mybir.dt.int32
    ALU, ACT, AX = mybir.AluOpType, mybir.ActivationFunctionType, mybir.AxisListType.X
    ds, ts = bass.ds, bass.ts
    x1_d, xn_d, yslot_d, gates_d, ga_d, mp_d = dram

    ctx = ExitStack()
    with ctx:
        SB = ctx.enter_context(nc.sbuf_tensor("arena", [P, 52992], f32))[:, :]
        PS = [ctx.enter_context(nc.psum_tensor(f"bank{i}", [P, 512], f32))[:, :] for i in range(8)]
        sems = {}

        def sem(name):
            if name not in sems:
                sems[name] = ctx.enter_context(nc.semaphore(name))
            return sems[name]

        def view(off, *dims):
            n = 1
            for d in dims:
                n *= d
            v = SB[:, off:off + n]
            if len(dims) == 2:
                v = v.rearrange("p (a b) -> p a b", a=dims[0])
            if len(dims) == 3:
                v = v.rearrange("p (a b c) -> p a b c", a=dims[0], b=dims[1])
            return v

        G_AX, G_LF, G_Z, G_D, G_MR, G_ARGS, B_CLEARED = range(1, 8)
        G_F, G_ZT, G_ZM, G_MT = range(1, 5)
        F_B, F_A = 2 * NT, 4 * NT
        G_LN, G_DONE = range(1, 3)
        VECS, MOD1 = range(1, 3)
        R_MS, R_PLACES, SLOTS_KNOWN = range(1, 4)
        CONSTS, R_IOTA, R_IOTAP = range(1, 4)
        COND, ADA_ROW0, ADA_ROW2, A_TANH, A_GSIG = range(1, 6)
        ROOT_KK = NT
        ROOT_A = ROOT_KK + 4

        RING = [view(0, 8, 512), view(4096, 8, 512)]
        HT = view(8192, KT, T)
        PA = view(16384, 8, T)
        ADA = [view(16384, 8, 512), view(20480, 8, 512)]
        QK = view(24576, 4, T)
        VO = view(28672, NT, 512)
        XB = [view(28672 + 1024 * i, D) for i in range(4)]
        QC = view(32768, 4, T)
        KC = view(36864, 9 * P)
        VC = view(38016, 9, 2, 65)
        TMP0 = 39296
        CS = view(TMP0, 2, 9, 129)
        KK = view(TMP0 + 2322, 2, T)
        BA = view(TMP0 + 4370, 2, T)
        TMP1 = TMP0 + 6418
        RAW = [view(TMP1, 1028), view(TMP1 + 1028, 1028)]
        at = [TMP1 + 2056]

        def small(*dims):
            n = 1
            for d in dims:
                n *= d
            v = view(at[0], *dims)
            at[0] += n
            assert at[0] <= 52992, at[0]
            return v

        ident, ones = small(P), small(P)
        msk = small(4, P)
        sU, U = msk[:, 0, :], msk[:, 1, :]
        dist = small(2, 2 * P)
        blk1 = small(P)
        hd2 = small(2)
        id64 = small(N)
        lvl = small(7, P)
        lnxg, lnxb, hng = small(256), small(256), small(256)
        w2a2 = small(256)
        g2s = small(256)
        wr = small(KT, 36)
        br = small(36)
        vecs = small(112)
        at_v = [0]

        def vcol(n):
            at_v[0] += n
            return vecs[:, at_v[0] - n:at_v[0]]

        badac, n1g, n2g, mu = vcol(48), vcol(8), vcol(8), vcol(8)
        w0c, a0c, kkc, kac, rkc = (vcol(2) for _ in range(5))
        cb, cw, cond, qkg = vcol(4), vcol(16), vcol(8), vcol(2)
        cw = cw.rearrange("p (j i) -> p j i", j=4)
        vrow = view(24576, P)
        sh1, sc1, sh2, sc2 = small(8), small(8), small(8), small(8)
        kac1 = small(2)
        bif = small(8)
        sinkr, sinkb = small(8), small(8)
        ss, rstd = small(8), small(8)
        gif = small(NT, 8)
        eps24 = small(1)
        rowb = VO[:, 6]
        ada_r = [view(TMP0 + 5416, 512), view(TMP0 + 4096, 512)]
        acc = small(512)

        c_sc = view(TMP0, 8, 2 * P)
        c_pT = view(TMP0 + 2048, 16, P)
        c_q = view(TMP0 + 4096, 4, P)
        c_y = view(TMP0 + 4608, 8, N)
        c_mx, c_nm, c_es, c_dn = (view(TMP0 + 5120 + 8 * i, 8) for i in range(4))
        c_k = view(TMP0 + 5160, 2 * P)
        c_sq = view(TMP0, T)
        c_rs = [view(TMP0 + 1024, 512), view(TMP0 + 1536, 512)]
        b0 = [TMP0 + 5416]

        def btmp(*dims):
            n = 1
            for d in dims:
                n *= d
            v = view(b0[0], *dims)
            b0[0] += n
            assert b0[0] <= TMP1
            return v

        g_ax, g_lf, g_F, g_FL, g_Z, g_ZM = (btmp(32) for _ in range(6))
        g_M = btmp(H, 9)
        g_ml, g_dec, g_w, g_mt, g_int, g_emt, g_t = (btmp(32) for _ in range(7))
        g_zT, g_cm, g_mr, g_D = btmp(P), btmp(P), btmp(P), btmp(32)
        g_mc = btmp(1)
        b0[0] = TMP0
        b_q, b_k, b_kt = btmp(2, P), btmp(2, P), btmp(256)
        b_v, b_wv, b_st = btmp(H, 65), btmp(H, 65), btmp(2, 65)
        b_bd, b_e, b_sw = btmp(H, P), btmp(H, P), btmp(H, P)
        b_h, b_hh, b_sq = btmp(H, 65), btmp(H, N), btmp(H, N)
        b_d, b_rd, b_ms = btmp(H), btmp(H), btmp(H)
        assert b0[0] <= TMP0 + 5416
        FW = view(0, 8, P)
        FWC = view(1024, 4, P)
        FWB, FBB = view(1536, 8, P), view(2560, 2, P)
        m_sg = [view(2816, 512), view(3328, 512)]
        ga_o = view(4096, T)
        mp, m_t = view(4096, T), view(5120, 512)
        WA = view(5632, 2, D)
        a0_ = [28672]

        def atmp(*dims):
            n = 1
            for d in dims:
                n *= d
            if a0_[0] <= 32768 < a0_[0] + n:
                a0_[0] = 36864
            if 36864 < a0_[0] < TMP0 < a0_[0] + n:
                a0_[0] = 26624
            v = view(a0_[0], *dims)
            a0_[0] += n
            assert a0_[0] <= TMP0 and (a0_[0] <= 28672 or n + a0_[0] > 28672)
            return v

        a_sm = atmp(H, 4, P)
        a_lo = [atmp(H, P), atmp(H, P)]
        a_T, a_Tt = atmp(H, P), atmp(H, P)
        a_A1, a_AZ, a_WU = atmp(H, P), atmp(H, P), atmp(H, P)
        a_tok = atmp(3, 256)
        a_ar, a_bk = atmp(2, 2, P), atmp(2, 2, P)
        a_v, a_rk = atmp(2, P), view(TMP1, 2, P)
        a_sg = view(TMP1 + 256, P)
        a_wr = view(TMP1 + 384, 2, P)
        a_e = view(TMP1 + 640, 2, 129)
        a_ei = view(TMP1 + 898, 2, P)
        a_qs = view(TMP1 + 1154, 2, N)
        a_st = view(TMP1 + 1282, 2, N)
        a_gs = view(TMP1 + 1410, 2, N)
        a_nb, a_g = view(TMP1 + 1538, 2), view(TMP1 + 1540, 2)
        a_pb = view(TMP1 + 1542, 2)
        a_y = view(TMP1 + 1544, H, N)
        a_t4, a_m4, a_bon = view(TMP1 + 1800, H), view(TMP1 + 1804, H), view(TMP1 + 1808, H)
        a_y2 = acc[:, 0:256].rearrange("p (h n) -> p h n", h=H)
        a_sgt = view(TMP1 + 1812, 2)
        k_sq = [view(30720, 512), view(31232, 512), RAW[0][:, 0:512], RAW[1][:, 0:512]]
        k_rn = [view(31744, T), view(36864, T)]
        MT = [HT[:, c] for c in range(8)]
        GA = [view(TMP0 + T * c, T) for c in range(6)] + [view(26624, T), view(27648, T)]
        YT = [PA[:, 0], PA[:, 1], QK[:, 0], QK[:, 1], QC[:, 0], QC[:, 1], QC[:, 2], QC[:, 3]]
        WO = [view(22528, 8, 512), view(18432, 8, 512)]
        o_x = [view(28672 + 1024 * i, D) for i in range(2)]
        o_n = [view(30720 + 1024 * i, D) for i in range(2)]
        gt1, gtb = view(36864, D), view(37888, D)
        o_hT = view(TMP0 + 1024, KT, P)
        o_sq = view(TMP0 + 2048, D)
        r_lg = view(TMP0 + 3072, NT, 36)
        r0_ = [TMP0 + 3072 + 288]

        def rtmp(*dims):
            n = 1
            for d in dims:
                n *= d
            v = view(r0_[0], *dims)
            r0_[0] += n
            assert r0_[0] <= TMP1 + 2056
            return v

        r_8 = [rtmp(NT) for _ in range(10)]
        r_g4 = [rtmp(NT, NG) for _ in range(3)]
        r_m1, r_m2 = rtmp(NT, NE), rtmp(NT, NE)
        r_em, r_t = rtmp(NT, NE), rtmp(NT, NE)
        r_nx, r_cum, r_ov, r_io = (rtmp(NE) for _ in range(4))
        r_i4 = rtmp(NG)
        r_ex = rtmp(NX, NE)
        r_iP, r_tok = rtmp(P), rtmp(NT)
        r_pos, r_blk = [rtmp(NT), rtmp(NT)], [rtmp(NT), rtmp(NT)]
        r_hot = [view(26624, NT, P), view(27648, NT, P)]
        r_in = [rtmp(NT, NBP), rtmp(NT, NBP)]
        r_pre, r_rk = rtmp(NT + 1, NE), rtmp(NT, NE)
        r_exs = rtmp(NX + 1)
        sb_i = ctx.enter_context(nc.sbuf_tensor("ints", [P, 160], i32))[:, :]
        i_tok, i_s1, i_s2 = (sb_i[:, 8 * k:8 * k + 8] for k in range(3))
        i_tab = sb_i[:, 40:40 + NBP]
        i_ex = sb_i[:, 88:88 + NX + 1]
        i_hi, i_lo = sb_i[:, 104:112], sb_i[:, 112:120]
        i_ix = [sb_i[:, 152:153], sb_i[:, 153:154], sb_i[:, 154:155]]
        WE = [[view(12288 * s + 4096 * j, 4, 1024) for j in range(3)] for s in range(2)]
        e_xs = [view(24576, D), view(25600, D)]
        e_xT = [view(26624, KT, P), view(27648, KT, P)]
        e_h, e_hT, e_g = view(32768, DE), view(33280, 4, P), view(33792, DE)
        e_y = [view(34304, D), view(35328, D)]
        gt2, gt2b = view(38912, D), e_y[1]
        f_x = [view(1024 * t, D) for t in range(NT)]
        f_y = [[view(12288 + 2048 * i, D), view(12288 + 2048 * i + 1024, D)] for i in range(4)]

        def bc(ap, n):
            return ap.unsqueeze(2).to_broadcast([ap.shape[0], ap.shape[1], n])

        def mm(o, l, r, start=True, stop=True):
            return nc.tensor.matmul(o, l, r, start=start, stop=stop)

        V, A, G, E = nc.vector, nc.scalar, nc.gpsimd, nc.tensor
        TT, TS, STT = V.tensor_tensor, V.tensor_scalar, V.scalar_tensor_tensor

        w_in = I["w_in"][0].rearrange("(k p) n -> p k n", p=P)
        w_ada = I["w_ada"][0].rearrange("(k p) n -> p k n", p=P)
        w_out = I["w_out"][0].rearrange("(k p) n -> p k n", p=P)
        w_bra = I["w_br_a"][0].rearrange("(k p) n -> p k n", p=P)
        w_brb = I["w_br_b"][0].rearrange("(k p) n -> p k n", p=P)
        w_brc = I["w_br_c"][0].rearrange("(a i q) n -> a q i n", a=2, q=N)
        x_t = I["x"][0].rearrange("(t p) n -> t p n", p=P)
        out_t = out[0].rearrange("(t p) n -> t p n", p=P)
        x1_t = x1_d.rearrange("(t p) n -> t p n", p=P)
        xn_t = xn_d.rearrange("(t p) n -> t p n", p=P)
        ys_b = yslot_d.rearrange("(b p) n -> b p n", p=P)
        OFF_QK, OFF_VO, OFF_IF, OFF_QC, OFF_KC, OFF_G = 1024, 1536, 2048, 2056, 2568, 2824

        def as_rows(ap):
            while len(ap.shape) > 1:
                ap = ap[0] if ap.shape[0] == 1 else ap.rearrange("a b -> (a b)")
            return ap.rearrange("(k p) -> k p", p=P)

        vec_rows, n = [], 0
        for name in ("b_ada", "norm1_g", "norm2_g", "mu_a", "w0_a", "a0_a", "kk_a", "ka_a", "rk_a", "conv_b_b", "conv_w_b", "c"):
            src = as_rows(I[name])
            vec_rows.append((vrow[n:n + src.shape[0], :], src))
            n += src.shape[0]
        for k, name in enumerate(("qn_g_c", "kn_g_c")):
            for a in range(2):
                vec_rows.append((vrow[n + k:n + k + 1, N * a:N * a + N], I[name]))
        NV = n + 2

        def slot_loads(r):
            w = RING[r % 2]
            if r == 0:
                return [(w[:, :, P * i + N * a:P * i + N * a + N],
                         w_in[:, :, OFF_QC + 256 * a + N * i:OFF_QC + 256 * a + N * i + N])
                        for i in range(4) for a in range(2)]
            if r == 1:
                return [(w[:, :, 0:256], w_in[:, :, OFF_KC:OFF_KC + 256]),
                        (w[:, :, 256:264], w_in[:, :, OFF_IF:OFF_IF + 8])]
            return [(w[:, :, :], w_in[:, :, (OFF_QK, OFF_VO)[r - 2]:(OFF_QK, OFF_VO)[r - 2] + 512])]

        slot_count = [16, 16]
        slot_target = []
        for r in range(4):
            slot_count[r % 2] += 16 * len(slot_loads(r))
            slot_target.append(slot_count[r % 2])
        s_slot = [sem("weights_slot0"), sem("weights_slot1")]
        fy_in = [(sem("fy_in0"), 0), (sem("fy_in1"), 0), (sem("xs0_in"), 16 * (NE // 2)), (sem("xs1_in"), 16 * (NE // 2))]
        m_in = [(sem("wide_in0"), 80), (sem("wide_in1"), 80), (s_slot[0], slot_target[2]), (s_slot[1], slot_target[3])]

        smalls = [
            (bif[:, 0:4], I["bi_b"].to_broadcast([P, 4])), (bif[:, 4:8], I["bf_b"].to_broadcast([P, 4])),
            (lnxg, I["lnx_g_a"].to_broadcast([P, 256])), (lnxb, I["lnx_b_a"].to_broadcast([P, 256])),
            (hng, I["hn_g_b"].rearrange("a h n -> a (h n)").to_broadcast([P, 256])),
            (w2a2[0:64, :], I["w2_a"][0]), (w2a2[64:128, :], I["a2_a"][0]), (g2s, I["g2_a"][0]),
            (wr[:, :, 0:4], I["w_rg"][0].rearrange("(k p) n -> p k n", p=P)),
            (wr[:, :, 4:36], I["w_re"][0].rearrange("(k p) n -> p k n", p=P)),
            (br[:, 0:4], I["b_rg"].to_broadcast([P, 4])), (br[:, 4:36], I["b_re"].to_broadcast([P, 32])),
            (sinkr, I["sink_c"].to_broadcast([P, CH])),
        ]

        block = ctx.enter_context(nc.Block())

        @block.sync
        def _(sp):
            for t in range(4):
                sp.dma_start(XB[t], x_t[t]).then_inc(sem(f"rows_in{t % 4}"), 16)
            sp.wait_ge(sem("vecs_in"), 16 * len(vec_rows))

            def ada(i):
                if i == 4:
                    sp.wait_ge(sem("ada_sum"), 1)
                if i >= 5:
                    sp.wait_ge(sem("ada_acc"), 1 if i == 5 else i - 3)
                dst, loaded = (RING[i - 2], s_slot[i - 2]) if i in (2, 3) else (ADA[i % 2], sem(f"wide_in{i % 2}"))
                sp.dma_start(dst, w_ada[:, :, 512 * i:512 * i + 512]).then_inc(loaded, 16)

            def weights(r):
                if r == 0:
                    sp.wait_ge(sem("ada_sum"), 2)
                if r == 1:
                    sp.wait_ge(sem("ada_acc"), 2)
                if r >= 2:
                    sp.wait_ge(sem("proj"), (8, 18)[r - 2])
                for dst, src in slot_loads(r):
                    sp.dma_start(dst, src).then_inc(s_slot[r % 2], 16)

            for i in range(4):
                ada(i)
            for t in range(4, NT):
                sp.wait_ge(sem("x_used"), t - 3)
                sp.dma_start(XB[t % 4], x_t[t]).then_inc(sem(f"rows_in{t % 4}"), 16)
            weights(0)
            weights(1)
            for i in range(4, 8):
                ada(i)
            weights(2)
            ada(8)
            ada(9)
            weights(3)
            ada(10)
            ada(11)

            def columns(dst, o, c):
                sp.dma_start(dst, w_in[:, :, ds(o + P * c, P)]).then_inc(sem("fill_w"), 16)
            sp.wait_ge(sem("proj"), 26)
            columns(FW, 0, 0)
            sp.wait_ge(sem("proj"), 34)
            sp.dma_start(WA, w_bra).then_inc(sem("merge_w"), 16)
            with sp.Fori(1, NT) as c:
                sp.wait_ge(sem("fill"), 2 * c)
                columns(FW, 0, c)
            sp.wait_ge(sem("fill"), F_B)
            columns(FW, OFF_G, 0)

            def first_gate(c):
                sp.wait_ge(sem("ga_out"), 2 * c)
                sp.dma_start(ga_d[ds(c - 1, 1)].rearrange("o p n -> (o p) n"), ga_o).then_inc(sem("part_st"), 16)
            with sp.Fori(1, NT) as c:
                sp.wait_ge(sem("fill"), F_B + 2 * c)
                columns(FW, OFF_G, c)
                first_gate(c)

            def weights_c(c):
                columns(FW, OFF_G + 2 * D, c)
                for a in range(2):
                    sp.dma_start(FWC[64 * a:64 * a + 64], w_brc[a, :, :, ds(P * c, P)]).then_inc(sem("fill_w"), 16)

            def weights_b(c):
                sp.dma_start(FWB, w_in[:, :, ds(OFF_G + D + P * c, P)]).then_inc(sem("fill_wb"), 16)
                sp.dma_start(FBB, w_brb[:, :, ds(P * c, P)]).then_inc(sem("fill_wb"), 16)
            sp.wait_ge(sem("fill"), F_A)
            weights_c(0)
            weights_b(0)
            first_gate(NT)

            def part(c):
                sp.wait_ge(sem("m_added"), 2 * c)
                sp.dma_start(mp_d[ds(c - 1, 1)].rearrange("o p n -> (o p) n"), mp).then_inc(sem("part_st"), 16)
            with sp.Fori(1, NT) as c:
                sp.wait_ge(sem("fill"), F_A + 8 * c - 4)
                weights_c(c)
                sp.wait_ge(sem("fill"), F_A + 8 * c)
                weights_b(c)
                part(c)
            part(NT)
            sp.wait_ge(sem("mix_done"), 3 * NT)
            sp.wait_ge(sem("fill"), F_A + 8 * NT)
            sp.wait_ge(sem("part_st"), 32 * NT)
            for c in range(KT):
                if c >= 4:
                    sp.wait_ge(sem("m_sg"), 4 * NT + c - 3)
                sp.dma_start(GA[c], ga_d[c]).then_inc(m_in[c % 4][0], 16)
                sp.dma_start(MT[c], mp_d[c]).then_inc(m_in[c % 4][0], 16)
            for j in range(2):
                sp.dma_start(WO[j], w_out[:, :, 512 * j:512 * j + 512]).then_inc(sem("merge_w"), 16)

            sp.wait_ge(sem("row_out"), 16 * 4)
            sp.dma_start(gt1, gates_d[0:1, :].to_broadcast([P, D])).then_inc(sem("gate_in"), 16)
            sp.dma_start(gtb, I["b_ada"][:, 2 * D:3 * D].to_broadcast([P, D])).then_inc(sem("gate_in"), 16)
            sp.wait_ge(sem("m_added"), 2 * NT + 2)
            sp.dma_start(gt2, gates_d[1:2, :].to_broadcast([P, D])).then_inc(sem("gt2_in"), 16)
            sp.dma_start(gt2b, I["b_ada"][:, 5 * D:6 * D].to_broadcast([P, D])).then_inc(sem("gt2_in"), 16)
            for t in range(NT):
                if t >= 2:
                    sp.wait_ge(sem(f"rows_st{t % 2}"), 16 * (t // 2))
                    sp.wait_ge(sem("o_norm"), t - 1)
                    sp.wait_ge(sem("o_ss"), t - 1)
                sp.dma_start(o_x[t % 2], x_t[t]).then_inc(sem(f"rows_in{t % 2}"), 16)

            def expert_weights(e, s, first):
                if not first:
                    sp.wait_ge(sem("win_used"), e - 1)
                for j in range(2):
                    if first:
                        sp.wait_ge(sem("o_mm" if e else "m_pair"), 16)
                    sp.dma_start(WE[s][j], I["w_e_in"][0, ds(e, 1), 512 * j:512 * j + 512, :]
                                 .rearrange("a (k p) n -> p (a k) n", p=P)).then_inc(sem(f"win{s}_in"), 16)
                if not first:
                    sp.wait_ge(sem("y"), 2 * (e - 1))
                if first:
                    sp.wait_ge(sem("o_mm"), 16)
                sp.dma_start(WE[s][2], I["w_e_out"][0, ds(e, 1)]
                             .rearrange("a (k p) n -> p (a k) n", p=P)).then_inc(sem(f"wout{s}_in"), 16)

            expert_weights(0, 0, True)
            expert_weights(1, 1, True)
            with sp.Fori(1, NE // 2) as i:
                for s in range(2):
                    expert_weights(2 * i + s, s, False)
            sp.wait_ge(sem("y"), 2 * (NE - 1))
            for t in range(NT):
                sp.dma_start(f_x[t], x1_t[t]).then_inc(sem("gate_in"), 16)
            sp.wait_ge(sem("router_dve"), SLOTS_KNOWN)
            n_extra = sp.value_load(i_ex[0:1, NX:NX + 1], min_val=0, max_val=NX)
            sp.wait_ge(sem("y"), 2 * NE)
            with sp.If(n_extra > 0):
                with sp.Fori(0, NX) as j:
                    with sp.If(n_extra > j):
                        e = sp.value_load(i_ex[0:1, ds(j, 1)], min_val=0, max_val=NE - 1)
                        sp.wait_ge(sem("extra_go"), j + 1)
                        for k in range(2):
                            sp.dma_start(WE[1][k], I["w_e_in"][0, ds(e, 1), 512 * k:512 * k + 512, :]
                                         .rearrange("a (k p) n -> p (a k) n", p=P)).then_inc(sem("extra_w"), 16)
                        sp.dma_start(WE[1][2], I["w_e_out"][0, ds(e, 1)]
                                     .rearrange("a (k p) n -> p (a k) n", p=P)).then_inc(sem("extra_w"), 16)
                    with sp.Else():
                        sp.nop()
            with sp.Else():
                sp.nop()

        @block.gpsimd
        def _(pool):
            chain = [0]

            def link(ins):
                chain[0] += 1
                ins.then_inc(sem("pool_step"), 1)
                pool.wait_ge(sem("pool_step"), chain[0])

            link(G.memset(ones, 1.0))
            link(G.memset(ident, 0.0))
            link(G.affine_select(out=ident, in_=ident, compare_op=ALU.not_equal, fill=1.0, base=0,
                                 pattern=[[-1, P]], channel_multiplier=1))
            link(G.memset(msk, 1.0))
            for k, op in ((0, ALU.is_gt), (1, ALU.is_ge)):
                link(G.affine_select(out=msk[:, k, :], in_=msk[:, k, :], compare_op=op, fill=0.0, base=0,
                                pattern=[[1, P]], channel_multiplier=-1))
                link(G.affine_select(out=msk[:, k + 2, :], in_=msk[:, k + 2, :], compare_op=op, fill=0.0, base=0,
                                pattern=[[1, P]], channel_multiplier=-1))
            link(G.memset(blk1, 0.0))
            link(G.memset(hd2, 0.0))
            link(G.memset(id64, 0.0))
            link(G.memset(lvl, 0.0))
            for a in range(2):
                link(G.memset(blk1[64 * a:64 * a + 64, 64 * a:64 * a + 64], 1.0))
                link(G.memset(hd2[64 * a:64 * a + 64, a:a + 1], 1.0))
                link(G.affine_select(out=id64[64 * a:64 * a + 64, :], in_=id64[64 * a:64 * a + 64, :], compare_op=ALU.not_equal,
                                fill=1.0, base=0, pattern=[[-1, N]], channel_multiplier=1))
            for q in range(7):
                n = 1 << q
                v = lvl[:, q, :].rearrange("p (a b c) -> p a b c", b=2, c=n)[:, :, 1, :]
                m = P // (2 * n)
                link(G.memset(v, 1.0))
                link(G.affine_select(out=v, in_=v, compare_op=ALU.is_ge, fill=0.0, base=0,
                                     pattern=[[-2 * n, m], [0, n]], channel_multiplier=1))
                link(G.affine_select(out=v, in_=v, compare_op=ALU.is_gt, fill=0.0, base=n,
                                     pattern=[[2 * n, m], [0, n]], channel_multiplier=-1))
            link(G.iota(dist, pattern=[[0, 2], [-1, 2 * P]], base=P, channel_multiplier=1,
                        allow_small_or_imprecise_dtypes=True))
            link(G.affine_select(out=dist, in_=dist, compare_op=ALU.is_ge, fill=BIG, base=P,
                                 pattern=[[0, 2], [-1, 2 * P]], channel_multiplier=1))
            link(G.affine_select(out=dist, in_=dist, compare_op=ALU.is_gt, fill=BIG, base=0,
                                 pattern=[[0, 2], [1, 2 * P]], channel_multiplier=-1))
            link(G.memset(dist[:, 0, 0:P], BIG))
            link(G.memset(KC[:, 0:P], 0.0))
            link(G.memset(VC[:, 0, :, 0:64], 0.0))
            link(G.memset(VC[:, :, :, 64:65], 1.0))
            link(G.memset(RAW[0][:, 0:3], 0.0))
            link(G.memset(RAW[1][:, 0:3], 0.0))
            link(G.iota(i_tok, pattern=[[P, NT]], base=0, channel_multiplier=1))
            G.memset(eps24, 1e-24).then_inc(sem("setup_pool"), 1)
            pool.wait_ge(sem("x_used"), NT)
            for b in range(NE, NB):
                pool.dma_start(ys_b[b].rearrange("p (a n) -> p a n", a=8), KC[:, 0:P].unsqueeze(1).to_broadcast([P, 8, P]))\
                    .then_inc(sem("slots_zero"), 16)

            pool.wait_ge(sem("c_normed"), 5)
            def attn(c, first=False):
                if not first:
                    pool.wait_ge(sem("c_scores"), c)
                G.tensor_copy(c_k, KC[:, ds(P * c, 2 * P)])
                G.tensor_copy(c_q, QC[:, :, ts(c, P)]).then_inc(sem("mix_staged"), 1)
            attn(0, True)
            with pool.Fori(1, NT) as c:
                attn(c)

            pool.wait_ge(sem("gates_dve"), B_CLEARED)
            pool.wait_ge(sem("b_silu"), 4)
            pool.wait_ge(sem("proj_out"), 34)
            def mlstm(c, first=False):
                if not first:
                    pool.wait_ge(sem("b_num"), c)
                    pool.wait_ge(sem("b_wv"), c)
                G.tensor_copy(b_q, QK[:, 0:2, ts(c, P)])
                G.tensor_copy(b_v[:, :, 0:64], VO[:, ds(c, 1), 0:256].rearrange("p o (h n) -> p (o h) n", h=H))\
                    .then_inc(sem("mix_staged"), 1)
                pool.wait_ge(sem("b_exp"), c + 1)
                G.tensor_tensor(b_e, b_e, U.unsqueeze(1).to_broadcast([P, H, P]), ALU.mult).then_inc(sem("b_masked"), 1)
            mlstm(0, True)
            with pool.Fori(1, NT) as c:
                mlstm(c)

            pool.wait_ge(sem("slots_zero"), 16 * NX)
            pool.wait_ge(sem("a_prep"), 1)
            def tmix(c, first=False):
                if not first:
                    pool.wait_ge(sem("a_tr"), c)
                G.tensor_copy(a_v, PA[:, 4:6, ts(c, P)]).then_inc(sem("mix_staged"), 1)
                pool.wait_ge(sem("a_sm"), 4 * c + 4)
                for q in range(7):
                    if q >= 2:
                        pool.wait_ge(sem("a_A1"), 7 * c + q - 1)
                    elif not first:
                        pool.wait_ge(sem("a_A1"), 7 * c)
                    if q == 2:
                        pool.wait_ge(sem("a_Tt"), 7 * c + 1)
                    G.tensor_tensor(a_lo[q % 2], a_sm[:, :, 0, :], lvl[:, q, :].unsqueeze(1).to_broadcast([P, H, P]),
                                    ALU.mult).then_inc(sem("a_lo"), 1)
                for half in range(2):
                    pool.wait_ge(sem("m_prod"), 4 * c + 3 + half)
                    G.tensor_tensor(mp[:, ts(half, 512)], mp[:, ts(half, 512)], m_t, ALU.add).then_inc(sem("m_added"), 1)
            tmix(0, True)
            with pool.Fori(1, NT) as c:
                tmix(c)

            for n in range(16):
                c, hs = n // 2, slice(512 * (n % 2), 512 * (n % 2) + 512)
                pool.wait_ge(sem("m_prod"), 4 * NT + n + 1)
                G.tensor_tensor(MT[c][:, hs], MT[c][:, hs], GA[c][:, hs], ALU.add).then_inc(sem("m_added"), 1)

            pool.wait_ge(sem("o_mm"), 2)
            link(G.iota(r_i4, pattern=[[1, NG]], base=0, channel_multiplier=0, allow_small_or_imprecise_dtypes=True))
            G.iota(r_io, pattern=[[1, NE]], base=0, channel_multiplier=0, allow_small_or_imprecise_dtypes=True)\
                .then_inc(sem("setup_pool"), 1)
            pool.wait_ge(sem("setup_pool"), R_IOTA)
            G.iota(r_iP, pattern=[[1, P]], base=0, channel_multiplier=0, allow_small_or_imprecise_dtypes=True)\
                .then_inc(sem("setup_pool"), 1)
            pool.wait_ge(sem("router_dve"), SLOTS_KNOWN)
            pool.wait_ge(sem("xn_st0"), 16 * NT // 2)
            pool.wait_ge(sem("xn_st1"), 16 * NT // 2)

            def gather(e, s, wait):
                G.tensor_copy(i_ix[s], i_tab[:, ds(e, 1)]).then_inc(sem("ix_set"), 1)
                pool.wait_ge(sem("ix_set"), e + 1)
                if wait:
                    pool.wait_ge(sem("xs_used"), e - 1)
                pool.sem_inc(sem("gather_go"), 1)
                pool.indirect_dma_start(out=e_xs[s], out_offset=None, in_=xn_d,
                                        in_offset=bass.IndirectOffsetOnAxis(ap=i_ix[s], axis=0))\
                    .then_inc(sem(f"xs{s}_in"), 16)
            gather(0, 0, False)
            gather(1, 1, False)
            with pool.Fori(1, NE // 2) as i:
                for s in range(2):
                    pool.wait_ge(sem(f"xs{s}_in"), 16 * i)
                    gather(2 * i + s, s, True)
            n_extra = pool.value_load(i_ex[0:1, NX:NX + 1], min_val=0, max_val=NX)
            pool.wait_ge(sem("xs_used"), NE)
            with pool.If(n_extra > 0):
                with pool.Fori(0, NX) as j:
                    with pool.If(n_extra > j):
                        pool.wait_ge(sem("extra_go"), j + 1)
                        G.tensor_copy(i_ix[2], i_tab[:, ds(NE + j, 1)]).then_inc(sem("ix_set"), 1)
                        pool.wait_ge(sem("ix_set"), NE + 1 + j)
                        pool.sem_inc(sem("gather_go"), 1)
                        pool.indirect_dma_start(out=e_xs[1], out_offset=None, in_=xn_d,
                                                in_offset=bass.IndirectOffsetOnAxis(ap=i_ix[2], axis=0))\
                            .then_inc(sem("extra_xs"), 16)
                    with pool.Else():
                        pool.nop()
            with pool.Else():
                pool.nop()
            pool.wait_ge(sem("slots_zero"), 16 * NX)
            pool.wait_ge(sem("extra_end"), 1)
            for t in range(NT):
                if t >= 4:
                    pool.wait_ge(sem("f_sum"), t - 3)
                for k, ix in enumerate((i_s1, i_s2)):
                    pool.indirect_dma_start(out=f_y[t % 4][k], out_offset=None, in_=yslot_d,
                                            in_offset=bass.IndirectOffsetOnAxis(ap=ix[:, t:t + 1], axis=0))\
                        .then_inc(fy_in[t % 4][0], 16)

        @block.tensor
        def _(pe):
            pe.wait_ge(sem("setup_pool"), CONSTS)
            pe.wait_ge(sem("vecs_in"), 16 * len(vec_rows))
            E.transpose(PS[7][:, 0:NV], vrow[0:NV, :], ident[0:NV, 0:NV]).then_inc(sem("vecs_T"), 1)
            def ada_row(i):
                pe.wait_ge(s_slot[0] if i else sem("wide_in0"), 16)
                for k in range(KT):
                    ins = mm(PS[7 - i][0:1, :], cond[:, k:k + 1], (RING[0] if i else ADA[0])[:, k, :], k == 0, k == KT - 1)
                ins.then_inc(sem("ada_sum"), 1)

            def ada_columns(i):
                pe.wait_ge(sem("setup_act"), ADA_ROW2 if i else ADA_ROW0)
                for q in range(4):
                    mm(PS[6][:, 4 * i + q:4 * i + q + 1], ada_r[i // 2][0:1, ts(q, P)], ones[0:1, 0:1])

            def ada(i):
                pe.wait_ge(sem("ada_acc"), i // 2 + 1 if i < 4 else i - 1)
                if i % 6 < 4:
                    for q in range(4):
                        ins = mm(PS[6][:, 4 * i + q:4 * i + q + 1], acc[:, ts(q, P)], ones[:, 0:1])
                else:
                    if i == 4:
                        pe.wait_ge(sem("setup_dve"), VECS)
                    if i > 4:
                        pe.wait_ge(sem("row"), (5, 10, 11).index(i) + 1)
                    ins = mm(PS[7][:, :], ones, acc)
                ins.then_inc(sem("ada_sum"), 1)

            pe.wait_ge(sem("setup_act"), COND)
            ada_row(0)
            ada_row(2)
            ada_columns(0)
            ada_columns(2)
            ada(1)
            ada(3)
            for t in range(NT):
                pe.wait_ge(sem("x_norm"), t + 1)
                if t >= 2:
                    pe.wait_ge(sem("xT_a"), t - 1)
                    pe.wait_ge(sem("xT_v"), t - 1)
                for k in range(KT):
                    ins = E.transpose(PS[2 * (t % 2) + k // 4][:, ts(k % 4, P)], XB[t % 4][:, ts(k, P)], ident)
                ins.then_inc(sem("x_used"), 1)
            pe.wait_ge(sem("xT_a"), NT)
            pe.wait_ge(sem("xT_v"), NT)

            g = [0]

            def group(width, operands, lastslot=None):
                b = PS[g[0] % 2]
                if g[0] >= 2:
                    pe.wait_ge(sem("proj_out"), g[0] - 1)
                for k in range(KT):
                    l, r = operands(k)
                    ins = mm(b[:, 0:width], l, r, k == 0, k == KT - 1)
                ins.then_inc(sem("proj"), 1)
                g[0] += 1
                return ins

            def by_channel(r, n_tiles, after=None):
                pe.wait_ge(s_slot[r % 2], slot_target[r])
                w = RING[r % 2]
                for i in range(n_tiles):
                    for half in range(2):
                        group(512, lambda k: (w[:, k, ts(i, P)], HT[:, k, ts(half, 512)]))
                    if after:
                        after(i)

            def c_norm(i):
                for half in range(2):
                    pe.wait_ge(sem("c_sq"), 2 * i + half + 1)
                    if i:
                        pe.wait_ge(sem("c_rs"), 2 * i + half - 1)
                    mm(PS[2 + half], blk1, c_sq[:, ts(half, 512)]).then_inc(sem("c_ss"), 1)

            def after_q(i):
                if i:
                    c_norm(i - 1)
                if i >= 2:
                    ada(i + 2)

            by_channel(0, 4, after_q)
            pe.wait_ge(s_slot[1], slot_target[1])
            w1 = RING[1]
            for half in range(2):
                group(512, lambda k: (w1[:, k, 0:P], HT[:, k, ts(half, 512)]))
            c_norm(3)
            ada(6)
            for t in range(NT):
                group(136, lambda k: (HT[:, k, ts(t, P)], w1[:, k, P:264]))
                if t == 0:
                    c_norm(4)
            by_channel(2, 4, lambda i: ada(7 + i))
            pe.wait_ge(s_slot[1], slot_target[3])
            def gates(n):
                pe.wait_ge(sem("gates_dve"), (G_LF, G_Z, G_D, G_MR)[n])
                if n == 0:
                    mm(PS[6][:, 0:32], U, g_lf)
                    ins = mm(PS[6][:, 32:64], ones, g_lf)
                if n == 1:
                    ins = E.transpose(PS[7][0:32, 0:P], g_Z, ident)
                if n == 2:
                    ins = mm(PS[6][:, 64:96], ones[0:32, :], g_D[0:32, :])
                if n == 3:
                    ins = E.transpose(PS[7][:, 128:160], g_mr[0:32, :], ident[0:32, 0:32])
                ins.then_inc(sem("gates_pe"), 1)
            for t in range(NT):
                group(512, lambda k: (HT[:, k, ts(t, P)], RING[1][:, k, :]))
                if t == 2:
                    ada(11)
                if t >= 4:
                    gates(t - 4)
            pe.wait_ge(sem("gates_dve"), G_ARGS)

            pe.wait_ge(sem("c_normed"), 5)
            pe.wait_ge(sem("proj_out"), g[0])
            def attn_fill(c, first, j0, j1):
                for j in range(j0, j1):
                    half, k = j // 8, j % 8
                    if j == 0:
                        pe.wait_ge(sem("fill_w"), 16 * c + 16)
                    if k == 0 and not (first and half == 0):
                        pe.wait_ge(sem("pa_out"), 2 * c + half)
                    ins = mm(PS[1], FW[:, k, :], HT[:, k, ts(half, 512)], k == 0, k == 7)
                    if k == 7:
                        ins.then_inc(sem("fill"), 1)

            def attn(c, first=False):
                pe.wait_ge(sem("mix_staged"), c + 1)
                for a in range(2):
                    for i in range(4):
                        ins = mm(PS[2 + 2 * a + i // 2][:, ts(i % 2, 2 * P)], c_q[64 * a:64 * a + 64, i, :],
                                 c_k[64 * a:64 * a + 64, :])
                ins.then_inc(sem("c_scores"), 1)
                attn_fill(c, first, 0, 11)
                pe.wait_ge(sem("c_p"), c + 1)
                for j in range(16):
                    ins = E.transpose(PS[2 + j // 4][:, ts(j % 4, P)], c_sc[:, j // 2, ts(j % 2, P)], ident)
                    if j % 4 == 3:
                        ins.then_inc(sem("c_pT"), 1)
                attn_fill(c, first, 11, 14)
                pe.wait_ge(sem("c_pT_out_v"), c + 1)
                pe.wait_ge(sem("c_pT_out_a"), c + 1)
                for j in range(8):
                    o = PS[6 + j // 4][:, ds(65 * (j % 4), 65)]
                    for kb in range(2):
                        ins = mm(o, c_pT[:, 2 * j + kb, :], VC[:, ds(c + kb, 1), j % 2, :].rearrange("p o n -> p (o n)"),
                                 kb == 0, kb == 1)
                ins.then_inc(sem("c_pv"), 1)
                attn_fill(c, first, 14, 16)
                pe.wait_ge(sem("mix_y"), c + 1)
                for i in range(4):
                    ins = E.transpose(PS[0][:, ts(i, P)], c_y[:, 2 * i:2 * i + 2, :].rearrange("p a n -> p (a n)"), ident)
                ins.then_inc(sem("mix_yT"), 1)
            attn(0, True)
            with pe.Fori(1, NT) as c:
                attn(c)
            pe.wait_ge(sem("mix_done"), NT)

            pe.wait_ge(sem("gates_dve"), B_CLEARED)
            pe.wait_ge(sem("gates_act"), G_DONE)

            def fill(c, first, j0, j1):
                for j in range(j0, j1):
                    half, k = j // 8, j % 8
                    if j == 0:
                        pe.wait_ge(sem("fill_w"), 16 * NT + 16 * c + 16)
                    if k == 0 and not first:
                        pe.wait_ge(sem("ga_out"), 2 * c + half - 1)
                    ins = mm(PS[5 + half], FW[:, k, :], HT[:, k, ts(half, 512)], k == 0, k == 7)
                    if k == 7:
                        ins.then_inc(sem("fill"), 1)

            def mlstm(c, first=False):
                pe.wait_ge(sem("mix_staged"), NT + c + 1)
                pe.wait_ge(sem("b_k"), c + 1)
                pe.wait_ge(sem("b_bd"), c + 1)
                mm(PS[0], ones[0:32, :], b_bd[0:32]).then_inc(sem("b_mu"), 1)
                for a in range(2):
                    for p in range(2):
                        ins = mm(PS[1 + a][:, ts(p, P)], b_k[64 * a:64 * a + 64, p, :], b_q[64 * a:64 * a + 64, p, :])
                for p in range(2):
                    ins = E.transpose(PS[3][:, ts(p, P)], b_k[:, p, :], ident)
                ins.then_inc(sem("b_scores"), 1)
                fill(c, first, 0, 3)
                if not first:
                    pe.wait_ge(sem("b_state"), c)
                pe.wait_ge(sem("b_kt"), c + 1)
                pe.wait_ge(sem("b_arg"), c + 1)
                for a in range(2):
                    for p in range(2):
                        ins = mm(PS[3 * a][:, ds(65 * p, 65)], b_q[64 * a:64 * a + 64, p, :], b_st[64 * a:64 * a + 64, p, :])
                pe.wait_ge(sem("b_wv"), c + 1)
                for h in range(H):
                    a, p = h % 2, h // 2
                    ins = mm(PS[7][64 * a:64 * a + 64, ds(65 * p, 65)], b_kt[:, ts(h, N)], b_wv[:, h, :])
                ins.then_inc(sem("b_inter"), 1)
                fill(c, first, 3, 8)
                pe.wait_ge(sem("b_sw"), c + 1)
                for h in range(H):
                    ins = mm(PS[4][:, ds(65 * h, 65)], b_sw[:, h, :], b_v[:, h, :])
                ins.then_inc(sem("b_num"), 1)
                fill(c, first, 8, 16)
                pe.wait_ge(sem("mix_y"), NT + c + 1)
                for p in range(2):
                    ins = E.transpose(PS[3][:, ts(2 + p, P)], b_hh[:, 2 * p:2 * p + 2, :].rearrange("p a n -> p (a n)"), ident)
                ins.then_inc(sem("mix_yT"), 1)
            mlstm(0, True)
            with pe.Fori(1, NT) as c:
                mlstm(c)
            pe.wait_ge(sem("mix_done"), NT + NT)

            pe.wait_ge(sem("setup_act"), A_TANH)
            q = 0
            for p in range(2):
                for half in range(2):
                    hs = slice(512 * half, 512 * half + 512)
                    if q >= 2:
                        pe.wait_ge(sem("a_sig"), 2 * (q - 1))
                    mm(PS[2 * (q % 2)], w2a2[0:64, ts(p, P)], PA[0:64, 6, hs])
                    mm(PS[2 * (q % 2) + 1], w2a2[64:128, ts(p, P)], PA[64:128, 6, hs]).then_inc(sem("a_lora"), 1)
                    q += 1
            pe.wait_ge(sem("ga_out"), F_B)
            for q in range(4):
                pe.wait_ge(sem("a_sq"), q + 1)
                mm(PS[4 + q], blk1, k_sq[q]).then_inc(sem("a_ss"), 1)
            pe.wait_ge(sem("a_prep"), 1)
            fill_sums = [(n, k, n_of) for n, n_of in enumerate((12, 12, 10, 10)) for k in range(n_of)]

            def side(c, first, j0, j1):
                for n, k, n_of in fill_sums[j0:j1]:
                    hs, third = slice(512 * (n % 2), 512 * (n % 2) + 512), n < 2
                    if k == 0:
                        if n == 0:
                            pe.wait_ge(sem("fill_w"), 16 * 2 * NT + 48 * c + 48)
                        if n == 2:
                            pe.wait_ge(sem("fill_wb"), 32 * c + 32)
                        if n or not first:
                            pe.wait_ge(sem("m_sg"), 4 * c + n)
                    if k == 8 and (n or not first):
                        pe.wait_ge(sem("m_prod"), 4 * c + n)
                    if k < 8:
                        ins = mm(PS[6], (FW if third else FWB)[:, k, :], HT[:, k, hs], k == 0, k == 7)
                    else:
                        w, y = (FWC, YT[4:8]) if third else (FBB, YT[2:4])
                        ins = mm(PS[7], w[:, k - 8, :], y[k - 8][:, hs], k == 8, k == n_of - 1)
                    if k == 7 or k == n_of - 1:
                        ins.then_inc(sem("fill"), 1)

            def tmix(c, first=False):
                side(c, first, 0, 4)
                pe.wait_ge(sem("a_abkr"), c + 1)
                pe.wait_ge(sem("mix_staged"), 2 * NT + c + 1)
                for p in range(2):
                    E.transpose(PS[0][:, ts(p, P)], a_ar[:, p, 0, :], ident)
                    E.transpose(PS[0][:, ts(2 + p, P)], a_bk[:, p, 0, :], ident)
                    E.transpose(PS[1][:, ts(p, P)], a_bk[:, p, 1, :], ident)
                    ins = E.transpose(PS[1][:, ts(2 + p, P)], a_v[:, p, :], ident)
                ins.then_inc(sem("a_tr"), 1)
                for h in range(H):
                    a, p = h % 2, h // 2
                    rows = slice(64 * a, 64 * a + 64)
                    ar = a_ar[rows, p].rearrange("p a n -> p (a n)")
                    mm(PS[2 + h][:, 0:256], a_bk[rows, p, 0, :], ar)
                    mm(PS[2 + h][:, 256:512], a_bk[rows, p, 1, :], ar).then_inc(sem("a_scores"), 1)
                side(c, first, 4, 8)
                for q in range(7):
                    if q:
                        side(c, first, 4 + 4 * q, 6 + 4 * q)
                    pe.wait_ge(sem("a_lo"), 7 * c + q + 1)
                    if q:
                        pe.wait_ge(sem("a_T"), 6 * c + q)
                        pe.wait_ge(sem("a_Tt"), 7 * c + q)
                    for h in range(H):
                        ins = mm(PS[2][:, ts(h, P)], a_lo[q % 2][:, h, :], ident if q == 0 else a_T[:, h, :])
                    ins.then_inc(sem("a_A1"), 1)
                    if q:
                        side(c, first, 6 + 4 * q, 8 + 4 * q)
                        pe.wait_ge(sem("a_A1s"), 6 * c + q)
                        if q < 6:
                            for h in range(H):
                                ins = mm(PS[3][:, ts(h, P)], a_Tt[:, h, :], a_A1[:, h, :])
                            ins.then_inc(sem("a_P2"), 1)
                        for h in range(H):
                            ins = mm(PS[4][:, ts(h, P)], a_A1[:, h, :], a_Tt[:, h, :])
                        ins.then_inc(sem("a_Pt"), 1)
                pe.wait_ge(sem("a_tok"), c + 1)
                for h in range(H):
                    ins = mm(PS[5][:, ts(h, N)], a_sm[:, h, 2, :], a_tok[:, 2, ts(h, N)])
                ins.then_inc(sem("a_Z"), 1)
                pe.wait_ge(sem("a_rk"), c + 1)
                pe.wait_ge(sem("a_sg"), c + 1)
                for p in range(2):
                    mm(PS[0][:, ds(256 + 2 * p, 2)], a_rk[:, p, :], hd2)
                mm(PS[1][:, 256:512], a_sg, g2s).then_inc(sem("a_gb"), 1)
                pe.wait_ge(sem("a_Zs"), c + 1)
                pe.wait_ge(sem("a_Tt"), 7 * c + 7)
                for h in range(H):
                    ins = mm(PS[2][:, ts(h, P)], a_Tt[:, h, :], a_AZ[:, h, :])
                ins.then_inc(sem("a_WU"), 1)
                side(c, first, 32, 34)
                pe.wait_ge(sem("a_WUs"), c + 1)
                for h in range(H):
                    a, p = h % 2, h // 2
                    rows = slice(64 * a, 64 * a + 64)
                    mm(PS[3][rows, ts(p, P)], a_WU[:, h, 0:N], a_sm[:, h, 1, :])
                    ins = mm(PS[4][rows, ts(p, N)], a_WU[:, h, 0:N], a_tok[:, 0, ts(h, N)])
                for h in range(H):
                    a, p = h % 2, h // 2
                    rows = slice(64 * a, 64 * a + 64)
                    mm(PS[5][rows, ds(256 + 64 * p, N)], a_tok[:, 1, ts(h, N)], a_tok[:, 2, ts(h, N)], True, False)
                    ins = mm(PS[5][rows, ds(256 + 64 * p, N)], a_tok[:, 0, ts(h, N)], a_WU[:, h, N:P], False, True)
                ins.then_inc(sem("a_GS"), 1)
                side(c, first, 34, 36)
                pe.wait_ge(sem("a_Qs"), c + 1)
                if not first:
                    pe.wait_ge(sem("a_state"), c)
                for h in range(H):
                    o = PS[1][:, ts(h, N)]
                    mm(o, a_sm[:, h, 3, :], a_tok[:, 2, ts(h, N)], True, False)
                    mm(o, a_sm[:, h, 1, :], a_WU[:, h, N:P], False, True)
                for h in range(H):
                    a, p = h % 2, h // 2
                    rows = slice(64 * a, 64 * a + 64)
                    mm(PS[3 + a][:, ts(p, N)], a_wr[rows, p, :], a_st[rows, p, :])
                    ins = mm(PS[3 + a][rows, ts(2 + p, N)], a_qs[rows, p, :], a_st[rows, p, :])
                ins.then_inc(sem("a_Y"), 1)
                side(c, first, 36, 44)
                pe.wait_ge(sem("mix_y"), 2 * NT + c + 1)
                for p in range(2):
                    ins = E.transpose(PS[0][:, ts(p, P)], a_y[:, 2 * p:2 * p + 2, :].rearrange("p a n -> p (a n)"), ident)
                ins.then_inc(sem("mix_yT"), 1)
                pe.wait_ge(sem("mix_done"), 2 * NT + c + 1)
            tmix(0, True)
            with pe.Fori(1, NT) as c:
                tmix(c)

            pe.wait_ge(sem("merge_w"), 16)
            for n in range(16):
                if n < 4:
                    pe.wait_ge(sem("m_prod"), 4 * NT)
                else:
                    pe.wait_ge(sem("m_prod"), 4 * NT + n - 3)
                for k in range(2):
                    ins = mm(PS[n % 4], WA[:, k, ts(n // 2, P)], YT[k][:, ts(n % 2, 512)], k == 0, k == 1)
                ins.then_inc(sem("m_pair"), 1)
            pe.wait_ge(sem("m_added"), 2 * NT + 16)
            pe.wait_ge(sem("m_prod"), 4 * NT + 16)
            pe.wait_ge(sem("merge_w"), 48)

            def router(t):
                pe.wait_ge(sem("o_norm"), t + 1)
                for k in range(KT):
                    ins = E.transpose(PS[4 + k // 4][:, ts(k % 4, P)], o_n[t % 2][:, ts(k, P)], ident)
                ins.then_inc(sem("o_T"), 1)
                pe.wait_ge(sem("o_hT_a"), t + 1)
                pe.wait_ge(sem("o_hT_v"), t + 1)
                if t:
                    pe.wait_ge(sem("r_lg"), t)
                for k in range(KT):
                    ins = mm(PS[6][:, 0:36], o_hT[:, k, :], wr[:, k, :], k == 0, k == KT - 1)
                ins.then_inc(sem("r_mm"), 1)

            for t in range(NT):
                for j in range(2):
                    if t >= 2:
                        pe.wait_ge(sem("o_out"), 2 * (t - 2) + j + 1)
                    for k in range(KT):
                        ins = mm(PS[2 * (t % 2) + j], MT[k][:, ts(t, P)], WO[j][:, k, :], k == 0, k == KT - 1)
                    ins.then_inc(sem("o_mm"), 1)
                if t:
                    router(t - 1)
            router(NT - 1)
            pe.wait_ge(sem("router_dve"), R_MS)
            members = r_t.rearrange("p t e -> p (t e)")
            mm(PS[7][:, 0:256], sU, members)
            ins = mm(PS[6][:, 64:320], ones, members)
            ins.then_inc(sem("r_rank"), 1)
            pe.wait_ge(sem("router_dve"), R_PLACES)
            for n in range(2 * NT):
                ins = mm(PS[7][:, 256:256 + NBP], r_hot[n % 2][:, n // 2, :], r_in[n % 2][:, n // 2, :], n == 0, n == 2 * NT - 1)
            ins.then_inc(sem("r_rank"), 1)
            pe.wait_ge(sem("router_dve"), SLOTS_KNOWN)

            def xT(e, s):
                for k in range(KT):
                    ins = E.transpose(PS[k // 4][:, ts(k % 4, P)], e_xs[s][:, ts(k, P)], ident)
                ins.then_inc(sem("xs_used"), 1)

            def first(s, j):
                for u in range(2):
                    for k in range(4):
                        ins = mm(PS[3 + u], e_xT[s][:, 4 * j + k, :], WE[s][j][:, k, ts(u, DE)], j == 0 and k == 0, j == 1 and k == 3)
                return ins

            def hT():
                for k in range(4):
                    ins = E.transpose(PS[2][:, ts(k, P)], e_h[:, ts(k, P)], ident)
                ins.then_inc(sem("hT"), 1)

            def second(s):
                for u in range(2):
                    for k in range(4):
                        ins = mm(PS[5 + u], e_hT[:, k, :], WE[s][2][:, k, ts(u, 512)], k == 0, k == 3)
                    ins.then_inc(sem("y"), 1)

            def step(e, s, lo, i):
                pe.wait_ge(sem(f"win{s}_in"), 32 * i + 32)
                pe.wait_ge(sem("e_xT"), e + 1)
                if lo:
                    pe.wait_ge(sem("e_act"), e)
                first(s, 0)
                if lo:
                    hT()
                first(s, 1).then_inc(sem("win_used"), 1)

            def close(e, s, i):
                pe.wait_ge(sem("e_hT"), e + 1)
                pe.wait_ge(sem(f"wout{s}_in"), 16 * i + 16)

            pe.wait_ge(sem("xs0_in"), 16)
            xT(0, 0)
            step(0, 0, False, 0)
            pe.wait_ge(sem("xs1_in"), 16)
            pe.wait_ge(sem("e_xT"), 1)
            xT(1, 1)
            step(1, 1, True, 0)
            pe.wait_ge(sem("xs0_in"), 32)
            pe.wait_ge(sem("e_xT"), 2)
            xT(2, 0)
            close(0, 0, 0)
            second(0)
            with pe.Fori(1, NE // 2) as i:
                e = 2 * i
                step(e, 0, True, i)
                pe.wait_ge(sem("xs1_in"), 16 * i + 16)
                pe.wait_ge(sem("e_xT"), e + 1)
                xT(e + 1, 1)
                close(e - 1, 1, i - 1)
                pe.wait_ge(sem("y_out"), 2 * (e - 1))
                second(1)
                step(e + 1, 1, True, i)
                with pe.If(i < NE // 2 - 1):
                    pe.wait_ge(sem("xs0_in"), 16 * i + 32)
                    pe.wait_ge(sem("e_xT"), e + 2)
                    xT(e + 2, 0)
                with pe.Else():
                    pe.nop()
                close(e, 0, i)
                pe.wait_ge(sem("y_out"), 2 * e)
                second(0)
            pe.wait_ge(sem("e_act"), NE)
            hT()
            close(NE - 1, 1, NE // 2 - 1)
            pe.wait_ge(sem("y_out"), 2 * (NE - 1))
            second(1)
            n_extra = pe.value_load(i_ex[0:1, NX:NX + 1], min_val=0, max_val=NX)
            with pe.If(n_extra > 0):
                with pe.Fori(0, NX) as j:
                    with pe.If(n_extra > j):
                        pe.wait_ge(sem("extra_xs"), 16 * j + 16)
                        pe.wait_ge(sem("extra_w"), 48 * j + 48)
                        pe.wait_ge(sem("e_xT"), NE + j)
                        xT(0, 1)
                        pe.wait_ge(sem("e_xT"), NE + j + 1)
                        pe.wait_ge(sem("e_act"), NE + j)
                        first(1, 0)
                        first(1, 1).then_inc(sem("win_used"), 1)
                        pe.wait_ge(sem("e_act"), NE + j + 1)
                        hT()
                        pe.wait_ge(sem("e_hT"), NE + j + 1)
                        pe.wait_ge(sem("y_out"), 2 * (NE + j))
                        second(1)
                    with pe.Else():
                        pe.nop()
            with pe.Else():
                pe.nop()

        @block.scalar
        def _(act):
            chain = [0]

            def link(ins):
                chain[0] += 1
                ins.then_inc(sem("act_step"), 1)
                act.wait_ge(sem("act_step"), chain[0])

            for dst, src in vec_rows:
                act.dma_start(dst, src).then_inc(sem("vecs_in"), 16)
            for dst, src in smalls:
                act.dma_start(dst, src).then_inc(sem("small_in"), 16)
            act.wait_ge(sem("setup_dve"), VECS)
            A.activation(cond, cond, ACT.Silu).then_inc(sem("setup_act"), 1)
            act.wait_ge(sem("setup_pool"), CONSTS)
            def squares(t):
                act.wait_ge(sem(f"rows_in{t % 4}"), 16 * (t // 4) + 16)
                if t:
                    act.wait_ge(sem("x_ss"), t)
                link(A.activation(c_sq, XB[t % 4], ACT.Square, accum_out=ss[:, t:t + 1]))
                A.activation(ss[:, t:t + 1], ss[:, t:t + 1], ACT.Sqrt, scale=1.0 / D, bias=EPS).then_inc(sem("x_ss"), 1)
            for t in range(4):
                squares(t)
            for n in range(2):
                act.wait_ge(sem("ada_sum"), n + 1)
                A.activation(ada_r[n][0:1, :], PS[7 - 2 * n][0:1, :], ACT.Copy).then_inc(sem("setup_act"), 1)
            act.wait_ge(sem("setup_dve"), MOD1)
            for t in range(NT):
                act.wait_ge(sem("x_used"), t + 1)
                for k in range(4):
                    ins = A.activation(HT[:, k, ts(t, P)], PS[2 * (t % 2)][:, ts(k, P)], ACT.Identity,
                                       scale=sc1[:, k:k + 1], bias=sh1[:, k:k + 1])
                ins.then_inc(sem("xT_a"), 1)
                if t + 4 < NT:
                    squares(t + 4)
            g = [0]

            def bank():
                act.wait_ge(sem("proj"), g[0] + 1)
                b = PS[g[0] % 2]
                g[0] += 1
                return b

            def done(ins):
                ins.then_inc(sem("proj_out"), 1)

            def c_root(i):
                if i:
                    act.wait_ge(sem("c_normed"), i)
                for half in range(2):
                    act.wait_ge(sem("c_ss"), 2 * i + half + 1)
                    A.activation(c_rs[half], PS[2 + half], ACT.Sqrt, scale=1.0 / N, bias=EPS).then_inc(sem("c_rs"), 1)

            def c_tile(dst, i):
                for half in range(2):
                    b = bank()
                    done(A.activation(dst[:, ts(half, 512)], b, ACT.Copy))
                if i:
                    c_root(i - 1)
                for half in range(2):
                    act.wait_ge(sem("proj_out"), g[0] - 1 + half)
                    A.activation(c_sq[:, ts(half, 512)], dst[:, ts(half, 512)], ACT.Square).then_inc(sem("c_sq"), 1)
            def row(n):
                act.wait_ge(sem("ada_sum"), (5, 6, 11, 12)[n])
                if n:
                    act.wait_ge(sem("row_out"), 16 * n)
                A.activation(rowb[0:1, :], PS[7][0:1, :], ACT.Copy).then_inc(sem("row"), 1)
                act.wait_ge(sem("row"), n + 1)
                act.dma_start(gates_d[n // 2:n // 2 + 1, ts(n % 2, 512)], rowb[0:1, :]).then_inc(sem("row_out"), 16)

            for i in range(4):
                c_tile(QC[:, i], i)
                if i >= 2:
                    row(i - 2)
            c_tile(KC[:, P:], 4)
            for t in range(NT):
                b = bank()
                A.activation(VC[:, t + 1, :, 0:64], b[:, 0:128].rearrange("p (a n) -> p a n", a=2), ACT.Copy)
                done(A.activation(gif[:, t, :], b[:, 128:136], ACT.Copy))
                if t == 0:
                    c_root(4)
            for i in range(4):
                if i >= 2:
                    act.wait_ge(sem("b_conv"), i - 1)
                for half in range(2):
                    b = bank()
                    done(A.activation(RAW[i % 2][:, ds(3 + 512 * half, 512)], b, ACT.Copy))
            row(2)

            def silu_qk(i):
                act.wait_ge(sem("b_conv"), i + 1)
                A.activation(QK[:, i], QK[:, i], ACT.Silu).then_inc(sem("b_silu"), 1)
            silu_qk(0)
            silu_qk(1)
            for t in range(NT):
                b = bank()
                A.activation(VO[:, t, 256:512], b[:, 256:512], ACT.Sigmoid)
                done(A.activation(VO[:, t, 0:256], b[:, 0:256], ACT.Copy))
                if t < 2:
                    silu_qk(2 + t)
                if t == 3:
                    row(3)
                    act.wait_ge(sem("row_out"), 64)
                    act.wait_ge(sem("gates_dve"), G_AX)
                    link(A.activation(g_t, g_ax, ACT.Exp, scale=-1.0))
                    A.activation(g_t, g_t, ACT.Ln, bias=1.0).then_inc(sem("gates_act"), 1)
            act.wait_ge(sem("gates_dve"), G_ARGS)
            for v, sc in ((g_dec, 1.0), (g_w, 1.0), (g_int, 1.0), (g_emt, -1.0)):
                ins = A.activation(v, v, ACT.Exp, scale=sc)
            ins.then_inc(sem("gates_act"), 1)

            def attn(c):
                act.wait_ge(sem("c_nm"), c + 1)
                for j in range(8):
                    A.activation(c_sc[:, j, :], c_sc[:, j, :], ACT.Exp, bias=c_nm[:, j:j + 1])
                A.activation(c_es, c_es, ACT.Exp).then_inc(sem("c_p"), 1)
                act.wait_ge(sem("c_pT"), 4 * c + 2)
                A.activation(c_pT[:, 0:4, :], PS[2], ACT.Copy)
                A.activation(c_pT[:, 4:8, :], PS[3], ACT.Copy).then_inc(sem("c_pT_out_a"), 1)
                act.wait_ge(sem("mix_yT"), c + 1)
                A.activation(QC[:, :, ts(c, P)], PS[0].rearrange("p (i n) -> p i n", i=4), ACT.Copy).then_inc(sem("mix_done"), 1)
            with act.Fori(0, NT) as c:
                attn(c)

            def root(v, n):
                act.wait_ge(sem("root_asked"), n)
                A.activation(v, v, ACT.Sqrt).then_inc(sem("root_done"), 1)

            def mlstm(c, first=False):
                if not first:
                    act.wait_ge(sem("b_inter"), c)
                    act.wait_ge(sem("b_scores"), c)
                A.activation(b_k, QK[:, 2:4, ts(c, P)], ACT.Copy, scale=N ** -0.5).then_inc(sem("b_k"), 1)
                act.wait_ge(sem("b_scores"), c + 1)
                A.activation(b_kt, PS[3][:, 0:256], ACT.Copy).then_inc(sem("b_kt"), 1)
                act.wait_ge(sem("b_arg"), c + 1)
                A.activation(b_e, b_e, ACT.Exp, scale=-1.0).then_inc(sem("b_exp"), 1)
                if not first:
                    act.wait_ge(sem("part_st"), 16 * c)
                act.wait_ge(sem("fill"), F_B + 2 * c + 1)
                A.activation(ga_o[:, 0:512], PS[5], ACT.Copy).then_inc(sem("ga_out"), 1)
                root(b_ms, c + 1)
                act.wait_ge(sem("fill"), F_B + 2 * c + 2)
                A.activation(ga_o[:, 512:1024], PS[6], ACT.Copy).then_inc(sem("ga_out"), 1)
                act.wait_ge(sem("mix_yT"), NT + c + 1)
                A.activation(QK[:, 0:2, ts(c, P)], PS[3][:, 256:512].rearrange("p (a n) -> p a n", a=2), ACT.Copy)\
                    .then_inc(sem("mix_done"), 1)
            mlstm(0, True)
            with act.Fori(1, NT) as c:
                mlstm(c)

            act.wait_ge(sem("a_shift"), 8)
            A.activation(PA[0:64, 6], PA[0:64, 6], ACT.Tanh).then_inc(sem("setup_act"), 1)
            q = 0
            for p in range(2):
                for half in range(2):
                    hs = slice(512 * half, 512 * half + 512)
                    act.wait_ge(sem("a_lora"), q + 1)
                    A.activation(KK[:, p, hs], PS[2 * (q % 2)], ACT.Sigmoid, bias=w0c[:, p:p + 1]).then_inc(sem("a_sig"), 1)
                    A.activation(BA[:, p, hs], PS[2 * (q % 2) + 1], ACT.Sigmoid, bias=a0c[:, p:p + 1]).then_inc(sem("a_sig"), 1)
                    q += 1
            A.activation(PA[:, 7], PA[:, 7], ACT.Sigmoid).then_inc(sem("setup_act"), 1)
            for q in range(4):
                act.wait_ge(sem("a_kk"), q // 2 + 1)
                A.activation(k_sq[q], KK[:, q // 2, ts(q % 2, 512)], ACT.Square).then_inc(sem("a_sq"), 1)
            act.wait_ge(sem("root_asked"), ROOT_KK + 4)
            A.activation(k_rn[0], k_rn[0], ACT.Ln)
            link(A.activation(k_rn[1], k_rn[1], ACT.Ln))
            for p in range(2):
                A.activation(k_rn[p], k_rn[p], ACT.Exp, scale=-0.5).then_inc(sem("root_done"), 2)
            act.wait_ge(sem("setup_act"), A_GSIG)
            act.wait_ge(sem("a_prep"), 1)

            def gate(c, n, first=False):
                act.wait_ge(sem("fill"), F_A + 8 * c + 2 * n + 1)
                if n >= 2 or not first:
                    act.wait_ge(sem("m_prod"), 4 * c + n - 1)
                A.activation(m_sg[n % 2], PS[6], ACT.Sigmoid).then_inc(sem("m_sg"), 1)

            def tmix(c, first=False):
                act.wait_ge(sem("a_nb"), c + 1)
                for p in range(2):
                    A.activation(a_e[:, p, :], CS[:, p, ds(c, 1), :].rearrange("p o n -> p (o n)"), ACT.Exp,
                                 scale=-KAPPA, bias=a_nb[:, p:p + 1])
                    A.activation(a_ei[:, p, :], CS[:, p, ds(c, 1), 1:129].rearrange("p o n -> p (o n)"), ACT.Exp,
                                 scale=KAPPA, bias=a_pb[:, p:p + 1])
                A.activation(a_g, a_sgt, ACT.Exp, scale=-KAPPA).then_inc(sem("a_e"), 1)
                A.activation(a_sg, PA[:, 7, ts(c, P)], ACT.Copy).then_inc(sem("a_sg"), 1)
                act.wait_ge(sem("a_tr"), c + 1)
                A.activation(a_AZ[:, :, 0:N], PS[0][:, 0:256].rearrange("p (h n) -> p h n", h=H), ACT.Copy)
                A.activation(a_tok[:, 0, :], PS[0][:, 256:512], ACT.Copy)
                A.activation(a_tok[:, 1:3, :], PS[1].rearrange("p (a n) -> p a n", a=2), ACT.Copy).then_inc(sem("a_tok"), 1)
                gate(c, 0, first)
                for q in range(1, 7):
                    act.wait_ge(sem("a_A1"), 7 * c + q + 1)
                    A.activation(a_A1, PS[2].rearrange("p (h n) -> p h n", h=H), ACT.Copy).then_inc(sem("a_A1s"), 1)
                    if q == 3:
                        gate(c, 1, first)
                act.wait_ge(sem("a_Z"), c + 1)
                A.activation(a_AZ[:, :, N:P], PS[5][:, 0:256].rearrange("p (h n) -> p h n", h=H), ACT.Copy).then_inc(sem("a_Zs"), 1)
                gate(c, 2, first)
                act.wait_ge(sem("a_WU"), c + 1)
                A.activation(a_WU, PS[2].rearrange("p (h n) -> p h n", h=H), ACT.Copy).then_inc(sem("a_WUs"), 1)
                root(a_t4, ROOT_A + 1 + c)
                gate(c, 3, first)
                act.wait_ge(sem("mix_yT"), 2 * NT + c + 1)
                A.activation(PA[:, 0:2, ts(c, P)], PS[0][:, 0:256].rearrange("p (a n) -> p a n", a=2), ACT.Copy)\
                    .then_inc(sem("mix_done"), 1)
            tmix(0, True)
            with act.Fori(1, NT) as c:
                tmix(c)

            for c in range(KT):
                act.wait_ge(m_in[c % 4][0], m_in[c % 4][1] + 32 * (c // 4) + 32)
                A.activation(GA[c], GA[c], ACT.Sigmoid).then_inc(sem("m_sg"), 1)

            for t in range(NT):
                act.wait_ge(sem("o_x1"), t + 1)
                act.dma_start(x1_t[t], o_x[t % 2]).then_inc(sem(f"rows_st{t % 2}"), 16)
                if t:
                    act.wait_ge(sem("o_ss"), t)
                link(A.activation(o_sq, o_x[t % 2], ACT.Square, accum_out=ss[:, t:t + 1]))
                A.activation(ss[:, t:t + 1], ss[:, t:t + 1], ACT.Sqrt, scale=1.0 / D, bias=EPS).then_inc(sem("o_ss"), 1)
                act.wait_ge(sem("o_norm"), t + 1)
                act.dma_start(xn_t[t], o_n[t % 2]).then_inc(sem(f"xn_st{t % 2}"), 16)
                act.wait_ge(sem("o_T"), t + 1)
                for k in range(4):
                    ins = A.activation(o_hT[:, k, :], PS[4][:, ts(k, P)], ACT.Identity, scale=sc2[:, k:k + 1], bias=sh2[:, k:k + 1])
                ins.then_inc(sem("o_hT_a"), 1)
            for n, v in enumerate((r_g4[1].rearrange("p a b -> p (a b)"), r_8[5])):
                act.wait_ge(sem("r_arg"), n + 1)
                A.activation(v, v, ACT.Exp).then_inc(sem("r_exp"), 1)
            act.wait_ge(sem("router_dve"), SLOTS_KNOWN)

            def xT_out(e, s):
                act.wait_ge(sem("xs_used"), e + 1)
                for k in range(KT):
                    ins = A.activation(e_xT[s][:, k, :], PS[k // 4][:, ts(k % 4, P)], ACT.Identity,
                                       scale=sc2[:, k:k + 1], bias=sh2[:, k:k + 1])
                ins.then_inc(sem("e_xT"), 1)

            def hT_out(e):
                act.wait_ge(sem("hT"), e + 1)
                A.activation(e_hT, PS[2].rearrange("p (k n) -> p k n", k=4), ACT.Copy).then_inc(sem("e_hT"), 1)

            def silu(e, first=False):
                act.wait_ge(sem("win_used"), e + 1)
                if not first:
                    act.wait_ge(sem("e_act"), e)
                A.activation(e_g, PS[3], ACT.Silu).then_inc(sem("e_silu"), 1)

            def store(e, s):
                act.wait_ge(sem("y_out"), 2 * e + 2)
                act.dma_start(ys_b[ds(e, 1)].rearrange("o p n -> (o p) n"), e_y[s]).then_inc(sem(f"y_st{s}"), 16)

            xT_out(0, 0)
            silu(0, True)
            xT_out(1, 1)
            hT_out(0)
            silu(1)
            xT_out(2, 0)
            store(0, 0)
            with act.Fori(1, NE // 2) as i:
                e = 2 * i
                hT_out(e - 1)
                silu(e)
                xT_out(e + 1, 1)
                store(e - 1, 1)
                hT_out(e)
                silu(e + 1)
                with act.If(i < NE // 2 - 1):
                    xT_out(e + 2, 0)
                with act.Else():
                    act.nop()
                store(e, 0)
            hT_out(NE - 1)
            store(NE - 1, 1)
            for s in range(2):
                act.wait_ge(sem(f"y_st{s}"), 16 * NE // 2)
            n_extra = act.value_load(i_ex[0:1, NX:NX + 1], min_val=0, max_val=NX)
            act.wait_ge(sem("slots_zero"), 16 * NX)
            act.sem_inc(sem("extra_go"), 1)
            with act.If(n_extra > 0):
                with act.Fori(0, NX) as j:
                    with act.If(n_extra > j):
                        xT_out(NE + j, 1)
                        silu(NE + j)
                        hT_out(NE + j)
                        act.wait_ge(sem("y_out"), 2 * (NE + j) + 2)
                        act.dma_start(ys_b[ds(NE + j, 1)].rearrange("o p n -> (o p) n"), e_y[0]).then_inc(sem("y_stx"), 16)
                        act.wait_ge(sem("y_stx"), 16 * j + 16)
                        act.sem_inc(sem("extra_go"), 1)
                    with act.Else():
                        act.nop()
            with act.Else():
                act.nop()
            act.sem_inc(sem("extra_end"), 1)
            for t in range(NT):
                act.wait_ge(sem("f_sum"), t + 1)
                act.dma_start(out_t[t], f_x[t]).then_inc(sem("rows_st0"), 16)
            act.wait_ge(sem("rows_st0"), 64 + 16 * NT)

        @block.vector
        def _(dve):
            chain = [0]
            dsem = sem("dve_step")

            def link(ins):
                chain[0] += 1
                ins.then_inc(dsem, 1)
                dve.wait_ge(dsem, chain[0])

            def body_link(per_turn, c, turns=NT, begin=0):
                n = [0]

                def f(ins):
                    n[0] += 1
                    ins.then_inc(dsem, 1)
                    dve.wait_ge(dsem, c * per_turn + begin + n[0])
                f.n = n
                return f

            def root_by_act(ins, n):
                ins.then_inc(sem("root_asked"), 1)
                dve.wait_ge(sem("root_done"), n)

            dve.wait_ge(sem("vecs_T"), 1)
            V.tensor_copy(vecs[:, 0:NV], PS[7][:, 0:NV]).then_inc(sem("setup_dve"), 1)
            dve.wait_ge(sem("setup_dve"), VECS)
            link(TS(qkg[:, 0:1], qkg[:, 0:1], N ** -0.5, None, ALU.mult))
            link(TS(kac1, kac, -1.0, 1.0, ALU.mult, ALU.add))

            def norm(t):
                dve.wait_ge(sem("x_ss"), t + 1)
                r = rstd[:, t:t + 1]
                link(V.reciprocal(r, ss[:, t:t + 1]))
                TS(XB[t % 4], XB[t % 4], r, None, ALU.mult).then_inc(sem("x_norm"), 1)

            def ada(i):
                if i == 3:
                    dve.wait_ge(s_slot[1], 16)
                else:
                    dve.wait_ge(sem(f"wide_in{i % 2}"), 16 * (i // 2 if i > 3 else 1))
                if i > 1:
                    dve.wait_ge(sem("ada_sum"), max(i, 3))
                w = RING[1] if i == 3 else ADA[i % 2]
                link(TS(acc, w[:, 0, :], cond[:, 0:1], None, ALU.mult))
                for k in range(1, KT):
                    ins = STT(acc, w[:, k, :], cond[:, k:k + 1], acc, ALU.mult, ALU.add)
                    if k < KT - 1:
                        link(ins)
                ins.then_inc(sem("ada_acc"), 1)


            dve.wait_ge(sem("setup_act"), COND)
            ada(1)
            for t in range(4):
                norm(t)
            ada(3)

            def modulation(i0, sh, sc, gamma):
                link(TT(sh, PS[6][:, 4 * i0:4 * i0 + 8], badac[:, 4 * i0:4 * i0 + 8], ALU.add))
                link(TT(sc, PS[6][:, 4 * i0 + 8:4 * i0 + 16], badac[:, 4 * i0 + 8:4 * i0 + 16], ALU.add))
                return STT(sc, sc, 1.0, gamma, ALU.add, ALU.mult)

            dve.wait_ge(sem("ada_sum"), 4)
            modulation(0, sh1, sc1, n1g).then_inc(sem("setup_dve"), 1)
            dve.wait_ge(sem("setup_dve"), MOD1)
            for t in range(NT):
                dve.wait_ge(sem("x_used"), t + 1)
                for k in range(4, 8):
                    ins = TS(HT[:, k, ts(t, P)], PS[2 * (t % 2) + 1][:, ts(k - 4, P)], sc1[:, k:k + 1], sh1[:, k:k + 1],
                             ALU.mult, ALU.add)
                ins.then_inc(sem("xT_v"), 1)
                if t + 4 < NT:
                    norm(t + 4)

            def c_norm(i):
                dst = QC[:, i] if i < 4 else KC[:, P:]
                g = qkg[:, 0:1] if i < 4 else qkg[:, 1:2]
                for half in range(2):
                    dve.wait_ge(sem("c_rs"), 2 * i + half + 1)
                    link(V.reciprocal(c_rs[half], c_rs[half]))
                    ins = STT(dst[:, ts(half, 512)], dst[:, ts(half, 512)], g, c_rs[half], ALU.mult, ALU.mult)
                ins.then_inc(sem("c_normed"), 1)

            dve.wait_ge(sem("small_in"), 16 * len(smalls))
            V.tensor_copy(sinkb.rearrange("p (i a) -> p a i", a=2), sinkr.rearrange("p (a i) -> p a i", a=2))
            for i in range(4):
                c_norm(i)
                ada(4 + i)
            c_norm(4)
            ada(8)

            for i in range(4):
                dve.wait_ge(sem("proj_out"), 18 + 2 * i + 2)
                link(TS(QK[:, i], RAW[i % 2][:, 3:3 + T], cw[:, 3, i:i + 1], cb[:, i:i + 1], ALU.mult, ALU.add))
                for j in (2, 1, 0):
                    ins = STT(QK[:, i], RAW[i % 2][:, j:j + T], cw[:, j, i:i + 1], QK[:, i], ALU.mult, ALU.add)
                    if j:
                        link(ins)
                ins.then_inc(sem("b_conv"), 1)
                if i < 3:
                    ada(9 + i)
            dve.wait_ge(sem("ada_sum"), 12)
            link(modulation(6, sh2, sc2, n2g))

            def g48(v):
                return v.rearrange("p (c h) -> p c h", h=H)
            V.memset(g_M, 0.0)
            link(TT(gif, gif, bif.unsqueeze(1).to_broadcast([P, NT, 8]), ALU.add))
            STT(g48(g_ax), gif[:, :, 4:8], -1.0, gif[:, :, 4:8], ALU.mult, ALU.max).then_inc(sem("gates_dve"), 1)
            dve.wait_ge(sem("gates_act"), G_LN)
            STT(g48(g_lf), gif[:, :, 4:8], 0.0, g48(g_t), ALU.min, ALU.subtract).then_inc(sem("gates_dve"), 1)

            dve.wait_ge(sem("gates_pe"), G_F)
            V.tensor_copy(g_F, PS[6][:, 0:32])
            V.tensor_copy(g_FL, PS[6][:, 32:64])
            TT(g48(g_Z), gif[:, :, 0:4], g48(PS[6][:, 0:32]), ALU.subtract).then_inc(sem("gates_dve"), 1)
            dve.wait_ge(sem("gates_pe"), G_ZT)
            link(V.tensor_copy(g_zT[0:32, :], PS[7][0:32, 0:P]))
            link(V.tensor_tensor_scan(out=g_cm[0:32, :], data0=g_zT[0:32, :], data1=g_zT[0:32, :], initial=-3e38,
                                      op0=ALU.max, op1=ALU.max))
            TS(g_D[0:32, :], ident[0:32, 0:32], g_cm[0:32, 127:128], None, ALU.mult).then_inc(sem("gates_dve"), 1)
            dve.wait_ge(sem("gates_pe"), G_ZM)
            link(V.tensor_copy(g_ZM, PS[6][:, 64:96]))
            for h in range(H):
                ins = V.tensor_tensor_scan(out=g_M[:, h, 1:9], data0=g48(g_ZM)[:, :, h], data1=g48(g_FL)[:, :, h],
                                           initial=0.0, op0=ALU.max, op1=ALU.add)
            link(ins)
            M0 = g_M[:, :, 0:8].rearrange("p h c -> p c h")
            M1 = g_M[:, :, 1:9].rearrange("p h c -> p c h")
            link(TT(g48(g_ml), M1, g48(g_FL), ALU.subtract))
            TT(g48(g_dec), M0, g48(g_ml), ALU.subtract)
            TT(g_w, g_Z, g_ml, ALU.subtract)
            link(TT(g48(g_t[0:32, :]), g48(ident[0:32, 0:32]), M0[0:32], ALU.mult))
            link(V.tensor_reduce(out=g_mc[0:32, :], in_=g_t[0:32, :], axis=AX, op=ALU.add))
            TS(g_mr[0:32, :], g_cm[0:32, :], g_mc[0:32, 0:1], None, ALU.max).then_inc(sem("gates_dve"), 1)
            dve.wait_ge(sem("gates_pe"), G_MT)
            link(V.tensor_copy(g_mt, PS[7][:, 128:160]))
            TT(g48(g_int), M0, g48(g_mt), ALU.subtract)
            TT(g_emt, g_F, g_mt, ALU.add).then_inc(sem("gates_dve"), 1)

            chain0 = chain[0]

            def attn(c, row):
                lk = body_link(6, c, begin=chain0)
                dve.wait_ge(sem("c_scores"), c + 1)
                for i in range(4):
                    for a in range(2):
                        slope = 2.0 ** -(4 * a + i + 1)
                        ins = STT(c_sc[:, 2 * i + a, :], dist[:, row, :], -slope,
                                  PS[2 + 2 * a + i // 2][:, ts(i % 2, 2 * P)], ALU.mult, ALU.add)
                lk(ins)
                lk(V.tensor_reduce(out=c_mx, in_=c_sc, axis=AX, op=ALU.max))
                lk(TT(c_mx, c_mx, sinkb, ALU.max))
                TS(c_nm, c_mx, -1.0, None, ALU.mult)
                TT(c_es, sinkb, c_mx, ALU.subtract).then_inc(sem("c_nm"), 1)
                dve.wait_ge(sem("fill"), 2 * c + 1)
                V.tensor_copy(RAW[0][:, 3:515], PS[1]).then_inc(sem("pa_out"), 1)
                dve.wait_ge(sem("c_pT"), 4 * c + 4)
                V.tensor_copy(c_pT[:, 8:12, :], PS[4])
                V.tensor_copy(c_pT[:, 12:16, :], PS[5]).then_inc(sem("c_pT_out_v"), 1)
                dve.wait_ge(sem("c_pv"), c + 1)
                pv = [PS[6 + k][:, 0:260].rearrange("p (j n) -> p j n", j=4) for k in range(2)]
                for k in range(2):
                    ins = TT(c_dn[:, 4 * k:4 * k + 4], pv[k][:, :, 64], c_es[:, 4 * k:4 * k + 4], ALU.add)
                lk(ins)
                lk(V.reciprocal(c_dn, c_dn))
                for k in range(2):
                    ins = TT(c_y[:, 4 * k:4 * k + 4, :], pv[k][:, :, 0:64], bc(c_dn[:, 4 * k:4 * k + 4], 64), ALU.mult)
                ins.then_inc(sem("mix_y"), 1)
                dve.wait_ge(sem("fill"), 2 * c + 2)
                V.tensor_copy(RAW[0][:, 515:1027], PS[1]).then_inc(sem("pa_out"), 1)
                dve.wait_ge(sem("pa_out"), 2 * c + 2)
                pa = PA[:, ds(c, 1), :].rearrange("p o n -> p (o n)")
                lk(TT(pa, RAW[0][:, 2:2 + T], RAW[0][:, 3:3 + T], ALU.subtract))
                STT(pa, pa, mu[:, ds(c, 1)], RAW[0][:, 3:3 + T], ALU.mult, ALU.add).then_inc(sem("a_shift"), 1)
            attn(0, 0)
            with dve.Fori(1, NT) as c:
                attn(c, 1)
            chain[0] += 6 * NT
            dve.wait_ge(sem("mix_done"), NT)

            V.memset(b_v[:, :, 64:65], 1.0)
            V.memset(b_st, 0.0).then_inc(sem("gates_dve"), 1)
            dve.wait_ge(sem("gates_act"), G_DONE)
            dve.wait_ge(sem("gates_dve"), G_MR)

            chain0 = chain[0]

            def mlstm(c):
                lk = body_link(11, c, begin=chain0)
                dve.wait_ge(sem("mix_staged"), NT + c + 1)
                TT(b_wv, b_v, bc(g_w[:, ts(c, 4)], 65), ALU.mult).then_inc(sem("b_wv"), 1)
                TT(b_bd[0:32], g_mr[0:32, :].unsqueeze(1).to_broadcast([32, H, P]), bc(ident[0:32, ts(c, 4)], P), ALU.mult)\
                    .then_inc(sem("b_bd"), 1)
                dve.wait_ge(sem("b_mu"), c + 1)
                for h in range(H):
                    ins = TS(b_e[:, h, :], PS[0][:, ts(h, P)], g_Z[:, ds(4 * c + h, 1)], 0.0, ALU.subtract, ALU.max)
                ins.then_inc(sem("b_arg"), 1)
                dve.wait_ge(sem("b_scores"), c + 1)
                dve.wait_ge(sem("b_masked"), c + 1)
                for a in range(2):
                    ins = TT(b_sw.rearrange("p (q a) n -> p q a n", a=2)[:, :, a, :], PS[1 + a][:, 0:256].rearrange("p (q n) -> p q n", q=2),
                             b_e.rearrange("p (q a) n -> p q a n", a=2)[:, :, a, :], ALU.mult)
                ins.then_inc(sem("b_sw"), 1)
                dve.wait_ge(sem("b_inter"), c + 1)
                for a in range(2):
                    ins = TT(b_h.rearrange("p (q a) n -> p q a n", a=2)[:, :, a, :], PS[3 * a][:, 0:130].rearrange("p (q n) -> p q n", q=2),
                             bc(g_int[:, ts(c, 4)].rearrange("p (q a) -> p q a", a=2)[:, :, a], 65), ALU.mult)
                lk(ins)
                for h in range(H):
                    a, p = h % 2, h // 2
                    rows = slice(64 * a, 64 * a + 64)
                    ins = STT(b_st[rows, p, :], b_st[rows, p, :], g_dec[rows, ds(4 * c + h, 1)], PS[7][rows, ds(65 * p, 65)],
                              ALU.mult, ALU.add)
                ins.then_inc(sem("b_state"), 1)
                dve.wait_ge(sem("b_num"), c + 1)
                lk(TT(b_h, b_h, PS[4][:, 0:260].rearrange("p (h n) -> p h n", h=H), ALU.add))
                lk(STT(b_d, b_h[:, :, 64], -1.0, b_h[:, :, 64], ALU.mult, ALU.max))
                lk(TT(b_d, b_d, g_emt[:, ts(c, 4)], ALU.max))
                lk(V.reciprocal(b_rd, b_d))
                lk(TT(b_hh, b_h[:, :, 0:64], bc(b_rd, 64), ALU.mult))
                lk(TT(b_sq, b_hh, b_hh, ALU.mult))
                lk(V.tensor_reduce(out=b_ms, in_=b_sq, axis=AX, op=ALU.add))
                root_by_act(TS(b_ms, b_ms, 1.0 / N, EPS, ALU.mult, ALU.add), c + 1)
                lk(V.reciprocal(b_ms, b_ms))
                lk(TT(b_hh, b_hh, bc(b_ms, 64), ALU.mult))
                lk(TT(b_hh, b_hh, hng.rearrange("p (h n) -> p h n", h=H), ALU.mult))
                TT(b_hh, b_hh, VO[:, ds(c, 1), 256:512].rearrange("p o (h n) -> p (o h) n", h=H), ALU.mult).then_inc(sem("mix_y"), 1)
            with dve.Fori(0, NT) as c:
                mlstm(c)
            chain[0] += 11 * NT
            dve.wait_ge(sem("mix_done"), NT + NT)

            dve.wait_ge(sem("a_sig"), 8)
            V.memset(CS[:, :, :, 0:1], 0.0)
            V.memset(CS[:, :, 8, 1:129], 0.0)
            for p in range(2):
                for c in range(NT):
                    ins = V.tensor_tensor_scan(out=CS[:, p, c, 1:129], data0=ones, data1=KK[:, p, ts(c, P)], initial=0.0,
                                               op0=ALU.mult, op1=ALU.add)
                link(ins)
                TS(KK[:, p], PA[:, 2 + p], kkc[:, p:p + 1], None, ALU.mult).then_inc(sem("a_kk"), 1)
                dve.wait_ge(sem("a_kk"), p + 1)
            dve.wait_ge(sem("slots_zero"), 16 * NX)
            tmp = RAW[0][:, 516:1028]
            for q in range(4):
                p, hs = q // 2, slice(512 * (q % 2), 512 * (q % 2) + 512)
                link(TS(tmp, BA[:, p, hs], kac[:, p:p + 1], kac1[:, p:p + 1], ALU.mult, ALU.add))
                link(TT(PA[:, 2 + p, hs], PA[:, 2 + p, hs], tmp, ALU.mult))
                dve.wait_ge(sem("a_ss"), q + 1)
                TS(k_rn[p][:, hs], PS[4 + q], 1e-24, None, ALU.max).then_inc(sem("root_asked"), 1)
            for p in range(2):
                dve.wait_ge(sem("root_done"), ROOT_KK + 2 * p + 2)
                link(TT(KK[:, p], KK[:, p], k_rn[p], ALU.mult))
                TT(BA[:, p], BA[:, p], KK[:, p], ALU.mult).then_inc(sem("a_kkn"), 1)
            dve.wait_ge(sem("a_kkn"), 2)
            V.memset(a_st, 0.0).then_inc(sem("a_prep"), 1)
            dve.wait_ge(sem("a_prep"), 1)

            chain0 = chain[0]

            def gated(c, n, first=False):
                dve.wait_ge(sem("fill"), F_A + 8 * c + 2 * n + 2)
                dve.wait_ge(sem("m_sg"), 4 * c + n + 1)
                if n == 0:
                    dve.wait_ge(sem("part_st"), 16 * NT + 16 * c)
                if n == 3 or (n == 2 and not first):
                    dve.wait_ge(sem("m_added"), 2 * c + n - 2)
                dst = mp[:, ts(n, 512)] if n < 2 else m_t
                TT(dst, m_sg[n % 2], PS[7], ALU.mult).then_inc(sem("m_prod"), 1)

            def tmix(c, first=False):
                lk = body_link(15, c, begin=chain0)
                mid = CS[:, :, ds(c, 1), 64].rearrange("p a o -> p (a o)")
                TS(a_pb, mid, -KAPPA, None, ALU.mult)
                TS(a_nb, mid, KAPPA, None, ALU.mult)
                lk(TT(a_sgt, CS[:, :, ds(c, 1), 128].rearrange("p a o -> p (a o)"), mid, ALU.subtract))
                TT(a_sgt, a_sgt, CS[:, :, ds(c + 1, 1), 64].rearrange("p a o -> p (a o)"), ALU.add).then_inc(sem("a_nb"), 1)
                cs = ts(c, P)
                for p in range(2):
                    ins = STT(a_rk[:, p, :], PA[:, p, cs], rkc[:, p:p + 1], PA[:, 2 + p, cs], ALU.mult, ALU.mult)
                ins.then_inc(sem("a_rk"), 1)
                dve.wait_ge(sem("a_e"), c + 1)
                STT(a_ar[:, :, 0, :], KK[:, :, cs], -1.0, a_e[:, :, 0:128], ALU.mult, ALU.mult)
                TT(a_ar[:, :, 1, :], PA[:, 0:2, cs], a_e[:, :, 1:129], ALU.mult)
                TT(a_bk[:, :, 0, :], BA[:, :, cs], a_ei, ALU.mult)
                TT(a_bk[:, :, 1, :], PA[:, 2:4, cs], a_ei, ALU.mult).then_inc(sem("a_abkr"), 1)
                for h in range(H):
                    dve.wait_ge(sem("a_scores"), 4 * c + h + 1)
                    TT(a_sm[:, h], PS[2 + h].rearrange("p (a n) -> p a n", a=4), msk, ALU.mult).then_inc(sem("a_sm"), 1)
                idb = ident.unsqueeze(1).to_broadcast([P, H, P])
                for q in range(7):
                    if q == 0:
                        dve.wait_ge(sem("a_lo"), 7 * c + 1)
                        TT(a_Tt, a_lo[0], idb, ALU.add).then_inc(sem("a_Tt"), 1)
                        dve.wait_ge(sem("a_A1"), 7 * c + 1)
                        TT(a_T, PS[2].rearrange("p (h n) -> p h n", h=H), idb, ALU.add).then_inc(sem("a_T"), 1)
                        continue
                    if q < 6:
                        dve.wait_ge(sem("a_P2"), 5 * c + q)
                        TT(a_T, a_T, PS[3].rearrange("p (h n) -> p h n", h=H), ALU.add).then_inc(sem("a_T"), 1)
                    dve.wait_ge(sem("a_Pt"), 6 * c + q)
                    TT(a_Tt, a_Tt, PS[4].rearrange("p (h n) -> p h n", h=H), ALU.add).then_inc(sem("a_Tt"), 1)
                    if q in (1, 4):
                        gated(c, q // 4, first)
                gated(c, 2, first)
                dve.wait_ge(sem("a_GS"), c + 1)
                TT(a_wr, PS[3][:, 0:256].rearrange("p (a n) -> p a n", a=2), a_ar[:, :, 1, :], ALU.add)
                TT(a_qs, PS[4][:, 0:128].rearrange("p (a n) -> p a n", a=2), id64.unsqueeze(1).to_broadcast([P, 2, N]), ALU.add)
                for p in range(2):
                    ins = TS(a_gs[:, p, :], PS[5][:, ds(256 + 64 * p, N)], a_g[:, p:p + 1], None, ALU.mult)
                ins.then_inc(sem("a_Qs"), 1)
                dve.wait_ge(sem("a_Qs"), c + 1)
                dve.wait_ge(sem("a_Y"), c + 1)
                for h in range(H):
                    a, p = h % 2, h // 2
                    rows = slice(64 * a, 64 * a + 64)
                    ins = STT(a_st[rows, p, :], PS[3 + a][rows, ts(2 + p, N)], a_g[rows, p:p + 1], a_gs[rows, p, :], ALU.mult, ALU.add)
                ins.then_inc(sem("a_state"), 1)
                for a in range(2):
                    ins = V.tensor_copy(a_y.rearrange("p (q a) n -> p q a n", a=2)[:, :, a, :],
                                        PS[3 + a][:, 0:128].rearrange("p (q n) -> p q n", q=2))
                lk(ins)
                lk(TT(a_y, a_y, PS[1][:, 0:256].rearrange("p (h n) -> p h n", h=H), ALU.add))
                lk(V.tensor_reduce(out=a_m4, in_=a_y, axis=AX, op=ALU.add))
                lk(TS(a_m4, a_m4, -1.0 / N, None, ALU.mult))
                lk(TT(a_y, a_y, bc(a_m4, N), ALU.add))
                lk(TT(a_y2, a_y, a_y, ALU.mult))
                lk(V.tensor_reduce(out=a_t4, in_=a_y2, axis=AX, op=ALU.add))
                root_by_act(TS(a_t4, a_t4, 1.0 / N, A_EPS, ALU.mult, ALU.add), ROOT_A + 1 + c)
                lk(V.reciprocal(a_t4, a_t4))
                lk(TT(a_y, a_y, bc(a_t4, N), ALU.mult))
                lk(TT(a_y, a_y, lnxg.rearrange("p (h n) -> p h n", h=H), ALU.mult))
                lk(TT(a_y, a_y, lnxb.rearrange("p (h n) -> p h n", h=H), ALU.add))
                dve.wait_ge(sem("a_gb"), c + 1)
                dve.wait_ge(sem("a_tok"), c + 1)
                lk(V.tensor_copy(a_bon, PS[0][:, 256:260]))
                lk(TT(a_y2, a_tok[:, 2, :].rearrange("p (h n) -> p h n", h=H), bc(a_bon, N), ALU.mult))
                lk(TT(a_y, a_y, a_y2, ALU.add))
                TT(a_y, a_y, PS[1][:, 256:512].rearrange("p (h n) -> p h n", h=H), ALU.mult).then_inc(sem("mix_y"), 1)
                gated(c, 3, first)
                assert lk.n[0] == 15, lk.n
            tmix(0, True)
            with dve.Fori(1, NT) as c:
                tmix(c)
            chain[0] += 15 * NT
            dve.wait_ge(sem("mix_done"), 2 * NT + NT)

            for n in range(16):
                dve.wait_ge(sem("m_pair"), n + 1)
                dve.wait_ge(sem("m_sg"), 4 * NT + n // 2 + 1)
                ga = GA[n // 2][:, ts(n % 2, 512)]
                TT(ga, ga, PS[n % 4], ALU.mult).then_inc(sem("m_prod"), 1)

            dve.wait_ge(sem("gate_in"), 32)
            link(TT(gt1, gt1, gtb, ALU.add))
            dve.wait_ge(sem("gt2_in"), 32)
            TT(gt2, gt2, gt2b, ALU.add)

            def router(t):
                dve.wait_ge(sem("o_T"), t + 1)
                for k in range(4, 8):
                    ins = TS(o_hT[:, k, :], PS[5][:, ts(k - 4, P)], sc2[:, k:k + 1], sh2[:, k:k + 1], ALU.mult, ALU.add)
                ins.then_inc(sem("o_hT_v"), 1)
                dve.wait_ge(sem("r_mm"), t + 1)
                TT(r_lg[:, t, :], PS[6][:, 0:36], br, ALU.add).then_inc(sem("r_lg"), 1)

            for t in range(NT):
                if t >= 2:
                    dve.wait_ge(sem(f"xn_st{t % 2}"), 16 * (t // 2))
                for j in range(2):
                    dve.wait_ge(sem("o_mm"), 2 * t + j + 1)
                    TT(o_n[t % 2][:, ts(j, 512)], PS[2 * (t % 2) + j], gt1[:, ts(j, 512)], ALU.mult).then_inc(sem("o_out"), 1)
                dve.wait_ge(sem("o_out"), 2 * t + 2)
                dve.wait_ge(sem(f"rows_in{t % 2}"), 32 + 16 * (t // 2) + 16)
                TT(o_x[t % 2], o_x[t % 2], o_n[t % 2], ALU.add).then_inc(sem("o_x1"), 1)
                dve.wait_ge(sem("o_ss"), t + 1)
                r = rstd[:, t:t + 1]
                link(V.reciprocal(r, ss[:, t:t + 1]))
                TS(o_n[t % 2], o_x[t % 2], r, None, ALU.mult).then_inc(sem("o_norm"), 1)
                if t == NT - 1:
                    router(t)
                if t < NT - 1:
                    router(t)

            dve.wait_ge(sem("r_lg"), NT)
            V.memset(r_pre[:, 0], 0.0)
            dve.wait_ge(sem("setup_pool"), R_IOTA)
            gmx, gsum, gi, l1, l2, te, w1, w2, s1, s2 = r_8
            gl = r_lg[:, :, 0:4]
            link(V.tensor_reduce(out=gmx, in_=gl, axis=AX, op=ALU.max))
            TT(r_g4[1], gl, bc(gmx, 4), ALU.subtract).then_inc(sem("r_arg"), 1)
            i4 = r_i4.unsqueeze(1).to_broadcast([P, NT, NG])
            i32_ = r_io.unsqueeze(1).to_broadcast([P, NT, NE])
            link(TT(r_g4[0], gl, bc(gmx, 4), ALU.is_lt))
            link(STT(r_g4[0], r_g4[0], 99.0, i4, ALU.mult, ALU.add))
            link(V.tensor_reduce(out=gi, in_=r_g4[0], axis=AX, op=ALU.min))
            link(TT(r_g4[2], i4, bc(gi, 4), ALU.not_equal))
            em4 = r_em.rearrange("p t (g e) -> p t g e", g=NG)
            for g in range(NG):
                ins = STT(em4[:, :, g, :], bc(r_g4[2][:, :, g], 8), -BIG, r_lg[:, :, 4 + 8 * g:12 + 8 * g], ALU.mult, ALU.add)
            link(ins)

            def best(l, m):
                link(V.tensor_reduce(out=l, in_=r_em, axis=AX, op=ALU.max))
                link(TT(r_t, r_em, bc(l, NE), ALU.is_lt))
                link(STT(r_t, r_t, 99.0, i32_, ALU.mult, ALU.add))
                link(V.tensor_reduce(out=te, in_=r_t, axis=AX, op=ALU.min))
                link(TT(m, i32_, bc(te, NE), ALU.is_equal))
            best(l1, r_m1)
            link(STT(r_em, r_m1, -2 * BIG, r_em, ALU.mult, ALU.add))
            best(l2, r_m2)
            TT(r_t, r_m1, r_m2, ALU.add).then_inc(sem("router_dve"), 1)
            dve.wait_ge(sem("router_dve"), R_MS)
            TT(te, l2, l1, ALU.subtract).then_inc(sem("r_arg"), 1)
            dve.wait_ge(sem("r_exp"), 2)
            link(V.tensor_reduce(out=gsum, in_=r_g4[1], axis=AX, op=ALU.add))
            link(TS(w2, te, 1.0, None, ALU.add))
            link(TT(gsum, gsum, w2, ALU.mult))
            link(V.reciprocal(w1, gsum))
            link(TT(w2, w1, te, ALU.mult))
            dve.wait_ge(sem("r_rank"), 1)
            for t in range(NT):
                link(TT(r_pre[:, t + 1], r_pre[:, t], PS[6][:, ds(64 + NE * t, NE)], ALU.add))
            TT(r_rk, r_pre[:, 0:NT], PS[7][:, 0:256].rearrange("p (t e) -> p t e", t=NT), ALU.add)
            r_cnt = r_pre[:, NT]
            link(TS(r_nx, r_cnt, float(P), None, ALU.is_gt))
            for m in range(2, NT):
                link(STT(r_nx, r_cnt, float(P * m), r_nx, ALU.is_gt, ALU.add))
            link(V.tensor_tensor_scan(out=r_cum, data0=ones[:, 0:NE], data1=r_nx, initial=0.0, op0=ALU.mult, op1=ALU.add))
            link(TT(r_ov, r_cum, r_nx, ALU.subtract))
            link(TT(r_ov, r_ov, r_io, ALU.subtract))
            link(TS(r_ov, r_ov, float(NE - 1), float(P), ALU.add, ALU.mult))
            link(TS(r_em, r_rk, float(P), None, ALU.is_ge))
            link(TT(r_em, r_em, r_ov.unsqueeze(1).to_broadcast([P, NT, NE]), ALU.mult))
            link(TT(r_em, r_em, r_rk, ALU.add))
            link(STT(r_em, i32_, float(P), r_em, ALU.mult, ALU.add))
            dve.wait_ge(sem("setup_pool"), R_IOTAP)
            link(V.tensor_copy(r_tok, i_tok))
            for a, (m, sl, isl) in enumerate(((r_m1, s1, i_s1), (r_m2, s2, i_s2))):
                link(TT(r_t, m, r_em, ALU.mult))
                link(V.tensor_reduce(out=sl, in_=r_t, axis=AX, op=ALU.add))
                link(V.tensor_copy(isl, sl))
                TS(i_hi, isl, 7, None, ALU.logical_shift_right)
                link(TS(i_lo, isl, P - 1, None, ALU.bitwise_and))
                V.tensor_copy(r_blk[a], i_hi)
                link(V.tensor_copy(r_pos[a], i_lo))
                TT(r_hot[a], r_iP.unsqueeze(1).to_broadcast([P, NT, P]), bc(r_pos[a], P), ALU.is_equal)
                link(TT(r_in[a], r_iP[:, 0:NBP].unsqueeze(1).to_broadcast([P, NT, NBP]), bc(r_blk[a], NBP), ALU.is_equal))
                ins = TT(r_in[a], r_in[a], bc(r_tok, NBP), ALU.mult)
            ins.then_inc(sem("router_dve"), 1)
            for j in range(NX):
                ins = TS(r_ex[:, j, :], r_cum, float(j), None, ALU.is_le)
            link(ins)
            link(V.tensor_reduce(out=r_exs[:, 0:NX], in_=r_ex, axis=AX, op=ALU.add))
            link(TS(r_exs[:, 0:NX], r_exs[:, 0:NX], float(NE - 1), None, ALU.min))
            link(V.tensor_copy(r_exs[:, NX:NX + 1], r_cum[:, NE - 1:NE]))
            link(V.tensor_copy(i_ex, r_exs))
            dve.wait_ge(sem("r_rank"), 2)
            V.tensor_copy(i_tab, PS[7][:, 256:256 + NBP]).then_inc(sem("router_dve"), 1)

            def activate(e):
                dve.wait_ge(sem("e_silu"), e + 1)
                TT(e_h, e_g, PS[4], ALU.mult).then_inc(sem("e_act"), 1)

            def y_out(e, s, wait):
                for u in range(2):
                    dve.wait_ge(sem("y"), 2 * e + u + 1)
                    if u == 0 and wait is not None:
                        dve.wait_ge(sem(f"y_st{s}"), wait)
                    TT(e_y[s][:, ts(u, 512)], PS[5 + u], gt2[:, ts(u, 512)], ALU.mult).then_inc(sem("y_out"), 1)

            activate(0)
            activate(1)
            y_out(0, 0, None)
            activate(2)
            y_out(1, 1, None)
            activate(3)
            y_out(2, 0, 16)
            with dve.Fori(2, NE // 2) as i:
                activate(2 * i)
                y_out(2 * i - 1, 1, 16 * (i - 1))
                activate(2 * i + 1)
                y_out(2 * i, 0, 16 * i)
            y_out(NE - 1, 1, 16 * (NE // 2 - 1))
            n_extra = dve.value_load(i_ex[0:1, NX:NX + 1], min_val=0, max_val=NX)
            with dve.If(n_extra > 0):
                with dve.Fori(0, NX) as j:
                    with dve.If(n_extra > j):
                        dve.wait_ge(sem("extra_go"), j + 1)
                        activate(NE + j)
                        y_out(NE + j, 0, None)
                    with dve.Else():
                        dve.nop()
            with dve.Else():
                dve.nop()

            dve.wait_ge(sem("gate_in"), 32 + 16 * NT)
            for t in range(NT):
                y0, y1 = f_y[t % 4]
                dve.wait_ge(fy_in[t % 4][0], fy_in[t % 4][1] + 32 * (t // 4) + 32)
                link(STT(f_x[t], y0, w1[:, t:t + 1], f_x[t], ALU.mult, ALU.add))
                STT(f_x[t], y1, w2[:, t:t + 1], f_x[t], ALU.mult, ALU.add).then_inc(sem("f_sum"), 1)


def kernel(**inputs):
    import numpy as np
    import concourse.bacc as bacc
    from concourse.bass_utils import run_bass_kernel_spmd

    nc = bacc.Bacc("TRN2", target_bir_lowering=False, num_devices=1)
    arrays, I = {}, {}
    for name, a in inputs.items():
        a = np.ascontiguousarray(a)
        arrays[f"in_{name}"] = a
        I[name] = nc.dram_tensor(f"in_{name}", a.shape, mybir.dt.from_np(a.dtype), kind="ExternalInput").ap()
    f32, i32 = mybir.dt.float32, mybir.dt.int32
    out = nc.dram_tensor("out_0", (1, T, D), f32, kind="ExternalOutput").ap()
    dram = [nc.dram_tensor(n, s, d, kind="Internal").ap() for n, s, d in (
        ("x1", (T, D), f32), ("xnorm", (T, D), f32), ("y_slots", (NB * P, D), f32),
        ("gate_rows", (2, D), f32),
        ("first_gate", (KT, P, T), f32), ("merged_part", (KT, P, T), f32))]
    hybrid_block(nc, I, out, dram)
    r = run_bass_kernel_spmd(nc, [arrays], core_ids=[0])
    return r.results[0]["out_0"]
```
